# Optimizing a Trainium2 kernel written in Bass

```python
import numpy as np
import jax
import jax.numpy as jnp
from jax import lax

D_MODEL = 1024
BATCH = 1
SEQ = 1024
DEPTH = 2

N_MIXERS = 4
PLE_DIM = 256
D_FF = 4 * D_MODEL
NORM_EPS = 1e-6

A_HEADS = 8
A_DV = D_MODEL // A_HEADS
A_DQK = A_DV // 2
A_CHUNK = 128
A_SPLITS = (A_HEADS * A_DQK, A_HEADS * A_DQK, D_MODEL, D_MODEL, A_HEADS, A_HEADS)

B_HEADS = 8
B_DK = 128
B_DV = D_MODEL // B_HEADS
B_FDIM = B_HEADS * B_DK
B_CHUNK = 16
B_SPLITS = (B_FDIM, B_FDIM, D_MODEL, D_MODEL)

C_HALF = 2 * D_MODEL
C_GROUPS = 8
C_GROUP_W = C_HALF // C_GROUPS
C_CHUNK = 128

D_RNN = D_MODEL
D_BLOCK_W = 256
D_BLOCKS = D_RNN // D_BLOCK_W
D_CONV = 4
RG_C = 8.0

kernel_name = 'hybrid_mlstm_hgrn2_gmlp_rglru_trunk'

def _rmsnorm(x, gain):
    x32 = x.astype(jnp.float32)
    y = x32 * lax.rsqrt(jnp.mean(x32 * x32, axis=-1, keepdims=True) + NORM_EPS)
    return (y * gain.astype(jnp.float32)).astype(x.dtype)

def _split(z, sizes):
    idx = np.cumsum(sizes)[:-1].tolist()
    return jnp.split(z, idx, axis=-1)

def _to_chunks(t, size):
    b, s, h = t.shape[:3]
    t = t.reshape((b, s // size, size, h) + t.shape[3:])
    return jnp.transpose(t, (1, 0, 3, 2) + tuple(range(4, t.ndim)))

def _from_chunks(t):
    t = jnp.transpose(t, (1, 0, 3, 2) + tuple(range(4, t.ndim)))
    b, nc, size, h = t.shape[:4]
    return t.reshape((b, nc * size, h) + t.shape[4:])

def _mlstm_chunkwise(q, k, v, log_i, log_f):
    bsz, _, nh, dk = q.shape
    dv = v.shape[-1]
    L = A_CHUNK
    mask = jnp.tril(jnp.ones((L, L), dtype=bool))

    def step(carry, inp):
        c_st, n_st, m_st = carry
        qc, kc, vc, ic, fc = inp
        b = jnp.cumsum(fc, axis=-1)
        inter = b + m_st[..., None]
        dmat = jnp.where(mask, b[..., :, None] - b[..., None, :] + ic[..., None, :], -jnp.inf)
        m_t = jnp.maximum(inter, jnp.max(dmat, axis=-1))
        s = jnp.einsum('bhtd,bhsd->bhts', qc, kc) * jnp.exp(dmat - m_t[..., None])
        w_inter = jnp.exp(inter - m_t)
        num = jnp.einsum('bhts,bhsv->bhtv', s, vc) + w_inter[..., None] * jnp.einsum('bhtd,bhdv->bhtv', qc, c_st)
        den = jnp.sum(s, axis=-1) + w_inter * jnp.einsum('bhtd,bhd->bht', qc, n_st)
        out = num / jnp.maximum(jnp.abs(den), jnp.exp(-m_t))[..., None]
        b_last = b[..., -1]
        tail = b_last[..., None] - b + ic
        m_new = jnp.maximum(b_last + m_st, jnp.max(tail, axis=-1))
        decay = jnp.exp(b_last + m_st - m_new)
        wk = jnp.exp(tail - m_new[..., None])
        c_new = decay[..., None, None] * c_st + jnp.einsum('bhs,bhsd,bhsv->bhdv', wk, kc, vc)
        n_new = decay[..., None] * n_st + jnp.einsum('bhs,bhsd->bhd', wk, kc)
        return (c_new, n_new, m_new), out

    init = (jnp.zeros((bsz, nh, dk, dv), jnp.float32),
            jnp.zeros((bsz, nh, dk), jnp.float32),
            jnp.zeros((bsz, nh), jnp.float32))
    xs = (_to_chunks(q, L), _to_chunks(k, L), _to_chunks(v, L), _to_chunks(log_i, L), _to_chunks(log_f, L))
    _, out = lax.scan(step, init, xs)
    return _from_chunks(out)

def _mlstm_mixer(x, w_in, ig_bias, fg_bias, head_gain, w_out):
    bsz, s, _ = x.shape
    f32 = jnp.float32
    q, k, v, o, ig, fg = _split(x @ w_in, A_SPLITS)
    q = q.reshape(bsz, s, A_HEADS, A_DQK).astype(f32) * (A_DQK ** -0.5)
    k = k.reshape(bsz, s, A_HEADS, A_DQK).astype(f32)
    v = v.reshape(bsz, s, A_HEADS, A_DV).astype(f32)
    log_i = ig.astype(f32) + ig_bias.astype(f32)
    log_f = jax.nn.log_sigmoid(fg.astype(f32) + fg_bias.astype(f32))
    hcell = _rmsnorm(_mlstm_chunkwise(q, k, v, log_i, log_f), head_gain)
    y = jax.nn.sigmoid(o.astype(f32)) * hcell.reshape(bsz, s, D_MODEL)
    return y.astype(x.dtype) @ w_out

def _hgrn2_chunkwise(q, k, v, log_f):
    bsz, _, nh, dk = q.shape
    dv = v.shape[-1]
    L = B_CHUNK
    mask = jnp.tril(jnp.ones((L, L), dtype=bool))[:, :, None]

    def step(s_st, inp):
        qc, kc, vc, gc = inp
        g = jnp.cumsum(gc, axis=-2)
        decay = jnp.exp(jnp.where(mask, g[..., :, None, :] - g[..., None, :, :], -jnp.inf))
        attn = jnp.einsum('bhtc,bhsc,bhtsc->bhts', qc, kc, decay)
        out = jnp.einsum('bhts,bhsv->bhtv', attn, vc) + jnp.einsum('bhtc,bhcv->bhtv', qc * jnp.exp(g), s_st)
        g_last = g[..., -1:, :]
        s_new = (jnp.exp(g_last[..., 0, :])[..., None] * s_st
                 + jnp.einsum('bhsc,bhsv->bhcv', kc * jnp.exp(g_last - g), vc))
        return s_new, out

    init = jnp.zeros((bsz, nh, dk, dv), jnp.float32)
    xs = (_to_chunks(q, L), _to_chunks(k, L), _to_chunks(v, L), _to_chunks(log_f, L))
    _, out = lax.scan(step, init, xs)
    return _from_chunks(out)

def _hgrn2_mixer(x, w_in, lower_bound, head_gain, w_out):
    bsz, s, _ = x.shape
    f32 = jnp.float32
    q, fz, i_in, g = _split(x @ w_in, B_SPLITS)
    fz = fz.astype(f32)
    lb = lower_bound.astype(f32)
    log_f = jnp.logaddexp(jnp.log(lb), jnp.log1p(-lb) + jax.nn.log_sigmoid(fz))
    key = (1.0 - lb) * jax.nn.sigmoid(-fz)
    shp = (bsz, s, B_HEADS, B_DK)
    o = _hgrn2_chunkwise(q.astype(f32).reshape(shp), key.reshape(shp),
                         i_in.astype(f32).reshape(bsz, s, B_HEADS, B_DV), log_f.reshape(shp))
    o = _rmsnorm(o, head_gain).reshape(bsz, s, D_MODEL) * jax.nn.silu(g.astype(f32))
    return o.astype(x.dtype) @ w_out

def _gmlp_mixer(x, w_in, ln_gain, ln_bias, w_s, b_s, w_out):
    bsz, s, _ = x.shape
    f32 = jnp.float32
    u, v = jnp.split(jax.nn.gelu(x @ w_in), 2, axis=-1)
    v32 = v.astype(f32)
    mu = jnp.mean(v32, axis=-1, keepdims=True)
    var = jnp.mean(jnp.square(v32 - mu), axis=-1, keepdims=True)
    v32 = (v32 - mu) * lax.rsqrt(var + NORM_EPS) * ln_gain.astype(f32) + ln_bias.astype(f32)
    vc = v32.reshape(bsz, s // C_CHUNK, C_CHUNK, C_GROUPS, C_GROUP_W)
    w_causal = jnp.tril(w_s.astype(f32))
    vm = jnp.einsum('gts,bnsgc->bntgc', w_causal, vc) + b_s.astype(f32).T[:, :, None]
    y = u.astype(f32) * vm.reshape(bsz, s, C_HALF)
    return y.astype(x.dtype) @ w_out

def _linrec_combine(e1, e2):
    a1, b1 = e1
    a2, b2 = e2
    return a1 * a2, a2 * b1 + b2

def _rglru_mixer(x, w_in, conv_w, conv_b, w_a, b_a, w_x, b_x, lam, w_out):
    bsz, s, _ = x.shape
    f32 = jnp.float32
    gate_br, xb = jnp.split(x @ w_in, 2, axis=-1)
    xb = lax.conv_general_dilated(xb, conv_w[:, None, :], window_strides=(1,), padding=[(D_CONV - 1, 0)],
                                  dimension_numbers=('NWC', 'WIO', 'NWC'), feature_group_count=D_RNN) + conv_b
    xg = xb.astype(f32).reshape(bsz, s, D_BLOCKS, D_BLOCK_W)
    r = jax.nn.sigmoid(jnp.einsum('bsnc,ncd->bsnd', xg, w_a.astype(f32)).reshape(bsz, s, D_RNN) + b_a.astype(f32))
    ig = jax.nn.sigmoid(jnp.einsum('bsnc,ncd->bsnd', xg, w_x.astype(f32)).reshape(bsz, s, D_RNN) + b_x.astype(f32))
    log_a = -RG_C * r * jax.nn.softplus(-lam.astype(f32))
    a = jnp.exp(log_a)
    beta = jnp.sqrt(-jnp.expm1(2.0 * log_a)) * (ig * xg.reshape(bsz, s, D_RNN))
    _, hseq = lax.associative_scan(_linrec_combine, (a, beta), axis=1)
    y = hseq * jax.nn.gelu(gate_br.astype(f32))
    return y.astype(x.dtype) @ w_out

def _sqrelu_mlp(x, w_up, w_down):
    return jnp.square(jax.nn.relu(x @ w_up)) @ w_down

def setup_inputs(seed: int = 0) -> dict:
    key = jax.random.key(seed)
    keys = iter(jax.random.split(key, 48))

    def nrm(shape, scale):
        return scale * jax.random.normal(next(keys), shape, jnp.float32)

    def gain(shape):
        return 1.0 + nrm(shape, 0.05)

    n_a, n_b, n_c, n_d = [len(range(m, DEPTH, N_MIXERS)) for m in range(N_MIXERS)]
    d = D_MODEL
    u = jax.random.uniform(next(keys), (n_d, D_RNN), jnp.float32, 0.9, 0.999)
    a0 = u ** (1.0 / RG_C)
    return {
        'x': nrm((BATCH, SEQ, d), 1.0),
        'p': nrm((DEPTH, BATCH, SEQ, PLE_DIM), 1.0),
        'norm_gains': gain((DEPTH, 5, d)),
        'mlp_w_up': nrm((DEPTH, d, D_FF), d ** -0.5),
        'mlp_w_down': nrm((DEPTH, D_FF, d), D_FF ** -0.5),
        'ple_w_up': nrm((DEPTH, PLE_DIM, d), PLE_DIM ** -0.5),
        'ple_w_gate': nrm((DEPTH, d, d), d ** -0.5),
        'a_w_in': nrm((n_a, d, sum(A_SPLITS)), d ** -0.5),
        'a_ig_bias': nrm((n_a, A_HEADS), 0.1),
        'a_fg_bias': jnp.linspace(3.0, 6.0, A_HEADS, dtype=jnp.float32) + nrm((n_a, A_HEADS), 0.1),
        'a_head_gain': gain((n_a, A_HEADS, A_DV)),
        'a_w_out': nrm((n_a, A_HEADS * A_DV, d), (A_HEADS * A_DV) ** -0.5),
        'b_w_in': nrm((n_b, d, sum(B_SPLITS)), d ** -0.5),
        'b_lower_bound': 1.0 + nrm((DEPTH, B_FDIM), 0.1),
        'b_head_gain': gain((n_b, B_HEADS, B_DV)),
        'b_w_out': nrm((n_b, B_HEADS * B_DV, d), (B_HEADS * B_DV) ** -0.5),
        'c_w_in': nrm((n_c, d, 2 * C_HALF), d ** -0.5),
        'c_ln_gain': gain((n_c, C_HALF)),
        'c_ln_bias': nrm((n_c, C_HALF), 0.02),
        'c_spatial_w': nrm((n_c, C_GROUPS, C_CHUNK, C_CHUNK), C_CHUNK ** -0.5),
        'c_spatial_b': 1.0 + nrm((n_c, C_GROUPS, C_CHUNK), 0.02),
        'c_w_out': nrm((n_c, C_HALF, d), C_HALF ** -0.5),
        'd_w_in': nrm((n_d, d, 2 * D_RNN), d ** -0.5),
        'd_conv_w': nrm((n_d, D_CONV, D_RNN), D_CONV ** -0.5),
        'd_conv_b': nrm((n_d, D_RNN), 0.02),
        'd_w_a': nrm((n_d, D_BLOCKS, D_BLOCK_W, D_BLOCK_W), D_BLOCK_W ** -0.5),
        'd_b_a': nrm((n_d, D_RNN), 0.02),
        'd_w_x': nrm((n_d, D_BLOCKS, D_BLOCK_W, D_BLOCK_W), D_BLOCK_W ** -0.5),
        'd_b_x': nrm((n_d, D_RNN), 0.02),
        'd_lambda': jnp.log(a0) - jnp.log1p(-a0),
        'd_w_out': nrm((n_d, D_RNN, d), D_RNN ** -0.5),
    }

def reference(x, p, norm_gains, mlp_w_up, mlp_w_down, ple_w_up, ple_w_gate,
              a_w_in, a_ig_bias, a_fg_bias, a_head_gain, a_w_out,
              b_w_in, b_lower_bound, b_head_gain, b_w_out,
              c_w_in, c_ln_gain, c_ln_bias, c_spatial_w, c_spatial_b, c_w_out,
              d_w_in, d_conv_w, d_conv_b, d_w_a, d_b_a, d_w_x, d_b_x, d_lambda, d_w_out):
    lb = jnp.cumsum(jax.nn.softmax(b_lower_bound.astype(jnp.float32), axis=0), axis=0)
    lb = lb - lb[0]
    h = x
    for i in range(DEPTH):
        kind, j = i % N_MIXERS, i // N_MIXERS
        hn = _rmsnorm(h, norm_gains[i, 0])
        if kind == 0:
            y = _mlstm_mixer(hn, a_w_in[j], a_ig_bias[j], a_fg_bias[j], a_head_gain[j], a_w_out[j])
        elif kind == 1:
            y = _hgrn2_mixer(hn, b_w_in[j], lb[i], b_head_gain[j], b_w_out[j])
        elif kind == 2:
            y = _gmlp_mixer(hn, c_w_in[j], c_ln_gain[j], c_ln_bias[j], c_spatial_w[j], c_spatial_b[j], c_w_out[j])
        else:
            y = _rglru_mixer(hn, d_w_in[j], d_conv_w[j], d_conv_b[j], d_w_a[j], d_b_a[j],
                             d_w_x[j], d_b_x[j], d_lambda[j], d_w_out[j])
        h = h + _rmsnorm(y, norm_gains[i, 1])
        y = _sqrelu_mlp(_rmsnorm(h, norm_gains[i, 2]), mlp_w_up[i], mlp_w_down[i])
        h = h + _rmsnorm(y, norm_gains[i, 3])
        gate = jax.nn.sigmoid(h @ ple_w_gate[i])
        h = h + _rmsnorm(gate * (p[i] @ ple_w_up[i]), norm_gains[i, 4])
    return h


_drawn_inputs = setup_inputs


def setup_inputs(seed=0):
    import zlib

    import numpy as np

    out = dict(_drawn_inputs(seed))
    spreads = {}
    factors = {'a_ig_bias': 200.0}
    for name, (base, spread) in spreads.items():
        noise = np.random.default_rng([zlib.crc32(name.encode()), seed]).standard_normal(out[name].shape)
        drawn = base * np.exp(spread * noise) if base else spread * noise
        out[name] = jnp.asarray(drawn.astype(out[name].dtype))
    for name, factor in factors.items():
        out[name] = (out[name] * factor).astype(out[name].dtype)
    return out
```

```python
from contextlib import ExitStack

import numpy as np

import concourse.bass as bass
from concourse import mybir

P = 128
D = 1024
S = 1024
NT = S // P
NC = D // P
FF = 4 * D
FG = 256
NG = FF // FG
BLK = D * 256 // P
HEADS = 8
DQK = 64
DV = 128
PLE = 256
EPS = 1e-6
LV = 7
NEG = -3.0e38

ALU = mybir.AluOpType
ACT = mybir.ActivationFunctionType
F32 = mybir.dt.float32
F32R = mybir.dt.float32r
AX_X = mybir.AxisListType.X

L0_GATES = 0
L0_HEADS = 1
L0_OUT = L0_HEADS + 2 * HEADS
L0_MLP = L0_OUT + 4
L0_GATE = L0_MLP + 2 * NG
L1_HEADS = L0_GATE + 5
L1_OUT = L1_HEADS + 2 * HEADS
L1_MLP = L1_OUT + 4
L1_GATE = L1_MLP + 2 * NG
BLOCKS = L1_GATE + 5
LOADED = 48


def shape_constants():
    i = np.arange(P)
    s, t = i[:, None], i[None, :]
    sums = np.zeros((P, LV + 2, P), np.float32)
    mask = np.zeros((P, LV + 1, P), np.float32)
    for l in range(LV):
        m = 64 >> l
        mid = (t // (2 * m)) * 2 * m + m
        sums[:, l] = np.where(t >= mid, (s >= mid) & (s <= t), (s > t) & (s < mid))
        mask[:, l] = (s // (2 * m) == t // (2 * m)) & (s % (2 * m) < m) & (t % (2 * m) >= m)
    sums[:, LV] = s <= t
    sums[:, LV + 1] = s > t
    mask[:, LV] = s == t
    causal = np.where(s <= t, 0.0, NEG).astype(np.float32)
    return {"c_sums": sums, "c_level_mask": mask, "c_causal": causal, "c_ident": np.eye(P, dtype=np.float32)}


class Link:

    def __init__(self, eng, sem):
        self.eng, self.sem, self.base, self.n = eng, sem, 0, 0

    def __call__(self, ins):
        ins.then_inc(self.sem, 1)
        self.n += 1
        self.eng.wait_ge(self.sem, self.base + self.n)


def trunk(nc, x, p, norm_gains, mlp_w_up, mlp_w_down, ple_w_up, ple_w_gate,
          a_w_in, a_ig_bias, a_fg_bias, a_head_gain, a_w_out,
          b_w_in, b_lower_bound, b_head_gain, b_w_out,
          c_sums, c_level_mask, c_causal, c_ident, out):
    ctx = ExitStack()
    with ctx:
        def sb(name, shape, dt=F32):
            return ctx.enter_context(nc.sbuf_tensor(name, shape, dt))

        def sem(name):
            return ctx.enter_context(nc.semaphore(name))

        XTh = sb("XTh", [P, NC, S], F32R)
        XTl = sb("XTl", [P, NC, S], F32R)
        H = sb("H", [P, NT, D])
        Y = sb("Y", [P, NT, D])
        Wh = [sb(f"Wh{i}", [P, BLK], F32R) for i in range(2)]
        Wl = [sb(f"Wl{i}", [P, BLK], F32R) for i in range(2)]
        Wraw = [sb(f"Wraw{i}", [P, BLK]) for i in range(2)]
        HTh = sb("HTh", [P, 2, S], F32R)
        HTl = sb("HTl", [P, 2, S], F32R)
        G = sb("G", [P, 2, D])
        TMP = sb("TMP", [P, D])
        IDN = sb("IDN", [P, P])
        zero1 = sb("zero1", [P, 1])
        eps1 = sb("eps1", [P, 1])
        ssA = sb("ssA", [P, NT])
        sdA = sb("sdA", [P, NT])
        rA = sb("rA", [P, NT])
        ssB = sb("ssB", [P, NT])
        sdB = sb("sdB", [P, NT])
        rB = sb("rB", [P, NT])
        small = sb("small", [P, 64])
        rows8 = sb("rows8", [HEADS, 32])
        PS = ctx.enter_context(nc.psum_tensor("PS", [P, 8, 512], F32))
        junk = PS[:, 6:8, :].rearrange("p a n -> p (a n)")

        h_dram = nc.dram_tensor("h_scratch", (S, D), F32, kind="Internal").ap()
        negm_dram = nc.dram_tensor("negm_scratch", (HEADS, S), F32, kind="Internal").ap()
        dec_dram = nc.dram_tensor("decay_scratch", (HEADS, NT), F32, kind="Internal").ap()

        tok = lambda a: a.rearrange("(t p) n -> p t n", p=P)
        x_tok = tok(x[0])
        out_tok = tok(out[0])
        h_tok = tok(h_dram)

        landed = [sem("landed0"), sem("landed1")]
        split_hi = sem("split_hi")
        split = sem("split")
        consts = sem("consts")
        ready = sem("ready")
        act_link = sem("act_link")
        dve_link = sem("dve_link")
        stage0 = sem("stage0")

        block = ctx.enter_context(nc.Block())

        def phase(name, names):
            return {n: sem(f"{name}_{n}") for n in names}

        T_SEMS = ["gain", "sdA", "hA", "sdB", "xs", "tr", "hi", "xt"]
        start = phase("start", ["gain", "hin", "sdB", "xs", "tr", "hi", "xt"])
        mix0 = phase("mix0", ["full", "free", "rows", "rows_tr", "scal", "scratch", "saved", "decb", "bcast", "const",
                              "prep", "args", "probs", "tr", "tq", "qk", "kv", "st", "outp", "num", "state",
                              "den", "postL", "done"])
        mix1 = phase("mix1", ["fullA", "fullB", "freeA", "sg", "freeB", "const", "bound", "boundS", "oml",
                              "onem", "lnf", "lfhi", "lf", "pe1", "decays", "tqk", "qeke", "kg",
                              "lev", "at", "outp", "kv", "oev", "state", "ss", "rstd", "done"])
        tm = [phase(f"tm{l}", ["gain", "xs", "tr", "hi", "xt"]) for l in range(2)]
        wo = [phase(f"wo{l}", ["full", "free"]) for l in range(2)]
        tw = [phase(f"tw{l}", T_SEMS + ["hin"]) for l in range(2)]
        mlp = [phase(f"mlp{l}", ["full", "free", "hi", "ht"]) for l in range(2)]
        tp = [phase(f"tp{l}", ["gain", "sdA", "hA", "tr", "hi", "xt"]) for l in range(2)]
        ple = [phase(f"ple{l}", ["full", "free", "sig", "pin", "ptr", "phi", "pt"]) for l in range(2)]
        te = [phase("te0", T_SEMS + ["hout"]), phase("te1", ["gain", "sdA", "hA", "hout"])]

        @block.sync
        def _(sp):
            def stage(n_parity, n_wait, parts):
                if n_wait is not None:
                    sp.wait_ge(split, n_wait)
                for k, (dst, src) in enumerate(parts):
                    add = LOADED - 16 * (len(parts) - 1) if k == 0 else 16
                    sp.dma_start(dst, src).then_inc(landed[n_parity], add)

            def cols(q, w, c0, n, at=0):
                return (Wraw[q][:].rearrange("p (c n) -> p c n", c=NC)[:, :, at:at + n],
                        w[:, c0].rearrange("(c p) n -> p c n", p=P))

            def rows(q, w, r0):
                return (Wraw[q][:].rearrange("p (c n) -> p c n", c=2),
                        w[r0, :].rearrange("(c p) n -> p c n", p=P))

            ds = bass.ds
            w = a_w_in[0]
            sp.wait_ge(stage0, 1)
            o_g = 2 * HEADS * DQK + 2 * D
            with nc.allow_non_contiguous_dma(reason="gate columns"):
                stage(0, None, [cols(0, w, ds(o_g, 8), 8), cols(0, w, ds(o_g + 8, 8), 8, 128)])
            sp.dma_start(IDN[:], c_ident).then_inc(consts, 16)

            def head0(h, n_wait_a, n_wait_b):
                stage(1, n_wait_a, [cols(1, w, ds(h * DQK, DQK), DQK),
                                    cols(1, w, ds(HEADS * DQK + h * DQK, DQK), DQK, DQK),
                                    cols(1, w, ds(2 * HEADS * DQK + h * DV, DV), DV, 2 * DQK)])
                stage(0, n_wait_b, [cols(0, w, ds(2 * HEADS * DQK + D + h * DV, DV), DV)])

            head0(0, None, 1)
            with sp.Fori(1, HEADS) as h:
                head0(h, 2 * h, 2 * h + 1)

            def tail(l, n_out, n_mlp, n_gate, w_out):
                for j in range(4):
                    q = (n_out + j) % 2
                    stage(q, n_out + j - 1, [rows(q, w_out[0], ds(256 * j, 256))])
                qu, qd = n_mlp % 2, (n_mlp + 1) % 2
                with sp.Fori(0, NG) as g:
                    stage(qu, 2 * g + (n_mlp - 1), [cols(qu, mlp_w_up[l], ds(g * FG, FG), FG)])
                    stage(qd, 2 * g + n_mlp, [rows(qd, mlp_w_down[l], ds(g * FG, FG))])
                for j in range(4):
                    q = (n_gate + j) % 2
                    stage(q, n_gate + j - 1, [rows(q, ple_w_gate[l], ds(256 * j, 256))])
                q = (n_gate + 4) % 2
                stage(q, n_gate + 3, [rows(q, ple_w_up[l], ds(0, 256))])

            tail(0, L0_OUT, L0_MLP, L0_GATE, a_w_out)
            w1 = b_w_in[0]
            with sp.Fori(0, HEADS) as h:
                stage(0, 2 * h + (L1_HEADS - 1), [cols(0, w1, ds(h * P, P), P), cols(0, w1, ds(D + h * P, P), P, P)])
                stage(1, 2 * h + L1_HEADS, [cols(1, w1, ds(2 * D + h * P, P), P), cols(1, w1, ds(3 * D + h * P, P), P, P)])
            tail(1, L1_OUT, L1_MLP, L1_GATE, b_w_out)

        @block.gpsimd
        def _(pool):
            zeros = zero1[:].to_broadcast([P, BLK])
            nc.gpsimd.memset(Wraw[0][:], 0.0).then_inc(stage0, 1)
            nc.gpsimd.memset(zero1[:], 0.0).then_inc(ready, 1)
            pool.wait_ge(ready, 1)
            nc.gpsimd.memset(eps1[:], EPS).then_inc(ready, 1)

            def split_block(q, n, used, nth):
                pool.wait_ge(landed[q], nth * LOADED + LOADED)
                if used:
                    pool.wait_ge(*used)
                nc.gpsimd.tensor_tensor(Wh[q][:], Wraw[q][:], zeros, ALU.subtract).then_inc(split_hi, 1)
                pool.wait_ge(split_hi, n + 1)
                nc.gpsimd.tensor_tensor(Wl[q][:], Wraw[q][:], Wh[q][:].bitcast(F32), ALU.subtract).then_inc(split, 1)

            def one(n, used=None):
                split_block(n % 2, n, used, n // 2)

            def pair(i, n0, used0, used1):
                split_block(n0 % 2, 2 * i + n0, used0, i + n0 // 2)
                split_block((n0 + 1) % 2, 2 * i + (n0 + 1), used1, i + (n0 + 1) // 2)

            one(0)
            one(1)
            one(2, (mix0["full"], 4))
            with pool.Fori(1, HEADS) as h:
                pair(h, L0_HEADS, (mix0["full"], 16 * h - 4), (mix0["full"], 16 * h + 4))

            def tail(l, n_out, n_mlp, n_gate, heads_done):
                one(n_out, heads_done[0])
                one(n_out + 1, heads_done[1])
                one(n_out + 2, (wo[l]["full"], 16))
                one(n_out + 3, (wo[l]["full"], 32))
                one(n_mlp, (wo[l]["full"], 48))
                one(n_mlp + 1, (wo[l]["full"], 64))
                with pool.Fori(1, NG) as g:
                    pair(g, n_mlp, (mlp[l]["full"], 20 * g - 16), (mlp[l]["full"], 20 * g))
                one(n_gate, (mlp[l]["full"], 20 * NG - 16))
                one(n_gate + 1, (mlp[l]["full"], 20 * NG))
                for j in range(2, 5):
                    one(n_gate + j, (ple[l]["full"], 16 * (j - 1)))

            tail(0, L0_OUT, L0_MLP, L0_GATE, ((mix0["full"], 16 * HEADS - 4), (mix0["full"], 16 * HEADS + 4)))
            one(L1_HEADS, (ple[0]["full"], 64))
            one(L1_HEADS + 1, (ple[0]["full"], 80))
            with pool.Fori(1, HEADS) as h:
                pair(h, L1_HEADS, (mix1["fullA"], 8 * h), (mix1["fullB"], 8 * h))
            tail(1, L1_OUT, L1_MLP, L1_GATE, ((mix1["fullA"], 8 * HEADS), (mix1["fullB"], 8 * HEADS)))

        @block.tensor
        def _(pe):
            def mm3(out_, sh, sl, mh, ml, start, stop):
                nc.tensor.matmul(out_, sh, mh, start=start, stop=False)
                nc.tensor.matmul(out_, sh, ml, start=False, stop=False)
                return nc.tensor.matmul(out_, sl, mh, start=False, stop=stop)

            def transpose_tile(ph, src, pre, t):
                pe.wait_ge(ph["xs"] if pre else ph["hA"], t + 1)
                if t:
                    pe.wait_ge(ph["xt"], 2 * t)
                for b in range(2):
                    for k in range(4):
                        c = 4 * b + k
                        last = nc.tensor.transpose(PS[:, 4 + b, k * P:(k + 1) * P], src[:, t, c * P:(c + 1) * P], IDN[:])
                    last.then_inc(ph["tr"], 1)

            def transition(ph, src, pre, first=0):
                for t in range(first, NT):
                    transpose_tile(ph, src, pre, t)

            def down_block(ph, q, n, k0, stat_h, stat_l, chunk0, tile_wait=None, bank_wait=None, behind=None):
                pe.wait_ge(split, n + 1)
                wh = Wh[q][:].rearrange("p (c n) -> p c n", c=2)
                wl = Wl[q][:].rearrange("p (c n) -> p c n", c=2)
                for t in range(NT):
                    if tile_wait:
                        tile_wait(t)
                    for nh in range(2):
                        m = 2 * t + nh
                        if bank_wait and m < 4:
                            bank_wait(m)
                        elif not (isinstance(k0, int) and k0 + m < 4):
                            pe.wait_ge(ph["free"], k0 + (m - 3))
                        for c in range(2):
                            cc = chunk0 + c
                            last = mm3(PS[:, m % 4, :], stat_h[:, cc, t * P:(t + 1) * P], stat_l[:, cc, t * P:(t + 1) * P],
                                       wh[:, c, nh * 512:(nh + 1) * 512], wl[:, c, nh * 512:(nh + 1) * 512],
                                       c == 0, c == 1)
                        last.then_inc(ph["full"], 1)
                    if behind and t >= 3:
                        behind(t - 3)

            pe.wait_ge(consts, 16)
            transition(start, Y, True)

            def gemm_tokens(ph_full, wait_free, n, q, width, t):
                wh = Wh[q][:].rearrange("p (c n) -> p c n", c=NC)
                wl = Wl[q][:].rearrange("p (c n) -> p c n", c=NC)
                if t == 0:
                    pe.wait_ge(split, n + 1)
                wait_free(t)
                for c in range(NC):
                    last = mm3(PS[:, t % 2, 0:width], XTh[:, c, t * P:(t + 1) * P], XTl[:, c, t * P:(t + 1) * P],
                               wh[:, c, 0:width], wl[:, c, 0:width], c == 0, c == NC - 1)
                last.then_inc(ph_full, 1)
                return last

            pe.wait_ge(split, 1)
            pe.wait_ge(start["xt"], 2 * NT)
            g_h = Wh[0][:].rearrange("p (c n) -> p c n", c=NC)
            g_l = Wl[0][:].rearrange("p (c n) -> p c n", c=NC)
            for kind in range(2):
                for half in range(2):
                    for c in range(NC):
                        hs = slice(half * 512, half * 512 + 512)
                        ws = slice(kind * P, kind * P + P)
                        last = mm3(PS[:, 2 * kind + half, :], g_h[:, c, ws], g_l[:, c, ws],
                                   XTh[:, c, hs], XTl[:, c, hs], c == 0, c == NC - 1)
                    last.then_inc(mix0["full"], 1)

            pe.wait_ge(mix0["rows"], 1)
            for qn in range(4):
                for c in range(NT):
                    o = (qn * NT + c) * HEADS
                    last = nc.tensor.transpose(PS[:, 4, o:o + HEADS],
                                               Y[0:HEADS, 3 + qn, c * P:(c + 1) * P], IDN[0:HEADS, 0:HEADS])
            last.then_inc(mix0["rows_tr"], 1)

            zA = H[:].rearrange("p t n -> p (t n)")[:, 0:NT * 260].rearrange("p (t n) -> p t n", n=260)
            M0 = layer0_views(H, G, TMP)

            with pe.Fori(0, HEADS) as h:
                def freeA(t):
                    pe.wait_ge(mix0["free"], 16 * h + (2 + t + 1 if t < 2 else t + 3))

                def freeB(t):
                    pe.wait_ge(mix0["free"], 16 * h + (11 + t))
                for t in range(NT):
                    last = gemm_tokens(mix0["full"], freeA, 2 * h + L0_HEADS, 1, 256, t)
                for t in range(NT):
                    last = gemm_tokens(mix0["full"], freeB, 2 * h + (L0_HEADS + 1), 0, DV, t)
                pe.wait_ge(mix0["prep"], h + 1)
                for c in range(NT):
                    if c:
                        pe.wait_ge(mix0["tq"], 8 * h + c)
                        pe.wait_ge(mix0["state"], 8 * h + c)
                    nc.tensor.matmul(PS[0:DQK, 7, 0:DV + 1], M0.KW[:, c, :], M0.z[:, c, 2 * DQK:2 * DQK + DV + 1],
                                     start=True, stop=True).then_inc(mix0["kv"], 1)
                    nc.tensor.transpose(PS[0:DQK, 4, 0:P], M0.QS[:, c, :], IDN[:])
                    nc.tensor.transpose(PS[0:DQK, 4, P:2 * P], M0.z[:, c, DQK:2 * DQK], IDN[:])
                    nc.tensor.transpose(PS[0:DQK, 4, 2 * P:3 * P], M0.QW[:, c, :], IDN[:]).then_inc(mix0["tr"], 1)
                    pe.wait_ge(mix0["tq"], 8 * h + c + 1)
                    if c:
                        pe.wait_ge(mix0["st"], 8 * h + c)
                    nc.tensor.matmul(PS[:, 5, 0:P], M0.TQ[0:DQK, P:2 * P], M0.TQ[0:DQK, 0:P],
                                     start=True, stop=True).then_inc(mix0["qk"], 1)
                    pe.wait_ge(mix0["st"], 8 * h + c + 1)
                    if c:
                        pe.wait_ge(mix0["num"], 8 * h + c)
                    nc.tensor.matmul(PS[:, 6, 0:DV + 1], M0.ST[:], M0.z[:, c, 2 * DQK:2 * DQK + DV + 1], start=True, stop=False)
                    nc.tensor.matmul(PS[:, 6, 0:DV + 1], M0.TQ[0:DQK, 2 * P:3 * P], M0.C[0:DQK, 0:DV + 1],
                                     start=False, stop=True).then_inc(mix0["outp"], 1)

            def tail(l, n_out, n_mlp, n_gate):
                transition(tm[l], Y, True)
                for j in range(4):
                    def wait_xt(t, j=j):
                        if j == 0:
                            pe.wait_ge(tm[l]["xt"], 2 * t + 2)
                    down_block(wo[l], (n_out + j) % 2, n_out + j, 16 * j, XTh, XTl, 2 * j, wait_xt,
                               behind=(lambda t: transpose_tile(tw[l], Y, True, t)) if j == 3 else None)
                transition(tw[l], Y, True, NT - 3)

                ph = mlp[l]
                qu, qd = n_mlp % 2, (n_mlp + 1) % 2
                uh = Wh[qu][:].rearrange("p (c n) -> p c n", c=NC)
                ul = Wl[qu][:].rearrange("p (c n) -> p c n", c=NC)

                def mlp_step(g, first=False, behind=None):
                    pe.wait_ge(split, 2 * g + (n_mlp + 1))
                    for j, (half, f) in enumerate(((0, 0), (0, 1), (1, 0), (1, 1))):
                        if first:
                            pe.wait_ge(tw[l]["xt"], 8 * half + 8)
                        else:
                            pe.wait_ge(ph["free"], 16 * g + (j - 3))
                        for c in range(NC):
                            last = mm3(PS[:, j, :], uh[:, c, f * P:(f + 1) * P], ul[:, c, f * P:(f + 1) * P],
                                       XTh[:, c, half * 512:half * 512 + 512], XTl[:, c, half * 512:half * 512 + 512],
                                       c == 0, c == NC - 1)
                        last.then_inc(ph["full"], 1)

                    def wait_ht(t):
                        if t % 4 == 0:
                            pe.wait_ge(ph["ht"], 4 * g + (2 if t == 0 else 4))

                    def wait_up(m):
                        pe.wait_ge(ph["ht"], 4 * g + (m + 1))
                    down_block(ph, qd, 2 * g + (n_mlp + 1), 16 * g, HTh, HTl, 0, wait_ht, wait_up, behind)

                mlp_step(0, True)
                with pe.Fori(1, NG - 1) as g:
                    mlp_step(g)
                mlp_step(NG - 1, behind=lambda t: transpose_tile(tp[l], H, False, t))
                transition(tp[l], H, False, NT - 3)

                ph = ple[l]
                for j in range(5):
                    if j in (1, 2):
                        hv = j - 1
                        pe.wait_ge(ph["pin"], 16 * hv + 16)
                        if hv == 0:
                            pe.wait_ge(tp[l]["xt"], 2 * NT)
                        else:
                            pe.wait_ge(ph["pt"], 2)
                        for c in range(2):
                            for k in range(4):
                                last = nc.tensor.transpose(PS[:, 4 + c, k * P:(k + 1) * P],
                                                           TMP[:, k * PLE + c * P:k * PLE + (c + 1) * P], IDN[:])
                            last.then_inc(ph["ptr"], 1)

                    def wait_in(t, j=j):
                        if j == 0:
                            pe.wait_ge(tp[l]["xt"], 2 * t + 2)
                        if j == 4 and t % 4 == 0:
                            pe.wait_ge(ph["pt"], 2 + t // 2)
                    stat = (HTh, HTl, 0) if j == 4 else (XTh, XTl, 2 * j)
                    down_block(ph, (n_gate + j) % 2, n_gate + j, 16 * j, *stat, wait_in,
                               behind=(lambda t: transpose_tile(te[l], Y, True, t)) if j == 4 and l == 0 else None)
                if l == 0:
                    transition(te[l], Y, True, NT - 3)

            tail(0, L0_OUT, L0_MLP, L0_GATE)

            M1 = layer1_views(H, G, TMP, HTh, HTl)
            pe.wait_ge(te[0]["xt"], 2 * NT)
            pe.wait_ge(mix1["const"], 1)
            with pe.Fori(0, HEADS) as h:
                def freeA(t):
                    if t >= 2:
                        pe.wait_ge(mix1["freeA"], 8 * h + (t - 1))

                def freeB(t):
                    if t < 2:
                        pe.wait_ge(mix1["freeA"], 8 * h + (7 + t))
                    else:
                        pe.wait_ge(mix1["freeB"], 8 * h + (t - 1))
                for t in range(NT):
                    gemm_tokens(mix1["fullA"], freeA, 2 * h + L1_HEADS, 0, 256, t)
                for t in range(NT):
                    gemm_tokens(mix1["fullB"], freeB, 2 * h + (L1_HEADS + 1), 1, 256, t)
                pe.wait_ge(mix1["lf"], h + 1)
                for c in range(NT):
                    if c:
                        pe.wait_ge(mix1["at"], 8 * h + c)
                    for b in range(2):
                        nc.tensor.matmul(PS[:, 4 + b, :], M1.LFh[:, c, :], M1.sums[:, b * 512:b * 512 + 512], start=True, stop=False)
                        nc.tensor.matmul(PS[:, 4 + b, :], M1.LFl[:, c, :], M1.sums[:, b * 512:b * 512 + 512], start=False, stop=True)
                    nc.tensor.matmul(PS[:, 7, 0:P], M1.sums[:, 8 * P:9 * P], M1.LFh[:, c, :], start=True, stop=False)
                    nc.tensor.matmul(PS[:, 7, 0:P], M1.sums[:, 8 * P:9 * P], M1.LFl[:, c, :], start=False, stop=True).then_inc(mix1["pe1"], 1)
                    nc.tensor.transpose(PS[:, 6, 0:P], M1.Zq[:, c, :], IDN[:])
                    nc.tensor.transpose(PS[:, 6, P:2 * P], M1.Zf[:, c, :], IDN[:]).then_inc(mix1["pe1"], 1)
                    pe.wait_ge(mix1["kg"], 8 * h + c + 1)
                    if c:
                        pe.wait_ge(mix1["state"], 8 * h + c)
                    nc.tensor.matmul(PS[:, 3, 0:P], M1.KG[:], M1.Zv[:, c, :], start=True, stop=True).then_inc(mix1["kv"], 1)
                    pe.wait_ge(mix1["qeke"], 8 * h + c + 1)
                    for l in range(LV + 1):
                        kk = M1.KE[:, l, :] if l < LV else M1.TQK[:, P:2 * P]
                        qq = M1.QE[:, l, :] if l < LV else M1.TQK[:, 0:P]
                        last = nc.tensor.matmul(PS[:, 4 + l // 4, (l % 4) * P:(l % 4 + 1) * P], kk, qq, start=True, stop=True)
                    last.then_inc(mix1["lev"], 1)
                    pe.wait_ge(mix1["at"], 8 * h + c + 1)
                    if c:
                        pe.wait_ge(mix1["oev"], 8 * h + c)
                    nc.tensor.matmul(PS[:, 2, 0:P], M1.AT[:], M1.Zv[:, c, :], start=True, stop=False)
                    nc.tensor.matmul(PS[:, 2, 0:P], M1.QG[:], M1.ST[:], start=False, stop=True).then_inc(mix1["outp"], 1)

            tail(1, L1_OUT, L1_MLP, L1_GATE)

        @block.scalar
        def _(act):
            link = Link(act, act_link)

            def transition(ph, post, pre, norm_pre=True, h_out=None):
                for k in range(NT + 3):
                    if post and k < NT:
                        act.wait_ge(post[0], post[1] + (2 * k + 2))
                        link(nc.scalar.activation(junk, Y[:, k, :], ACT.Square, accum_out=ssA[:, k:k + 1]))
                        nc.scalar.activation(sdA[:, k:k + 1], ssA[:, k:k + 1], ACT.Sqrt, bias=eps1[:], scale=1.0 / D).then_inc(ph["sdA"], 1)
                    t = k - 1
                    if 0 <= t < NT and post:
                        act.wait_ge(ph["hA"], t + 1)
                    if 0 <= t < NT and pre and norm_pre:
                        if not post:
                            act.wait_ge(ph["hin"], 16)
                        link(nc.scalar.activation(junk, H[:, t, :], ACT.Square, accum_out=ssB[:, t:t + 1]))
                        nc.scalar.activation(sdB[:, t:t + 1], ssB[:, t:t + 1], ACT.Sqrt, bias=eps1[:], scale=1.0 / D).then_inc(ph["sdB"], 1)
                    if 0 <= t < NT and h_out is not None:
                        act.dma_start(h_out[:, t, :], H[:, t, :]).then_inc(ph["hout"], 16)
                    t = k - 3
                    if t >= 0 and not (h_out is out_tok):
                        for b in range(2):
                            act.wait_ge(ph["tr"], 2 * t + b + 1)
                            nc.scalar.activation(XTh[:, 4 * b:4 * b + 4, t * P:(t + 1) * P],
                                                 PS[:, 4 + b, :].rearrange("p (k n) -> p k n", k=4), ACT.Copy).then_inc(ph["hi"], 1)

            def gain(ph, slot, row):
                act.dma_start(G[:, slot, :], row.partition_broadcast(P)).then_inc(ph["gain"], 16)

            act.wait_ge(ready, 2)
            gain(start, 1, norm_gains[0, 0])
            act.dma_start(H[:], x_tok).then_inc(start["hin"], 16)
            transition(start, False, True)

            M0 = layer0_views(H, G, TMP)
            R = lambda i: Y[0:HEADS, i, :]
            act.wait_ge(start["xt"], 2 * NT)
            act.dma_start(M0.causal, c_causal).then_inc(mix0["const"], 16)
            act.dma_start(rows8[:, 0:1], a_ig_bias.rearrange("a h -> h a")).then_inc(mix0["const"], 16)
            act.dma_start(rows8[:, 1:2], a_fg_bias.rearrange("a h -> h a") if len(a_fg_bias.shape) == 2
                          else a_fg_bias.rearrange("(h a) -> h a", a=1)).then_inc(mix0["const"], 16)
            act.wait_ge(mix0["const"], 48)
            for half in range(2):
                hs = slice(half * 512, half * 512 + 512)
                act.wait_ge(mix0["full"], half + 1)
                nc.scalar.activation(R(0)[:, hs], PS[0:HEADS, half, :], ACT.Identity, bias=rows8[:, 0:1]).then_inc(mix0["free"], 1)
            for half in range(2):
                hs = slice(half * 512, half * 512 + 512)
                act.wait_ge(mix0["full"], 2 + half + 1)
                nc.scalar.activation(R(1)[:, hs], PS[0:HEADS, 2 + half, :], ACT.Identity, bias=rows8[:, 1:2]).then_inc(mix0["free"], 1)
            act.wait_ge(mix0["free"], 4)
            link(nc.scalar.activation(R(2), R(1), ACT.Abs))
            link(nc.scalar.activation(R(2), R(2), ACT.Exp, scale=-1.0))
            nc.scalar.activation(R(2), R(2), ACT.Ln, bias=1.0).then_inc(mix0["scal"], 1)
            act.wait_ge(mix0["scal"], 2)
            nc.scalar.activation(Y[0:HEADS, 4:7, :], Y[0:HEADS, 4:7, :], ACT.Exp).then_inc(mix0["rows"], 1)
            nc.scalar.activation(rows8[:, 16:24], rows8[:, 16:24], ACT.Exp).then_inc(mix0["scratch"], 1)
            act.wait_ge(mix0["scratch"], 1)
            act.dma_start(dec_dram, rows8[:, 16:24]).then_inc(mix0["saved"], 16)
            act.dma_start(negm_dram, R(7)).then_inc(mix0["saved"], 16)
            act.wait_ge(mix0["saved"], 32)
            act.dma_start(M0.DEC[:], dec_dram.rearrange("h c -> (h c)").partition_broadcast(P)).then_inc(mix0["decb"], 16)
            with act.Fori(0, HEADS) as h:
                act.dma_start(M0.NM, negm_dram[bass.ds(h, 1), :].rearrange("a n -> (a n)").partition_broadcast(P)).then_inc(mix0["bcast"], 16)
                for t in range(NT):
                    act.wait_ge(mix0["full"], 16 * h + (4 + t + 1))
                    nc.scalar.activation(M0.z[:, t, 0:256], PS[:, t % 2, 0:256], ACT.Copy).then_inc(mix0["free"], 1)
                for t in range(NT):
                    if t == 0:
                        act.wait_ge(mix0["done"], h + 1)
                    act.wait_ge(mix0["full"], 16 * h + (12 + t + 1))
                    nc.scalar.activation(M0.O[:, t, :], PS[:, t % 2, 0:DV], ACT.Sigmoid).then_inc(mix0["free"], 1)
                act.wait_ge(mix0["args"], h + 1)
                nc.scalar.activation(M0.PR[:], M0.PR[:], ACT.Exp).then_inc(mix0["probs"], 1)
                for c in range(NT):
                    act.wait_ge(mix0["tr"], 8 * h + c + 1)
                    if c:
                        act.wait_ge(mix0["outp"], 8 * h + c)
                    nc.scalar.activation(M0.TQ[0:DQK, :], PS[0:DQK, 4, 0:3 * P], ACT.Copy).then_inc(mix0["tq"], 1)
                    act.wait_ge(mix0["outp"], 8 * h + c + 1)
                    nc.scalar.activation(M0.NUM[:, c, 0:DV + 1], PS[:, 6, 0:DV + 1], ACT.Copy).then_inc(mix0["num"], 1)
                act.wait_ge(mix0["den"], 2 * h + 1)
                nc.scalar.activation(M0.den, M0.den, ACT.Abs).then_inc(mix0["postL"], 1)
                act.wait_ge(mix0["den"], 2 * h + 2)
                nc.scalar.activation(M0.rs, M0.rs, ACT.Ln, bias=eps1[:], scale=1.0 / DV).then_inc(mix0["postL"], 1)
                act.wait_ge(mix0["postL"], 3 * h + 2)
                nc.scalar.activation(M0.rs, M0.rs, ACT.Exp, scale=-0.5).then_inc(mix0["postL"], 1)

            def tail(l, head_gain, h_src, mix_done):
                mix_done()
                gain(tm[l], 1, head_gain[0].rearrange("h v -> (h v)"))
                act.dma_start(H[:], h_src).then_inc(tw[l]["hin"], 16)
                transition(tm[l], False, True, norm_pre=False)
                act.wait_ge(tm[l]["xt"], 2 * NT)
                gain(tw[l], 0, norm_gains[l, 1])
                gain(tw[l], 1, norm_gains[l, 2])
                transition(tw[l], (wo[l]["free"], 48), True)
                act.wait_ge(tw[l]["xt"], 2 * NT)
                gain(tp[l], 0, norm_gains[l, 3])
                ph = mlp[l]

                def mlp_step(g):
                    for j, (half, f) in enumerate(((0, 0), (0, 1), (1, 0), (1, 1))):
                        sq = TMP[:, (j % 2) * 512:(j % 2) * 512 + 512]
                        act.wait_ge(ph["full"], 20 * g + (j + 1))
                        if j >= 2 or not isinstance(g, int):
                            act.wait_ge(ph["ht"], 4 * g + (j - 1))
                        link(nc.scalar.activation(sq, PS[:, j, :], ACT.Relu))
                        link(nc.scalar.activation(sq, sq, ACT.Square))
                        nc.scalar.activation(HTh[:, f, half * 512:half * 512 + 512], sq, ACT.Copy).then_inc(ph["hi"], 1)
                mlp_step(0)
                base = link.base + link.n
                with act.Fori(1, NG) as g:
                    link.base, link.n = 8 * g + (base - 8), 0
                    mlp_step(g)
                link.base, link.n = base + 8 * (NG - 1), 0
                transition(tp[l], (mlp[l]["free"], 16 * (NG - 1)), True, norm_pre=False)
                act.wait_ge(tp[l]["xt"], 2 * NT)
                gain(te[l], 0, norm_gains[l, 4])
                if l == 0:
                    gain(te[l], 1, norm_gains[1, 0])
                ph = ple[l]
                for hv in range(2):
                    if hv == 0:
                        act.wait_ge(mlp[l]["ht"], 4 * NG)
                    else:
                        act.wait_ge(ph["ptr"], 2)
                    act.dma_start(TMP[:].rearrange("p (k n) -> p k n", k=4),
                                  tok(p[l, 0])[:, 4 * hv:4 * hv + 4, :]).then_inc(ph["pin"], 16)
                    for c in range(2):
                        act.wait_ge(ph["ptr"], 2 * hv + c + 1)
                        nc.scalar.activation(HTh[:, c, hv * 512:hv * 512 + 512], PS[:, 4 + c, :], ACT.Copy).then_inc(ph["phi"], 1)
                for t in range(NT):
                    act.wait_ge(ph["free"], 48 + 2 * t + 2)
                    nc.scalar.activation(Y[:, t, :], Y[:, t, :], ACT.Sigmoid).then_inc(ph["sig"], 1)
                transition(te[l], (ple[l]["free"], 64), l == 0, h_out=h_tok if l == 0 else out_tok)

            def mix0_done():
                act.wait_ge(mix0["done"], HEADS + 1)
            tail(0, a_head_gain, x_tok, mix0_done)

            M1 = layer1_views(H, G, TMP, HTh, HTl)
            act.wait_ge(te[0]["hout"], 16 * NT)
            act.wait_ge(te[0]["xt"], 2 * NT)
            act.dma_start(Y[:, 0:2, :].rearrange("p a n -> p (a n)")[:, 0:(LV + 2) * P],
                          c_sums.rearrange("p l n -> p (l n)")).then_inc(mix1["bound"], 16)
            act.dma_start(M1.MASK[:], c_level_mask.rearrange("p l n -> p (l n)")).then_inc(mix1["bound"], 16)
            act.dma_start(Y[:, 2:4, :].rearrange("p a n -> p (a n)"),
                          b_lower_bound.rearrange("a n -> (a n)").partition_broadcast(P)).then_inc(mix1["bound"], 16)
            act.wait_ge(mix1["boundS"], 1)
            nc.scalar.activation(M1.OML[:], Y[:, 2, :], ACT.Sigmoid).then_inc(mix1["oml"], 1)
            with act.Fori(0, HEADS) as h:
                act.wait_ge(mix1["done"], h + 1)
                for t in range(NT):
                    act.wait_ge(mix1["fullA"], 8 * h + t + 1)
                    nc.scalar.activation(M1.Zq[:, t, :], PS[:, t % 2, 0:P], ACT.Copy)
                    nc.scalar.activation(M1.Zf[:, t, :], PS[:, t % 2, P:2 * P], ACT.Sigmoid, scale=-1.0).then_inc(mix1["freeA"], 1)
                for t in range(NT):
                    act.wait_ge(mix1["fullB"], 8 * h + t + 1)
                    nc.scalar.activation(M1.Zv[:, t, :], PS[:, t % 2, 0:P], ACT.Copy)
                    nc.scalar.activation(M1.Zg[:, t, :], PS[:, t % 2, P:2 * P], ACT.Sigmoid).then_inc(mix1["sg"], 1)
                act.wait_ge(mix1["onem"], h + 1)
                nc.scalar.activation(TMP[:], TMP[:], ACT.Ln).then_inc(mix1["lnf"], 1)
                act.wait_ge(mix1["lnf"], h + 1)
                nc.scalar.activation(M1.LFh[:].rearrange("p t n -> p (t n)"), TMP[:], ACT.Copy).then_inc(mix1["lfhi"], 1)
                for c in range(NT):
                    act.wait_ge(mix1["pe1"], 16 * h + (2 * c + 1))
                    if c:
                        act.wait_ge(mix1["at"], 8 * h + c)
                        act.wait_ge(mix1["state"], 8 * h + c)
                    nc.scalar.activation(M1.E[:], PS[:, 4:6, :].rearrange("p a n -> p (a n)"), ACT.Exp).then_inc(mix1["decays"], 1)
                    if c:
                        act.wait_ge(mix1["kv"], 8 * h + c)
                    nc.scalar.activation(M1.KG[:], PS[:, 7, 0:P], ACT.Exp).then_inc(mix1["decays"], 1)
                    act.wait_ge(mix1["outp"], 8 * h + c + 1)
                    nc.scalar.activation(M1.Zq[:, c, :], PS[:, 2, 0:P], ACT.Copy).then_inc(mix1["oev"], 1)
                act.wait_ge(mix1["ss"], h + 1)
                nc.scalar.activation(M1.rs, M1.rs, ACT.Ln, bias=eps1[:], scale=1.0 / DV).then_inc(mix1["rstd"], 1)
                act.wait_ge(mix1["rstd"], 2 * h + 1)
                nc.scalar.activation(M1.rs, M1.rs, ACT.Exp, scale=-0.5).then_inc(mix1["rstd"], 1)

            def mix1_done():
                act.wait_ge(mix1["done"], HEADS + 1)
            tail(1, b_head_gain, h_tok, mix1_done)
            act.wait_ge(te[1]["hout"], 16 * NT)

        @block.vector
        def _(dve):
            link = Link(dve, dve_link)
            V = nc.vector

            def stage_a(ph, t):
                dve.wait_ge(ph["sdA"], t + 1)
                link(V.reciprocal(rA[:, t:t + 1], sdA[:, t:t + 1]))
                link(V.scalar_tensor_tensor(out=Y[:, t, :], in0=Y[:, t, :], scalar=rA[:, t:t + 1], in1=G[:, 0, :],
                                            op0=ALU.mult, op1=ALU.mult))
                V.tensor_tensor(H[:, t, :], H[:, t, :], Y[:, t, :], ALU.add).then_inc(ph["hA"], 1)

            def stage_b(ph, t, norm, post):
                if norm:
                    dve.wait_ge(ph["sdB"], t + 1)
                    if post:
                        dve.wait_ge(ph["hA"], t + 1)
                    link(V.reciprocal(rB[:, t:t + 1], sdB[:, t:t + 1]))
                    V.scalar_tensor_tensor(out=Y[:, t, :], in0=H[:, t, :], scalar=rB[:, t:t + 1], in1=G[:, 1, :],
                                           op0=ALU.mult, op1=ALU.mult).then_inc(ph["xs"], 1)
                else:
                    V.tensor_tensor(Y[:, t, :], Y[:, t, :], G[:, 1, :], ALU.mult).then_inc(ph["xs"], 1)

            def stage_c(ph, t):
                for b in range(2):
                    dve.wait_ge(ph["hi"], 2 * t + b + 1)
                    V.tensor_tensor(XTl[:, 4 * b:4 * b + 4, t * P:(t + 1) * P],
                                    PS[:, 4 + b, :].rearrange("p (k n) -> p k n", k=4),
                                    XTh[:, 4 * b:4 * b + 4, t * P:(t + 1) * P].bitcast(F32), ALU.subtract).then_inc(ph["xt"], 1)

            def transition(ph, finish, post, pre, norm_pre, c_on, gains):
                for k in range(NT + 3):
                    if finish and k < NT:
                        finish(k)
                    if k == 1:
                        dve.wait_ge(ph["gain"], 16 * gains)
                    if post and 0 <= k - 1 < NT:
                        stage_a(ph, k - 1)
                    if pre and 0 <= k - 2 < NT:
                        stage_b(ph, k - 2, norm_pre, post)
                    if c_on and 0 <= k - 3 < NT:
                        stage_c(ph, k - 3)

            dve.wait_ge(ready, 2)
            transition(start, None, False, True, True, True, 1)

            M0 = layer0_views(H, G, TMP)
            R = lambda i: Y[0:HEADS, i, :]
            dve.wait_ge(mix0["scal"], 1)
            dve.wait_ge(mix0["free"], 4)
            link(V.memset(rows8[:, 8:9], 0.0))
            dve.wait_ge(start["xs"], NT)
            link(V.scalar_tensor_tensor(out=R(1), in0=R(1), scalar=0.0, in1=R(2), op0=ALU.min, op1=ALU.subtract))
            link(V.memset(R(2), 1.0))
            ones = TMP[0:HEADS, 0:P]
            link(V.memset(ones, 1.0))
            for c in range(NT):
                cs = slice(c * P, c * P + P)
                last = V.tensor_tensor_scan(out=R(2)[:, cs], data0=ones, data1=R(1)[:, cs], initial=0.0,
                                            op0=ALU.mult, op1=ALU.add)
            link(last)
            link(V.tensor_tensor(R(3), R(0), R(2), ALU.subtract))
            for c in range(NT):
                cs = slice(c * P, c * P + P)
                link(V.tensor_tensor_scan(out=R(1)[:, cs], data0=R(3)[:, cs], data1=R(3)[:, cs],
                                          initial=rows8[:, 8 + c:9 + c], op0=ALU.max, op1=ALU.max))
                if c < NT - 1:
                    link(V.tensor_tensor(rows8[:, 9 + c:10 + c], R(2)[:, c * P + P - 1:c * P + P],
                                         R(1)[:, c * P + P - 1:c * P + P], ALU.add))
            v3 = lambda i: R(i).rearrange("h (c t) -> h c t", c=NT)
            mst = rows8[:, 8:16].unsqueeze(2).to_broadcast([HEADS, NT, P])
            ml = v3(1)[:, :, P - 1:P].to_broadcast([HEADS, NT, P])
            V.tensor_tensor(v3(4), mst, v3(1), ALU.subtract)
            V.tensor_tensor(v3(5), v3(3), ml, ALU.subtract)
            V.scalar_tensor_tensor(out=R(6), in0=R(2), scalar=-1.0, in1=R(1), op0=ALU.mult, op1=ALU.subtract)
            V.tensor_scalar(R(7), R(1), -1.0, None, ALU.mult)
            V.tensor_tensor(rows8[:, 16:24], rows8[:, 8:16], v3(1)[:, :, P - 1], ALU.subtract).then_inc(mix0["scal"], 1)
            dve.wait_ge(mix0["rows_tr"], 1)
            link(V.tensor_copy(M0.TS[:], PS[:, 4, 0:4 * NT * HEADS]))
            V.memset(M0.z[:, :, 256:257], 1.0).then_inc(mix0["done"], 1)
            ts = M0.TS[:].rearrange("p (q c h) -> p q c h", q=4, c=NT)
            base0 = link.n
            dve.wait_ge(mix0["decb"], 16)
            with dve.Fori(0, HEADS) as h:
                per = LINKS0
                link.base, link.n = h * per + base0, 0
                link(V.tensor_copy(M0.th[:], ts[:, :, :, bass.ds(h, 1)]))
                u, wi, wk, em = (M0.th[:, i * NT:(i + 1) * NT, 0] for i in range(4))
                dve.wait_ge(mix0["bcast"], 16 * h + 16)
                link(V.tensor_tensor(M0.PR3, M0.NM3, u.unsqueeze(2).to_broadcast([P, NT, P]), ALU.add))
                V.tensor_tensor(M0.PR3, M0.PR3, M0.causal.unsqueeze(1).to_broadcast([P, NT, P]), ALU.min).then_inc(mix0["args"], 1)
                dve.wait_ge(mix0["free"], 16 * h + 12)
                link(V.tensor_scalar(M0.QS[:], M0.z[:, :, 0:DQK], DQK ** -0.5, None, ALU.mult))
                V.tensor_tensor(M0.QW[:], M0.QS[:], wi.unsqueeze(2).to_broadcast([P, NT, DQK]), ALU.mult)
                link(V.memset(M0.C[:], 0.0))
                V.tensor_tensor(M0.KW[:], M0.z[:, :, DQK:2 * DQK], wk.unsqueeze(2).to_broadcast([P, NT, DQK]),
                                ALU.mult).then_inc(mix0["prep"], 1)
                dve.wait_ge(mix0["probs"], h + 1)
                for c in range(NT):
                    dve.wait_ge(mix0["qk"], 8 * h + c + 1)
                    V.tensor_tensor(M0.ST[:], PS[:, 5, 0:P], M0.PR3[:, c, :], ALU.mult).then_inc(mix0["st"], 1)
                    dve.wait_ge(mix0["outp"], 8 * h + c + 1)
                    dve.wait_ge(mix0["kv"], 8 * h + c + 1)
                    link(V.tensor_copy(M0.dec1[0:DQK, :], M0.DEC[0:DQK, bass.ds(h * NT + c, 1)]))
                    V.scalar_tensor_tensor(out=M0.C[0:DQK, :], in0=M0.C[0:DQK, :], scalar=M0.dec1[0:DQK, :],
                                           in1=PS[0:DQK, 7, 0:DV + 1], op0=ALU.mult, op1=ALU.add).then_inc(mix0["state"], 1)
                dve.wait_ge(mix0["num"], 8 * h + 8)
                dve.wait_ge(mix0["state"], 8 * h + 8)
                V.tensor_copy(M0.den, M0.NUM[:, :, DV]).then_inc(mix0["den"], 1)
                dve.wait_ge(mix0["postL"], 3 * h + 1)
                link(V.tensor_tensor(M0.den, M0.den, em, ALU.max))
                link(V.reciprocal(M0.den, M0.den))
                link(V.tensor_tensor(M0.NUM[:, :, 0:DV], M0.NUM[:, :, 0:DV], M0.den.unsqueeze(2).to_broadcast([P, NT, DV]), ALU.mult))
                link(V.tensor_tensor(M0.PR3, M0.NUM[:, :, 0:DV], M0.NUM[:, :, 0:DV], ALU.mult))
                V.tensor_reduce(M0.rs, M0.PR3, AX_X, ALU.add).then_inc(mix0["den"], 1)
                dve.wait_ge(mix0["postL"], 3 * h + 3)
                dve.wait_ge(mix0["free"], 16 * h + 20)
                link(V.tensor_tensor(M0.NUM[:, :, 0:DV], M0.NUM[:, :, 0:DV], M0.rs.unsqueeze(2).to_broadcast([P, NT, DV]), ALU.mult))
                V.tensor_tensor(Y[:, :, bass.ds(h * DV, DV)], M0.NUM[:, :, 0:DV], M0.O[:], ALU.mult).then_inc(mix0["done"], 1)
                assert link.n == per, link.n
            link.base, link.n = base0 + HEADS * LINKS0, 0

            def tail(l):
                dve.wait_ge(mix0["done"] if l == 0 else mix1["done"], HEADS + 1)
                transition(tm[l], None, False, True, False, True, 1)

                def sums(ph, k0, j, t):
                    for nh in range(2):
                        m = 2 * t + nh
                        dve.wait_ge(ph["full"], k0 + (m + 1))
                        ys = Y[:, t, nh * 512:nh * 512 + 512]
                        if j == 0:
                            V.tensor_copy(ys, PS[:, m % 4, :]).then_inc(ph["free"], 1)
                        else:
                            V.tensor_tensor(ys, ys, PS[:, m % 4, :], ALU.add).then_inc(ph["free"], 1)

                def finish(ph, k0):
                    return lambda t: sums(ph, k0, 1, t)

                for j in range(3):
                    for t in range(NT):
                        sums(wo[l], 16 * j, j, t)
                dve.wait_ge(tw[l]["hin"], 16)
                transition(tw[l], finish(wo[l], 48), True, True, True, True, 2)

                ph = mlp[l]

                def lo_part(g, j, half, f):
                    dve.wait_ge(ph["hi"], 4 * g + (j + 1))
                    V.tensor_tensor(HTl[:, f, half * 512:half * 512 + 512], TMP[:, (j % 2) * 512:(j % 2) * 512 + 512],
                                    HTh[:, f, half * 512:half * 512 + 512].bitcast(F32), ALU.subtract).then_inc(ph["ht"], 1)

                def mlp_up(g):
                    for j, (half, f) in enumerate(((0, 0), (0, 1), (1, 0), (1, 1))):
                        lo_part(g, j, half, f)

                mlp_up(0)
                for t in range(NT):
                    sums(ph, 4, 0, t)
                with dve.Fori(1, NG - 1) as g:
                    mlp_up(g)
                    for t in range(NT):
                        sums(ph, 20 * g + 4, 1, t)
                mlp_up(NG - 1)
                transition(tp[l], finish(ph, 20 * (NG - 1) + 4), True, False, False, True, 1)

                ph = ple[l]
                for j in range(3):
                    for t in range(NT):
                        sums(ph, 16 * j, j, t)
                    if j in (0, 1):
                        for c in range(2):
                            dve.wait_ge(ph["phi"], 2 * j + c + 1)
                            V.tensor_tensor(HTl[:, c, j * 512:j * 512 + 512], PS[:, 4 + c, :],
                                            HTh[:, c, j * 512:j * 512 + 512].bitcast(F32), ALU.subtract).then_inc(ph["pt"], 1)
                for t in range(NT):
                    sums(ph, 48, 3, t)

                def gated(t):
                    dve.wait_ge(ph["sig"], t + 1)
                    for nh in range(2):
                        m = 2 * t + nh
                        dve.wait_ge(ph["full"], 64 + m + 1)
                        ys = Y[:, t, nh * 512:nh * 512 + 512]
                        V.tensor_tensor(ys, ys, PS[:, m % 4, :], ALU.mult).then_inc(ph["free"], 1)
                transition(te[l], gated, True, l == 0, True, l == 0, 2 if l == 0 else 1)

            tail(0)

            M1 = layer1_views(H, G, TMP, HTh, HTl)
            dve.wait_ge(mix1["bound"], 48)
            V.tensor_copy(M1.sums[:], Y[:, 0:2, :].rearrange("p a n -> p (a n)")[:, 0:(LV + 2) * P]).then_inc(mix1["const"], 1)
            V.tensor_tensor(Y[:, 2, :], Y[:, 2, :], Y[:, 3, :], ALU.subtract).then_inc(mix1["boundS"], 1)
            V.memset(M1.dec, 0.0).then_inc(mix1["done"], 1)
            dve.wait_ge(mix1["oml"], 1)
            b1 = link.base + link.n
            with dve.Fori(0, HEADS) as h:
                link.base, link.n = h * LINKS1 + b1, 0
                for t in range(NT):
                    dve.wait_ge(mix1["sg"], 8 * h + t + 1)
                    V.tensor_tensor(M1.Zg[:, t, :], M1.Zg[:, t, :], PS[:, t % 2, P:2 * P], ALU.mult).then_inc(mix1["freeB"], 1)
                dve.wait_ge(mix1["freeA"], 8 * h + 8)
                link(V.tensor_tensor(M1.Zf[:], M1.Zf[:], M1.OML[:, bass.ds(h * P, P)].unsqueeze(1).to_broadcast([P, NT, P]), ALU.mult))
                link(V.tensor_scalar(TMP[:], M1.Zf[:].rearrange("p t n -> p (t n)"), -1.0, 1.0, ALU.mult, ALU.add))
                V.tensor_scalar(TMP[:], TMP[:], 1e-9, None, ALU.max).then_inc(mix1["onem"], 1)
                dve.wait_ge(mix1["lfhi"], h + 1)
                V.tensor_tensor(M1.LFl[:].rearrange("p t n -> p (t n)"), TMP[:],
                                M1.LFh[:].rearrange("p t n -> p (t n)").bitcast(F32), ALU.subtract).then_inc(mix1["lf"], 1)
                link(V.memset(M1.ST[:], 0.0))
                E3 = M1.E[:].rearrange("p (l n) -> p l n", n=P)
                for c in range(NT):
                    dve.wait_ge(mix1["pe1"], 16 * h + 2 * c + 2)
                    link(V.tensor_copy(M1.TQK[:], PS[:, 6, 0:2 * P]))
                    dve.wait_ge(mix1["decays"], 16 * h + 2 * c + 2)
                    V.tensor_tensor(M1.KG[:], M1.KG[:], M1.Zf[:, c, :], ALU.mult).then_inc(mix1["kg"], 1)
                    V.tensor_tensor(M1.QG[:], M1.TQK[:, 0:P], E3[:, LV, :], ALU.mult)
                    V.tensor_copy(M1.dec, E3[:, LV, P - 1:P])
                    V.tensor_tensor(M1.QE[:], M1.TQK[:, 0:P].unsqueeze(1).to_broadcast([P, LV, P]), E3[:, 0:LV, :], ALU.mult)
                    V.tensor_tensor(M1.KE[:], M1.TQK[:, P:2 * P].unsqueeze(1).to_broadcast([P, LV, P]), E3[:, 0:LV, :],
                                    ALU.mult).then_inc(mix1["qeke"], 1)
                    dve.wait_ge(mix1["qeke"], 8 * h + c + 1)
                    dve.wait_ge(mix1["lev"], 8 * h + c + 1)
                    link(V.tensor_tensor(M1.E[:], PS[:, 4:6, :].rearrange("p a n -> p (a n)"), M1.MASK[:], ALU.mult))
                    V.tensor_reduce(M1.AT[:], M1.E[:].rearrange("p (l n) -> p n l", n=P), AX_X, ALU.add).then_inc(mix1["at"], 1)
                    dve.wait_ge(mix1["outp"], 8 * h + c + 1)
                    V.scalar_tensor_tensor(out=M1.ST[:], in0=M1.ST[:], scalar=M1.dec, in1=PS[:, 3, 0:P],
                                           op0=ALU.mult, op1=ALU.add).then_inc(mix1["state"], 1)
                dve.wait_ge(mix1["oev"], 8 * h + 8)
                T3 = TMP[:].rearrange("p (t n) -> p t n", n=P)
                link(V.tensor_tensor(T3, M1.Zq[:], M1.Zq[:], ALU.mult))
                V.tensor_reduce(M1.rs, T3, AX_X, ALU.add).then_inc(mix1["ss"], 1)
                dve.wait_ge(mix1["rstd"], 2 * h + 2)
                link(V.tensor_tensor(M1.Zq[:], M1.Zq[:], M1.rs.unsqueeze(2).to_broadcast([P, NT, P]), ALU.mult))
                V.tensor_tensor(Y[:, :, bass.ds(h * P, P)], M1.Zq[:], M1.Zg[:], ALU.mult).then_inc(mix1["done"], 1)
                assert link.n == LINKS1, link.n
            link.base, link.n = b1 + HEADS * LINKS1, 0
            tail(1)


LINKS0 = 4 + 8 + 5
LINKS1 = 3 + 2 * 8 + 2


class Views:
    pass


def layer0_views(H, G, TMP):
    v = Views()
    flat = H[:].rearrange("p t n -> p (t n)")
    at = [0]

    def take(src, n):
        a = src[:, at[0]:at[0] + n]
        at[0] += n
        return a
    v.z = take(flat, NT * 260).rearrange("p (t n) -> p t n", n=260)
    v.O = take(flat, NT * DV).rearrange("p (t n) -> p t n", n=DV)
    v.QS = take(flat, NT * DQK).rearrange("p (t n) -> p t n", n=DQK)
    v.QW = take(flat, NT * DQK).rearrange("p (t n) -> p t n", n=DQK)
    v.KW = take(flat, NT * DQK).rearrange("p (t n) -> p t n", n=DQK)
    v.PR = take(flat, S)
    v.PR3 = v.PR.rearrange("p (t n) -> p t n", n=P)
    v.NM = take(flat, S)
    v.NM3 = v.NM.rearrange("p (t n) -> p t n", n=P)
    v.NUM = take(flat, NT * 132).rearrange("p (t n) -> p t n", n=132)
    assert at[0] <= NT * D
    g = G[:].rearrange("p a n -> p (a n)")
    at[0] = 0
    v.TQ = take(g, 3 * P)
    v.ST = take(g, P)
    v.C = take(g, DV + 1)
    v.dec1 = take(g, 1)
    v.DEC = take(g, HEADS * NT)
    v.TS = take(g, 4 * NT * HEADS)
    v.th = take(g, 4 * NT).rearrange("p (q a) -> p q a", a=1)
    v.den = take(g, NT)
    v.rs = take(g, NT)
    v.causal = take(g, P)
    return v


def layer1_views(H, G, TMP, HTh, HTl):
    v = Views()
    flat = H[:].rearrange("p t n -> p (t n)")
    at = [0]

    def take(src, n):
        a = src[:, at[0]:at[0] + n]
        at[0] += n
        return a
    v.Zq, v.Zf, v.Zv, v.Zg = (take(flat, S).rearrange("p (t n) -> p t n", n=P) for _ in range(4))
    v.OML = take(flat, D)
    v.E = take(flat, (LV + 1) * P)
    v.QE = take(flat, LV * P).rearrange("p (l n) -> p l n", n=P)
    v.KE = take(flat, LV * P).rearrange("p (l n) -> p l n", n=P)
    v.ST = take(flat, P)
    g = G[:].rearrange("p a n -> p (a n)")
    at[0] = 0
    v.MASK = take(g, (LV + 1) * P)
    v.TQK = take(g, 2 * P)
    v.AT = take(g, P)
    v.QG = take(g, P)
    v.KG = take(g, P)
    v.dec = take(g, 1)
    v.rs = take(g, NT)
    hh = HTh[:].rearrange("p a n -> p (a n)")
    hl = HTl[:].rearrange("p a n -> p (a n)")
    v.sums = hh[:, 0:(LV + 2) * P]
    v.LFh = hl[:, 0:S].rearrange("p (t n) -> p t n", n=P)
    v.LFl = hl[:, S:2 * S].rearrange("p (t n) -> p t n", n=P)
    return v


_INS = ["x", "p", "norm_gains", "mlp_w_up", "mlp_w_down", "ple_w_up", "ple_w_gate",
        "a_w_in", "a_ig_bias", "a_fg_bias", "a_head_gain", "a_w_out",
        "b_w_in", "b_lower_bound", "b_head_gain", "b_w_out"]


def kernel(**inputs):
    import concourse.bacc as _bacc
    from concourse import mybir as _mybir
    from concourse.bass_utils import run_bass_kernel_spmd as _run

    nc = _bacc.Bacc("TRN2", target_bir_lowering=False, num_devices=1)
    arrays, args = {}, []
    named = [(n, np.ascontiguousarray(inputs[n])) for n in _INS] + list(shape_constants().items())
    for name, a in named:
        arrays[f"in_{name}_dram"] = a
        args.append(nc.dram_tensor(f"in_{name}_dram", a.shape, _mybir.dt.from_np(a.dtype), kind="ExternalInput").ap())
    args.append(nc.dram_tensor("out_0_dram", (1, S, D), F32, kind="ExternalOutput").ap())
    trunk(nc, *args)
    r = _run(nc, [arrays], core_ids=[0])
    return r.results[0]["out_0_dram"]
```

```python
from contextlib import ExitStack

import numpy as np

import concourse.bass as bass
from concourse import mybir

P = 128
D = 1024
S = 1024
NT = S // P
NC = D // P
FF = 4 * D
FG = 256
NG = FF // FG
BLK = D * 256 // P
HEADS = 8
DQK = 64
DV = 128
PLE = 256
EPS = 1e-6
LV = 7
NEG = -3.0e38

ALU = mybir.AluOpType
ACT = mybir.ActivationFunctionType
F32 = mybir.dt.float32
F32R = mybir.dt.float32r
AX_X = mybir.AxisListType.X

L0_GATES = 0
L0_HEADS = 1
L0_OUT = L0_HEADS + 2 * HEADS
L0_MLP = L0_OUT + 4
L0_GATE = L0_MLP + 2 * NG
L1_HEADS = L0_GATE + 5
L1_OUT = L1_HEADS + 2 * HEADS
L1_MLP = L1_OUT + 4
L1_GATE = L1_MLP + 2 * NG
BLOCKS = L1_GATE + 5
LOADED = 48


def shape_constants():
    i = np.arange(P)
    s, t = i[:, None], i[None, :]
    sums = np.zeros((P, LV + 2, P), np.float32)
    mask = np.zeros((P, LV + 1, P), np.float32)
    for l in range(LV):
        m = 64 >> l
        mid = (t // (2 * m)) * 2 * m + m
        sums[:, l] = np.where(t >= mid, (s >= mid) & (s <= t), (s > t) & (s < mid))
        mask[:, l] = (s // (2 * m) == t // (2 * m)) & (s % (2 * m) < m) & (t % (2 * m) >= m)
    sums[:, LV] = s <= t
    sums[:, LV + 1] = s > t
    mask[:, LV] = s == t
    causal = np.where(s <= t, 0.0, NEG).astype(np.float32)
    return {"c_sums": sums, "c_level_mask": mask, "c_causal": causal, "c_ident": np.eye(P, dtype=np.float32)}


class Link:

    def __init__(self, eng, sem):
        self.eng, self.sem, self.base, self.n = eng, sem, 0, 0

    def __call__(self, ins):
        ins.then_inc(self.sem, 1)
        self.n += 1
        self.eng.wait_ge(self.sem, self.base + self.n)


def trunk(nc, x, p, norm_gains, mlp_w_up, mlp_w_down, ple_w_up, ple_w_gate,
          a_w_in, a_ig_bias, a_fg_bias, a_head_gain, a_w_out,
          b_w_in, b_lower_bound, b_head_gain, b_w_out,
          c_sums, c_level_mask, c_causal, c_ident, out):
    ctx = ExitStack()
    with ctx:
        def sb(name, shape, dt=F32):
            return ctx.enter_context(nc.sbuf_tensor(name, shape, dt))

        def sem(name):
            return ctx.enter_context(nc.semaphore(name))

        XTh = sb("XTh", [P, NC, S], F32R)
        XTl = sb("XTl", [P, NC, S], F32R)
        H = sb("H", [P, NT, D])
        Y = sb("Y", [P, NT, D])
        Wh = [sb(f"Wh{i}", [P, BLK], F32R) for i in range(2)]
        Wl = [sb(f"Wl{i}", [P, BLK], F32R) for i in range(2)]
        Wraw = [sb(f"Wraw{i}", [P, BLK]) for i in range(2)]
        HTh = sb("HTh", [P, 2, S], F32R)
        HTl = sb("HTl", [P, 2, S], F32R)
        G = sb("G", [P, 2, D])
        TMP = sb("TMP", [P, D])
        IDN = sb("IDN", [P, P])
        zero1 = sb("zero1", [P, 1])
        eps1 = sb("eps1", [P, 1])
        ssA = sb("ssA", [P, NT])
        sdA = sb("sdA", [P, NT])
        rA = sb("rA", [P, NT])
        ssB = sb("ssB", [P, NT])
        sdB = sb("sdB", [P, NT])
        rB = sb("rB", [P, NT])
        small = sb("small", [P, 64])
        rows8 = sb("rows8", [HEADS, 32])
        PS = ctx.enter_context(nc.psum_tensor("PS", [P, 8, 512], F32))
        junk = PS[:, 6:8, :].rearrange("p a n -> p (a n)")

        h_dram = nc.dram_tensor("h_scratch", (S, D), F32, kind="Internal").ap()
        negm_dram = nc.dram_tensor("negm_scratch", (HEADS, S), F32, kind="Internal").ap()
        dec_dram = nc.dram_tensor("decay_scratch", (HEADS, NT), F32, kind="Internal").ap()

        tok = lambda a: a.rearrange("(t p) n -> p t n", p=P)
        x_tok = tok(x[0])
        out_tok = tok(out[0])
        h_tok = tok(h_dram)

        landed = [sem("landed0"), sem("landed1")]
        split_hi = sem("split_hi")
        split = sem("split")
        consts = sem("consts")
        ready = sem("ready")
        act_link = sem("act_link")
        dve_link = sem("dve_link")
        stage0 = sem("stage0")

        block = ctx.enter_context(nc.Block())

        def phase(name, names):
            return {n: sem(f"{name}_{n}") for n in names}

        T_SEMS = ["gain", "sdA", "hA", "sdB", "xs", "tr", "hi", "xt"]
        start = phase("start", ["gain", "hin", "sdB", "xs", "tr", "hi", "xt"])
        mix0 = phase("mix0", ["full", "free", "rows", "rows_tr", "scal", "scratch", "saved", "decb", "bcast", "const",
                              "prep", "args", "probs", "tr", "tq", "qk", "kv", "st", "outp", "num", "state",
                              "gated", "ss", "rstd", "done"])
        mix1 = phase("mix1", ["fullA", "fullB", "freeA", "freeB", "const", "bound", "boundS", "oml",
                              "sg", "onem", "lnf", "lfhi", "lf", "sums", "decays", "kg", "qe", "lev", "kv",
                              "state", "at", "outp", "oev", "ss", "rstd", "done"])
        tm = [phase(f"tm{l}", ["gain", "xs", "tr", "hi", "xt"]) for l in range(2)]
        wo = [phase(f"wo{l}", ["full", "free"]) for l in range(2)]
        tw = [phase(f"tw{l}", T_SEMS + ["hin"]) for l in range(2)]
        mlp = [phase(f"mlp{l}", ["full", "free", "hi", "ht"]) for l in range(2)]
        tp = [phase(f"tp{l}", ["gain", "sdA", "hA", "tr", "hi", "xt"]) for l in range(2)]
        ple = [phase(f"ple{l}", ["full", "free", "sig", "pin", "ptr", "phi", "pt"]) for l in range(2)]
        te = [phase("te0", T_SEMS + ["hout"]), phase("te1", ["gain", "sdA", "hA", "hout"])]

        @block.sync
        def _(sp):
            def stage(n_parity, n_wait, parts):
                if n_wait is not None:
                    sp.wait_ge(split, n_wait)
                for k, (dst, src) in enumerate(parts):
                    add = LOADED - 16 * (len(parts) - 1) if k == 0 else 16
                    sp.dma_start(dst, src).then_inc(landed[n_parity], add)

            def cols(q, w, c0, n, at=0):
                return (Wraw[q][:].rearrange("p (c n) -> p c n", c=NC)[:, :, at:at + n],
                        w[:, c0].rearrange("(c p) n -> p c n", p=P))

            def rows(q, w, r0):
                return (Wraw[q][:].rearrange("p (c n) -> p c n", c=2),
                        w[r0, :].rearrange("(c p) n -> p c n", p=P))

            ds = bass.ds
            w = a_w_in[0]
            sp.wait_ge(stage0, 1)
            o_g = 2 * HEADS * DQK + 2 * D
            with nc.allow_non_contiguous_dma(reason="gate columns"):
                stage(0, None, [cols(0, w, ds(o_g, 8), 8), cols(0, w, ds(o_g + 8, 8), 8, 128)])
            sp.dma_start(IDN[:], c_ident).then_inc(consts, 16)

            def head0(h, n_wait_a, n_wait_b):
                stage(1, n_wait_a, [cols(1, w, ds(h * DQK, DQK), DQK),
                                    cols(1, w, ds(HEADS * DQK + h * DQK, DQK), DQK, DQK),
                                    cols(1, w, ds(2 * HEADS * DQK + h * DV, DV), DV, 2 * DQK)])
                stage(0, n_wait_b, [cols(0, w, ds(2 * HEADS * DQK + D + h * DV, DV), DV)])

            head0(0, None, 1)
            with sp.Fori(1, HEADS) as h:
                head0(h, 2 * h, 2 * h + 1)

            def tail(l, n_out, n_mlp, n_gate, w_out):
                for j in range(4):
                    q = (n_out + j) % 2
                    stage(q, n_out + j - 1, [rows(q, w_out[0], ds(256 * j, 256))])
                qu, qd = n_mlp % 2, (n_mlp + 1) % 2
                with sp.Fori(0, NG) as g:
                    stage(qu, 2 * g + (n_mlp - 1), [cols(qu, mlp_w_up[l], ds(g * FG, FG), FG)])
                    stage(qd, 2 * g + n_mlp, [rows(qd, mlp_w_down[l], ds(g * FG, FG))])
                for j in range(4):
                    q = (n_gate + j) % 2
                    stage(q, n_gate + j - 1, [rows(q, ple_w_gate[l], ds(256 * j, 256))])
                q = (n_gate + 4) % 2
                stage(q, n_gate + 3, [rows(q, ple_w_up[l], ds(0, 256))])

            tail(0, L0_OUT, L0_MLP, L0_GATE, a_w_out)
            w1 = b_w_in[0]
            with sp.Fori(0, HEADS) as h:
                stage(0, 2 * h + (L1_HEADS - 1), [cols(0, w1, ds(h * P, P), P), cols(0, w1, ds(D + h * P, P), P, P)])
                stage(1, 2 * h + L1_HEADS, [cols(1, w1, ds(2 * D + h * P, P), P), cols(1, w1, ds(3 * D + h * P, P), P, P)])
            tail(1, L1_OUT, L1_MLP, L1_GATE, b_w_out)

        @block.gpsimd
        def _(pool):
            zeros = zero1[:].to_broadcast([P, BLK])
            nc.gpsimd.memset(Wraw[0][:], 0.0).then_inc(stage0, 1)
            nc.gpsimd.memset(zero1[:], 0.0).then_inc(ready, 1)
            pool.wait_ge(ready, 1)
            nc.gpsimd.memset(eps1[:], EPS).then_inc(ready, 1)

            def split_block(q, n, used, nth):
                pool.wait_ge(landed[q], nth * LOADED + LOADED)
                if used:
                    pool.wait_ge(*used)
                nc.gpsimd.tensor_tensor(Wh[q][:], Wraw[q][:], zeros, ALU.subtract).then_inc(split_hi, 1)
                pool.wait_ge(split_hi, n + 1)
                nc.gpsimd.tensor_tensor(Wl[q][:], Wraw[q][:], Wh[q][:].bitcast(F32), ALU.subtract).then_inc(split, 1)

            def one(n, used=None):
                split_block(n % 2, n, used, n // 2)

            def pair(i, n0, used0, used1):
                split_block(n0 % 2, 2 * i + n0, used0, i + n0 // 2)
                split_block((n0 + 1) % 2, 2 * i + (n0 + 1), used1, i + (n0 + 1) // 2)

            one(0)
            one(1)
            one(2, (mix0["full"], 4))
            with pool.Fori(1, HEADS) as h:
                pair(h, L0_HEADS, (mix0["full"], 16 * h - 4), (mix0["full"], 16 * h + 4))

            def tail(l, n_out, n_mlp, n_gate, heads_done):
                one(n_out, heads_done[0])
                one(n_out + 1, heads_done[1])
                one(n_out + 2, (wo[l]["full"], 16))
                one(n_out + 3, (wo[l]["full"], 32))
                one(n_mlp, (wo[l]["full"], 48))
                one(n_mlp + 1, (wo[l]["full"], 64))
                with pool.Fori(1, NG) as g:
                    pair(g, n_mlp, (mlp[l]["full"], 20 * g - 16), (mlp[l]["full"], 20 * g))
                one(n_gate, (mlp[l]["full"], 20 * NG - 16))
                one(n_gate + 1, (mlp[l]["full"], 20 * NG))
                for j in range(2, 5):
                    one(n_gate + j, (ple[l]["full"], 16 * (j - 1)))

            tail(0, L0_OUT, L0_MLP, L0_GATE, ((mix0["full"], 16 * HEADS - 4), (mix0["full"], 16 * HEADS + 4)))
            one(L1_HEADS, (ple[0]["full"], 64))
            one(L1_HEADS + 1, (ple[0]["full"], 80))
            with pool.Fori(1, HEADS) as h:
                pair(h, L1_HEADS, (mix1["fullA"], 8 * h), (mix1["fullB"], 8 * h))
            tail(1, L1_OUT, L1_MLP, L1_GATE, ((mix1["fullA"], 8 * HEADS), (mix1["fullB"], 8 * HEADS)))

        @block.tensor
        def _(pe):
            def mm3(out_, sh, sl, mh, ml, start, stop):
                nc.tensor.matmul(out_, sh, mh, start=start, stop=False)
                nc.tensor.matmul(out_, sh, ml, start=False, stop=False)
                return nc.tensor.matmul(out_, sl, mh, start=False, stop=stop)

            def transpose_tile(ph, src, pre, t):
                pe.wait_ge(ph["xs"] if pre else ph["hA"], t + 1)
                if t:
                    pe.wait_ge(ph["xt"], 2 * t)
                for b in range(2):
                    for k in range(4):
                        c = 4 * b + k
                        last = nc.tensor.transpose(PS[:, 4 + b, k * P:(k + 1) * P], src[:, t, c * P:(c + 1) * P], IDN[:])
                    last.then_inc(ph["tr"], 1)

            def transition(ph, src, pre, first=0):
                for t in range(first, NT):
                    transpose_tile(ph, src, pre, t)

            def down_block(ph, q, n, k0, stat_h, stat_l, chunk0, tile_wait=None, bank_wait=None, behind=None):
                pe.wait_ge(split, n + 1)
                wh = Wh[q][:].rearrange("p (c n) -> p c n", c=2)
                wl = Wl[q][:].rearrange("p (c n) -> p c n", c=2)
                for t in range(NT):
                    if tile_wait:
                        tile_wait(t)
                    for nh in range(2):
                        m = 2 * t + nh
                        if bank_wait and m < 4:
                            bank_wait(m)
                        elif not (isinstance(k0, int) and k0 + m < 4):
                            pe.wait_ge(ph["free"], k0 + (m - 3))
                        for c in range(2):
                            cc = chunk0 + c
                            last = mm3(PS[:, m % 4, :], stat_h[:, cc, t * P:(t + 1) * P], stat_l[:, cc, t * P:(t + 1) * P],
                                       wh[:, c, nh * 512:(nh + 1) * 512], wl[:, c, nh * 512:(nh + 1) * 512],
                                       c == 0, c == 1)
                        last.then_inc(ph["full"], 1)
                    if behind and t >= 3:
                        behind(t - 3)

            pe.wait_ge(consts, 16)
            transition(start, Y, True)

            def gemm0(n, which, t, part=None):
                lo, hi = part or (0, NC)
                q, width = (1, 256) if which == 0 else (0, DV)
                wh = Wh[q][:].rearrange("p (c n) -> p c n", c=NC)
                wl = Wl[q][:].rearrange("p (c n) -> p c n", c=NC)
                if lo == 0:
                    if t == 0:
                        pe.wait_ge(split, 2 * n + (L0_HEADS + 1 + which))
                    pe.wait_ge(mix0["free"], 16 * n + (8 * which + t + 1))
                for c in range(lo, hi):
                    last = mm3(PS[:, t % 4, 0:width], XTh[:, c, t * P:(t + 1) * P], XTl[:, c, t * P:(t + 1) * P],
                               wh[:, c, 0:width], wl[:, c, 0:width], c == 0, c == NC - 1)
                if hi == NC:
                    last.then_inc(mix0["full"], 1)

            pe.wait_ge(split, 1)
            pe.wait_ge(start["xt"], 2 * NT)
            g_h = Wh[0][:].rearrange("p (c n) -> p c n", c=NC)
            g_l = Wl[0][:].rearrange("p (c n) -> p c n", c=NC)
            for kind in range(2):
                for half in range(2):
                    for c in range(NC):
                        hs = slice(half * 512, half * 512 + 512)
                        ws = slice(kind * P, kind * P + P)
                        last = mm3(PS[:, 2 * kind + half, :], g_h[:, c, ws], g_l[:, c, ws],
                                   XTh[:, c, hs], XTl[:, c, hs], c == 0, c == NC - 1)
                    last.then_inc(mix0["full"], 1)

            for which in range(2):
                for t in range(NT):
                    gemm0(0, which, t)

            pe.wait_ge(mix0["rows"], 1)
            for qn in range(4):
                for c in range(NT):
                    o = (qn * NT + c) * HEADS
                    last = nc.tensor.transpose(PS[:, 4, o:o + HEADS],
                                               Y[0:HEADS, 3 + qn, c * P:(c + 1) * P], IDN[0:HEADS, 0:HEADS])
            last.then_inc(mix0["rows_tr"], 1)

            M0 = layer0_views(H, G, TMP)

            def steps0(n, gemm):
                def fill(c, lo, hi):
                    if gemm:
                        gemm0(n, 0, c, (lo, hi))
                pe.wait_ge(mix0["prep"], n)
                for c in range(NT):
                    if c < NT - 1:
                        if c:
                            pe.wait_ge(mix0["state"], 7 * n + (c - 7))
                        nc.tensor.matmul(PS[0:DQK, 7, 0:DV + 1], M0.KW[:, c, :], M0.z[:, c, 2 * DQK:2 * DQK + DV + 1],
                                         start=True, stop=True).then_inc(mix0["kv"], 1)
                    nc.tensor.transpose(PS[0:DQK, 4, 0:P], M0.QS[:, c, :], IDN[:])
                    nc.tensor.transpose(PS[0:DQK, 4, P:2 * P], M0.z[:, c, DQK:2 * DQK], IDN[:])
                    nc.tensor.transpose(PS[0:DQK, 4, 2 * P:3 * P], M0.QW[:, c, :], IDN[:]).then_inc(mix0["tr"], 1)
                    fill(c, 0, 3)
                    pe.wait_ge(mix0["tq"], 8 * n + (c - 7))
                    nc.tensor.matmul(PS[:, 5, 0:P], M0.TQ[0:DQK, P:2 * P], M0.TQ[0:DQK, 0:P],
                                     start=True, stop=True).then_inc(mix0["qk"], 1)
                    fill(c, 3, 6)
                    if c:
                        pe.wait_ge(mix0["num"], 8 * n + (c - 8))
                    if c == NT - 1:
                        pe.wait_ge(mix0["state"], 7 * n)
                    pe.wait_ge(mix0["st"], 8 * n + (c - 7))
                    nc.tensor.matmul(PS[:, 6, 0:DV + 1], M0.ST[:], M0.z[:, c, 2 * DQK:2 * DQK + DV + 1], start=True, stop=False)
                    nc.tensor.matmul(PS[:, 6, 0:DV + 1], M0.TQ[0:DQK, 2 * P:3 * P], M0.C[0:DQK, 0:DV + 1],
                                     start=False, stop=True).then_inc(mix0["outp"], 1)
                    fill(c, 6, NC)

            with pe.Fori(1, HEADS) as n:
                steps0(n, True)
                for t in range(NT):
                    gemm0(n, 1, t)
            steps0(HEADS, False)

            def tail(l, n_out, n_mlp, n_gate):
                transition(tm[l], Y, True)
                for j in range(4):
                    def wait_xt(t, j=j):
                        if j == 0:
                            pe.wait_ge(tm[l]["xt"], 2 * t + 2)
                    down_block(wo[l], (n_out + j) % 2, n_out + j, 16 * j, XTh, XTl, 2 * j, wait_xt,
                               behind=(lambda t: transpose_tile(tw[l], Y, True, t)) if j == 3 else None)
                transition(tw[l], Y, True, NT - 3)

                ph = mlp[l]
                qu, qd = n_mlp % 2, (n_mlp + 1) % 2
                uh = Wh[qu][:].rearrange("p (c n) -> p c n", c=NC)
                ul = Wl[qu][:].rearrange("p (c n) -> p c n", c=NC)

                def mlp_step(g, first=False, behind=None):
                    pe.wait_ge(split, 2 * g + (n_mlp + 1))
                    for j, (half, f) in enumerate(((0, 0), (0, 1), (1, 0), (1, 1))):
                        if first:
                            pe.wait_ge(tw[l]["xt"], 8 * half + 8)
                        else:
                            pe.wait_ge(ph["free"], 16 * g + (j - 3))
                        for c in range(NC):
                            last = mm3(PS[:, j, :], uh[:, c, f * P:(f + 1) * P], ul[:, c, f * P:(f + 1) * P],
                                       XTh[:, c, half * 512:half * 512 + 512], XTl[:, c, half * 512:half * 512 + 512],
                                       c == 0, c == NC - 1)
                        last.then_inc(ph["full"], 1)

                    def wait_ht(t):
                        if t % 4 == 0:
                            pe.wait_ge(ph["ht"], 4 * g + (2 if t == 0 else 4))

                    def wait_up(m):
                        pe.wait_ge(ph["ht"], 4 * g + (m + 1))
                    down_block(ph, qd, 2 * g + (n_mlp + 1), 16 * g, HTh, HTl, 0, wait_ht, wait_up, behind)

                mlp_step(0, True)
                with pe.Fori(1, NG - 1) as g:
                    mlp_step(g)
                mlp_step(NG - 1, behind=lambda t: transpose_tile(tp[l], H, False, t))
                transition(tp[l], H, False, NT - 3)

                ph = ple[l]
                for j in range(5):
                    if j in (1, 2):
                        hv = j - 1
                        pe.wait_ge(ph["pin"], 16 * hv + 16)
                        if hv == 0:
                            pe.wait_ge(tp[l]["xt"], 2 * NT)
                        else:
                            pe.wait_ge(ph["pt"], 2)
                        for c in range(2):
                            for k in range(4):
                                last = nc.tensor.transpose(PS[:, 4 + c, k * P:(k + 1) * P],
                                                           TMP[:, k * PLE + c * P:k * PLE + (c + 1) * P], IDN[:])
                            last.then_inc(ph["ptr"], 1)

                    def wait_in(t, j=j):
                        if j == 0:
                            pe.wait_ge(tp[l]["xt"], 2 * t + 2)
                        if j == 4 and t % 4 == 0:
                            pe.wait_ge(ph["pt"], 2 + t // 2)
                    stat = (HTh, HTl, 0) if j == 4 else (XTh, XTl, 2 * j)
                    down_block(ph, (n_gate + j) % 2, n_gate + j, 16 * j, *stat, wait_in,
                               behind=(lambda t: transpose_tile(te[l], Y, True, t)) if j == 4 and l == 0 else None)
                if l == 0:
                    transition(te[l], Y, True, NT - 3)

            tail(0, L0_OUT, L0_MLP, L0_GATE)

            M1 = layer1_views(H, G, TMP, HTh, HTl)
            pe.wait_ge(te[0]["xt"], 2 * NT)
            pe.wait_ge(mix1["const"], 1)

            def gemm1(n, which, t, part=None):
                lo, hi = part or (0, NC)
                wh = Wh[which][:].rearrange("p (c n) -> p c n", c=NC)
                wl = Wl[which][:].rearrange("p (c n) -> p c n", c=NC)
                bank = t % (4 if which else 2)
                if lo == 0:
                    if t == 0:
                        pe.wait_ge(split, 2 * n + (L1_HEADS + 1 + which))
                    if which == 0 and t >= 2:
                        pe.wait_ge(mix1["freeA"], 8 * n + (t - 1))
                    if which == 1 and t < 2:
                        pe.wait_ge(mix1["freeA"], 8 * n + (7 + t))
                    if which == 1 and t >= 4:
                        pe.wait_ge(mix1["freeB"], 8 * n + (t - 3))
                for c in range(lo, hi):
                    last = mm3(PS[:, bank, 0:256], XTh[:, c, t * P:(t + 1) * P], XTl[:, c, t * P:(t + 1) * P],
                               wh[:, c, :], wl[:, c, :], c == 0, c == NC - 1)
                if hi == NC:
                    last.then_inc(mix1["fullB" if which else "fullA"], 1)

            def decay_sums(c):
                for b in range(2):
                    nc.tensor.matmul(PS[:, 2 + b, :], M1.LFh[:, c, :], M1.sums[:, b * 512:b * 512 + 512], start=True, stop=False)
                    nc.tensor.matmul(PS[:, 2 + b, :], M1.LFl[:, c, :], M1.sums[:, b * 512:b * 512 + 512], start=False, stop=True)
                nc.tensor.matmul(PS[:, 6, 2 * P:3 * P], M1.sums[:, 8 * P:9 * P], M1.LFh[:, c, :], start=True, stop=False)
                nc.tensor.matmul(PS[:, 6, 2 * P:3 * P], M1.sums[:, 8 * P:9 * P], M1.LFl[:, c, :], start=False, stop=True)
                nc.tensor.transpose(PS[:, 6, 0:P], M1.Zq[:, c, :], IDN[:])
                nc.tensor.transpose(PS[:, 6, P:2 * P], M1.Zf[:, c, :], IDN[:]).then_inc(mix1["sums"], 1)

            def levels(l0, l1):
                for l in range(l0, l1):
                    kk = M1.KE[:, l, :] if l < LV else M1.TQK[:, P:2 * P]
                    qq = M1.QE[:, l, :] if l < LV else M1.TQK[:, 0:P]
                    last = nc.tensor.matmul(PS[:, 4 + l // 4, (l % 4) * P:(l % 4 + 1) * P], kk, qq, start=True, stop=True)
                last.then_inc(mix1["lev"], 1)

            def steps1(n, gemm):
                def fill(c, lo, hi):
                    if gemm:
                        gemm1(n, 0, c, (lo, hi))
                pe.wait_ge(mix1["lf"], n)
                pe.wait_ge(mix1["freeB"], 8 * n)
                decay_sums(0)
                for c in range(NT):
                    fill(c, 0, 3)
                    pe.wait_ge(mix1["qe"], 16 * n + (2 * c - 15))
                    levels(0, 4)
                    if c < NT - 1:
                        decay_sums(c + 1)
                    fill(c, 3, 6)
                    pe.wait_ge(mix1["qe"], 16 * n + (2 * c - 14))
                    levels(4, 8)
                    if c < NT - 1:
                        nc.tensor.matmul(PS[:, 7, 0:P], M1.KG[:], M1.Zv[:, c, :], start=True, stop=True).then_inc(mix1["kv"], 1)
                    fill(c, 6, NC)
                    pe.wait_ge(mix1["at"], 8 * n + (c - 7))
                    nc.tensor.matmul(PS[:, 7, P:2 * P], M1.AT[:], M1.Zv[:, c, :], start=True, stop=False)
                    nc.tensor.matmul(PS[:, 7, P:2 * P], M1.QG[:], M1.ST[:], start=False, stop=True).then_inc(mix1["outp"], 1)

            for which in range(2):
                for t in range(NT):
                    gemm1(0, which, t)
            with pe.Fori(1, HEADS) as n:
                steps1(n, True)
                for t in range(NT):
                    gemm1(n, 1, t)
            steps1(HEADS, False)

            tail(1, L1_OUT, L1_MLP, L1_GATE)

        @block.scalar
        def _(act):
            link = Link(act, act_link)

            def transition(ph, post, pre, norm_pre=True, h_out=None):
                for k in range(NT + 3):
                    if post and k < NT:
                        act.wait_ge(post[0], post[1] + (2 * k + 2))
                        link(nc.scalar.activation(junk, Y[:, k, :], ACT.Square, accum_out=ssA[:, k:k + 1]))
                        nc.scalar.activation(sdA[:, k:k + 1], ssA[:, k:k + 1], ACT.Sqrt, bias=eps1[:], scale=1.0 / D).then_inc(ph["sdA"], 1)
                    t = k - 1
                    if 0 <= t < NT and post:
                        act.wait_ge(ph["hA"], t + 1)
                    if 0 <= t < NT and pre and norm_pre:
                        if not post:
                            act.wait_ge(ph["hin"], 16)
                        link(nc.scalar.activation(junk, H[:, t, :], ACT.Square, accum_out=ssB[:, t:t + 1]))
                        nc.scalar.activation(sdB[:, t:t + 1], ssB[:, t:t + 1], ACT.Sqrt, bias=eps1[:], scale=1.0 / D).then_inc(ph["sdB"], 1)
                    if 0 <= t < NT and h_out is not None:
                        act.dma_start(h_out[:, t, :], H[:, t, :]).then_inc(ph["hout"], 16)
                    t = k - 3
                    if t >= 0 and not (h_out is out_tok):
                        for b in range(2):
                            act.wait_ge(ph["tr"], 2 * t + b + 1)
                            nc.scalar.activation(XTh[:, 4 * b:4 * b + 4, t * P:(t + 1) * P],
                                                 PS[:, 4 + b, :].rearrange("p (k n) -> p k n", k=4), ACT.Copy).then_inc(ph["hi"], 1)

            def gain(ph, slot, row):
                act.dma_start(G[:, slot, :], row.partition_broadcast(P)).then_inc(ph["gain"], 16)

            act.wait_ge(ready, 2)
            gain(start, 1, norm_gains[0, 0])
            act.dma_start(H[:], x_tok).then_inc(start["hin"], 16)
            transition(start, False, True)

            M0 = layer0_views(H, G, TMP)
            R = lambda i: Y[0:HEADS, i, :]
            act.wait_ge(start["xt"], 2 * NT)
            act.dma_start(M0.causal, c_causal).then_inc(mix0["const"], 16)
            act.dma_start(rows8[:, 0:1], a_ig_bias.rearrange("a h -> h a")).then_inc(mix0["const"], 16)
            act.dma_start(rows8[:, 1:2], a_fg_bias.rearrange("a h -> h a")).then_inc(mix0["const"], 16)
            act.wait_ge(mix0["const"], 48)
            for half in range(2):
                hs = slice(half * 512, half * 512 + 512)
                act.wait_ge(mix0["full"], half + 1)
                nc.scalar.activation(R(0)[:, hs], PS[0:HEADS, half, :], ACT.Identity, bias=rows8[:, 0:1]).then_inc(mix0["free"], 1)
            for half in range(2):
                hs = slice(half * 512, half * 512 + 512)
                act.wait_ge(mix0["full"], 2 + half + 1)
                nc.scalar.activation(R(1)[:, hs], PS[0:HEADS, 2 + half, :], ACT.Identity, bias=rows8[:, 1:2]).then_inc(mix0["free"], 1)
            act.wait_ge(mix0["free"], 4)
            link(nc.scalar.activation(R(2), R(1), ACT.Abs))
            link(nc.scalar.activation(R(2), R(2), ACT.Exp, scale=-1.0))
            nc.scalar.activation(R(2), R(2), ACT.Ln, bias=1.0).then_inc(mix0["scal"], 1)

            def evac_qkv(n, t):
                act.wait_ge(mix0["full"], 16 * n + (4 + t + 1))
                nc.scalar.activation(M0.z[:, t, 0:256], PS[:, t % 4, 0:256], ACT.Copy).then_inc(mix0["free"], 1)

            def evac_o(n, t):
                act.wait_ge(mix0["full"], 16 * n + (12 + t + 1))
                nc.scalar.activation(M0.O[:, t, :], PS[:, t % 4, 0:DV], ACT.Sigmoid).then_inc(mix0["free"], 1)

            for t in range(NT):
                evac_qkv(0, t)
            for t in range(NT):
                evac_o(0, t)
            act.wait_ge(mix0["scal"], 2)
            nc.scalar.activation(Y[0:HEADS, 4:7, :], Y[0:HEADS, 4:7, :], ACT.Exp).then_inc(mix0["rows"], 1)
            nc.scalar.activation(rows8[:, 16:24], rows8[:, 16:24], ACT.Exp).then_inc(mix0["scratch"], 1)
            act.wait_ge(mix0["scratch"], 1)
            act.dma_start(dec_dram, rows8[:, 16:24]).then_inc(mix0["saved"], 16)
            act.dma_start(negm_dram, R(7)).then_inc(mix0["saved"], 16)
            act.wait_ge(mix0["saved"], 32)
            act.dma_start(M0.DEC[:], dec_dram.rearrange("h c -> (h c)").partition_broadcast(P)).then_inc(mix0["decb"], 16)

            def load_max(n):
                act.dma_start(M0.NM, negm_dram[bass.ds(n, 1), :].rearrange("a n -> (a n)").partition_broadcast(P)).then_inc(mix0["bcast"], 16)

            def steps0(n, gemm):
                for c in range(NT):
                    act.wait_ge(mix0["tr"], 8 * n + (c - 7))
                    nc.scalar.activation(M0.TQ[0:DQK, :], PS[0:DQK, 4, 0:3 * P], ACT.Copy).then_inc(mix0["tq"], 1)
                    act.wait_ge(mix0["outp"], 8 * n + (c - 7))
                    nc.scalar.activation(M0.NUM[:, c, 0:DV + 1], PS[:, 6, 0:DV + 1], ACT.Copy)
                    nc.scalar.activation(TMP[:, c * P:c * P + P], PS[:, 6, 0:DV], ACT.Square,
                                         accum_out=M0.ss[:, c:c + 1]).then_inc(mix0["num"], 1)
                    if gemm:
                        evac_qkv(n, c)

            def boundary0(n, last, nxt):
                if last and nxt:
                    act.wait_ge(mix0["gated"], n)
                    for t in range(NT // 2):
                        evac_o(n, t)
                if last:
                    act.wait_ge(mix0["ss"], n)
                    nc.scalar.activation(M0.rs, M0.rs, ACT.Ln, bias=eps1[:], scale=1.0 / DV).then_inc(mix0["rstd"], 1)
                    act.wait_ge(mix0["rstd"], 2 * n - 1)
                    nc.scalar.activation(M0.rs, M0.rs, ACT.Exp, scale=-0.5).then_inc(mix0["rstd"], 1)
                if nxt:
                    act.wait_ge(mix0["args"], n + 1)
                    nc.scalar.activation(M0.PR[:], M0.PR[:], ACT.Exp).then_inc(mix0["probs"], 1)
                if last and nxt:
                    for t in range(NT // 2, NT):
                        evac_o(n, t)

            load_max(0)
            boundary0(0, False, True)
            with act.Fori(1, HEADS) as n:
                act.wait_ge(mix0["args"], n)
                load_max(n)
                steps0(n, True)
                boundary0(n, True, True)
            steps0(HEADS, False)
            boundary0(HEADS, True, False)

            def tail(l, head_gain, h_src, mix_done):
                mix_done()
                gain(tm[l], 1, head_gain[0].rearrange("h v -> (h v)"))
                act.dma_start(H[:], h_src).then_inc(tw[l]["hin"], 16)
                transition(tm[l], False, True, norm_pre=False)
                act.wait_ge(tm[l]["xt"], 2 * NT)
                gain(tw[l], 0, norm_gains[l, 1])
                gain(tw[l], 1, norm_gains[l, 2])
                transition(tw[l], (wo[l]["free"], 48), True)
                act.wait_ge(tw[l]["xt"], 2 * NT)
                gain(tp[l], 0, norm_gains[l, 3])
                ph = mlp[l]

                def mlp_step(g):
                    for j, (half, f) in enumerate(((0, 0), (0, 1), (1, 0), (1, 1))):
                        sq = TMP[:, (j % 2) * 512:(j % 2) * 512 + 512]
                        act.wait_ge(ph["full"], 20 * g + (j + 1))
                        if j >= 2 or not isinstance(g, int):
                            act.wait_ge(ph["ht"], 4 * g + (j - 1))
                        link(nc.scalar.activation(sq, PS[:, j, :], ACT.Relu))
                        link(nc.scalar.activation(sq, sq, ACT.Square))
                        nc.scalar.activation(HTh[:, f, half * 512:half * 512 + 512], sq, ACT.Copy).then_inc(ph["hi"], 1)
                mlp_step(0)
                base = link.base + link.n
                with act.Fori(1, NG) as g:
                    link.base, link.n = 8 * g + (base - 8), 0
                    mlp_step(g)
                link.base, link.n = base + 8 * (NG - 1), 0
                transition(tp[l], (mlp[l]["free"], 16 * (NG - 1)), True, norm_pre=False)
                act.wait_ge(tp[l]["xt"], 2 * NT)
                gain(te[l], 0, norm_gains[l, 4])
                if l == 0:
                    gain(te[l], 1, norm_gains[1, 0])
                ph = ple[l]
                for hv in range(2):
                    if hv == 0:
                        act.wait_ge(mlp[l]["ht"], 4 * NG)
                    else:
                        act.wait_ge(ph["ptr"], 2)
                    act.dma_start(TMP[:].rearrange("p (k n) -> p k n", k=4),
                                  tok(p[l, 0])[:, 4 * hv:4 * hv + 4, :]).then_inc(ph["pin"], 16)
                    for c in range(2):
                        act.wait_ge(ph["ptr"], 2 * hv + c + 1)
                        nc.scalar.activation(HTh[:, c, hv * 512:hv * 512 + 512], PS[:, 4 + c, :], ACT.Copy).then_inc(ph["phi"], 1)
                for t in range(NT):
                    act.wait_ge(ph["free"], 48 + 2 * t + 2)
                    nc.scalar.activation(Y[:, t, :], Y[:, t, :], ACT.Sigmoid).then_inc(ph["sig"], 1)
                transition(te[l], (ple[l]["free"], 64), l == 0, h_out=h_tok if l == 0 else out_tok)

            def mix0_done():
                act.wait_ge(mix0["done"], HEADS + 1)
            tail(0, a_head_gain, x_tok, mix0_done)

            M1 = layer1_views(H, G, TMP, HTh, HTl)
            act.wait_ge(te[0]["hout"], 16 * NT)
            act.wait_ge(te[0]["xt"], 2 * NT)
            act.dma_start(Y[:, 0:2, :].rearrange("p a n -> p (a n)")[:, 0:(LV + 2) * P],
                          c_sums.rearrange("p l n -> p (l n)")).then_inc(mix1["bound"], 16)
            act.dma_start(M1.MASK[:], c_level_mask.rearrange("p l n -> p (l n)")).then_inc(mix1["bound"], 16)
            act.dma_start(Y[:, 2:4, :].rearrange("p a n -> p (a n)"),
                          b_lower_bound.rearrange("a n -> (a n)").partition_broadcast(P)).then_inc(mix1["bound"], 16)
            act.wait_ge(mix1["boundS"], 1)
            nc.scalar.activation(M1.OML[:], Y[:, 2, :], ACT.Sigmoid).then_inc(mix1["oml"], 1)

            def evac_qf(n, t):
                act.wait_ge(mix1["fullA"], 8 * n + (t + 1))
                nc.scalar.activation(M1.Zqf[:, :, t, :], PS[:, t % 2, 0:256].rearrange("p (a n) -> p a n", a=2),
                                     ACT.Copy).then_inc(mix1["freeA"], 1)

            def decays(n, c):
                act.wait_ge(mix1["sums"], 8 * n + (c - 7))
                if c:
                    act.wait_ge(mix1["qe"], 16 * n + (2 * c - 16))
                nc.scalar.activation(M1.E[:], PS[:, 2:4, :].rearrange("p a n -> p (a n)"), ACT.Exp)
                if c:
                    act.wait_ge(mix1["kv"], 7 * n + (c - 7))
                nc.scalar.activation(M1.KG[:], PS[:, 6, 2 * P:3 * P], ACT.Exp)
                nc.scalar.activation(M1.TQK[:], PS[:, 6, 0:2 * P], ACT.Copy).then_inc(mix1["decays"], 1)

            def boundary1(n, last, nxt):
                if last:
                    act.wait_ge(mix1["at"], 8 * n)
                    sg = nc.scalar.activation(TMP[:], M1.Zg[:].rearrange("p t n -> p (t n)"), ACT.Sigmoid)
                if nxt:
                    act.wait_ge(mix1["freeA"], 8 * n + 8)
                    sg = nc.scalar.activation(M1.Zf[:], M1.Zf[:], ACT.Sigmoid, scale=-1.0)
                sg.then_inc(mix1["sg"], 1)
                if last:
                    act.wait_ge(mix1["ss"], n)
                    nc.scalar.activation(M1.rs, M1.rs, ACT.Ln, bias=eps1[:], scale=1.0 / DV).then_inc(mix1["rstd"], 1)
                if nxt:
                    act.wait_ge(mix1["onem"], n + 1)
                    nc.scalar.activation(TMP[:], TMP[:], ACT.Ln).then_inc(mix1["lnf"], 1)
                    act.wait_ge(mix1["lnf"], n + 1)
                    nc.scalar.activation(M1.LFh[:].rearrange("p t n -> p (t n)"), TMP[:], ACT.Copy).then_inc(mix1["lfhi"], 1)
                if last:
                    act.wait_ge(mix1["rstd"], 2 * n - 1)
                    nc.scalar.activation(M1.rs, M1.rs, ACT.Exp, scale=-0.5).then_inc(mix1["rstd"], 1)
                if nxt:
                    act.wait_ge(mix1["done"], n + 1)
                    for t in range(NT):
                        act.wait_ge(mix1["fullB"], 8 * n + (t + 1))
                        nc.scalar.activation(M1.Zvg[:, :, t, :], PS[:, t % 4, 0:256].rearrange("p (a n) -> p a n", a=2),
                                             ACT.Copy).then_inc(mix1["freeB"], 1)

            def steps1(n, gemm):
                decays(n, 0)
                for c in range(NT):
                    if c < NT - 1:
                        decays(n, c + 1)
                    if gemm:
                        act.wait_ge(mix1["kg"], 8 * n + (c - 7))
                        evac_qf(n, c)

            act.wait_ge(mix1["done"], 1)
            for t in range(NT):
                evac_qf(0, t)
            boundary1(0, False, True)
            with act.Fori(1, HEADS) as n:
                steps1(n, True)
                boundary1(n, True, True)
            steps1(HEADS, False)
            boundary1(HEADS, True, False)

            def mix1_done():
                act.wait_ge(mix1["done"], HEADS + 1)
            tail(1, b_head_gain, h_tok, mix1_done)
            act.wait_ge(te[1]["hout"], 16 * NT)

        @block.vector
        def _(dve):
            link = Link(dve, dve_link)
            V = nc.vector

            def stage_a(ph, t):
                dve.wait_ge(ph["sdA"], t + 1)
                link(V.reciprocal(rA[:, t:t + 1], sdA[:, t:t + 1]))
                link(V.scalar_tensor_tensor(out=Y[:, t, :], in0=Y[:, t, :], scalar=rA[:, t:t + 1], in1=G[:, 0, :],
                                            op0=ALU.mult, op1=ALU.mult))
                V.tensor_tensor(H[:, t, :], H[:, t, :], Y[:, t, :], ALU.add).then_inc(ph["hA"], 1)

            def stage_b(ph, t, norm, post):
                if norm:
                    dve.wait_ge(ph["sdB"], t + 1)
                    if post:
                        dve.wait_ge(ph["hA"], t + 1)
                    link(V.reciprocal(rB[:, t:t + 1], sdB[:, t:t + 1]))
                    V.scalar_tensor_tensor(out=Y[:, t, :], in0=H[:, t, :], scalar=rB[:, t:t + 1], in1=G[:, 1, :],
                                           op0=ALU.mult, op1=ALU.mult).then_inc(ph["xs"], 1)
                else:
                    V.tensor_tensor(Y[:, t, :], Y[:, t, :], G[:, 1, :], ALU.mult).then_inc(ph["xs"], 1)

            def stage_c(ph, t):
                for b in range(2):
                    dve.wait_ge(ph["hi"], 2 * t + b + 1)
                    V.tensor_tensor(XTl[:, 4 * b:4 * b + 4, t * P:(t + 1) * P],
                                    PS[:, 4 + b, :].rearrange("p (k n) -> p k n", k=4),
                                    XTh[:, 4 * b:4 * b + 4, t * P:(t + 1) * P].bitcast(F32), ALU.subtract).then_inc(ph["xt"], 1)

            def transition(ph, finish, post, pre, norm_pre, c_on, gains):
                for k in range(NT + 3):
                    if finish and k < NT:
                        finish(k)
                    if k == 1:
                        dve.wait_ge(ph["gain"], 16 * gains)
                    if post and 0 <= k - 1 < NT:
                        stage_a(ph, k - 1)
                    if pre and 0 <= k - 2 < NT:
                        stage_b(ph, k - 2, norm_pre, post)
                    if c_on and 0 <= k - 3 < NT:
                        stage_c(ph, k - 3)

            dve.wait_ge(ready, 2)
            transition(start, None, False, True, True, True, 1)

            M0 = layer0_views(H, G, TMP)
            R = lambda i: Y[0:HEADS, i, :]
            dve.wait_ge(mix0["scal"], 1)
            dve.wait_ge(mix0["free"], 4)
            link(V.memset(rows8[:, 8:9], 0.0))
            dve.wait_ge(start["xs"], NT)
            link(V.scalar_tensor_tensor(out=R(1), in0=R(1), scalar=0.0, in1=R(2), op0=ALU.min, op1=ALU.subtract))
            link(V.memset(R(2), 1.0))
            ones = TMP[0:HEADS, 0:P]
            link(V.memset(ones, 1.0))
            for c in range(NT):
                cs = slice(c * P, c * P + P)
                last = V.tensor_tensor_scan(out=R(2)[:, cs], data0=ones, data1=R(1)[:, cs], initial=0.0,
                                            op0=ALU.mult, op1=ALU.add)
            link(last)
            link(V.tensor_tensor(R(3), R(0), R(2), ALU.subtract))
            for c in range(NT):
                cs = slice(c * P, c * P + P)
                link(V.tensor_tensor_scan(out=R(1)[:, cs], data0=R(3)[:, cs], data1=R(3)[:, cs],
                                          initial=rows8[:, 8 + c:9 + c], op0=ALU.max, op1=ALU.max))
                if c < NT - 1:
                    link(V.tensor_tensor(rows8[:, 9 + c:10 + c], R(2)[:, c * P + P - 1:c * P + P],
                                         R(1)[:, c * P + P - 1:c * P + P], ALU.add))
            v3 = lambda i: R(i).rearrange("h (c t) -> h c t", c=NT)
            mst = rows8[:, 8:16].unsqueeze(2).to_broadcast([HEADS, NT, P])
            ml = v3(1)[:, :, P - 1:P].to_broadcast([HEADS, NT, P])
            V.tensor_tensor(v3(4), mst, v3(1), ALU.subtract)
            V.tensor_tensor(v3(5), v3(3), ml, ALU.subtract)
            V.scalar_tensor_tensor(out=R(6), in0=R(2), scalar=-1.0, in1=R(1), op0=ALU.mult, op1=ALU.subtract)
            V.tensor_scalar(R(7), R(1), -1.0, None, ALU.mult)
            V.tensor_tensor(rows8[:, 16:24], rows8[:, 8:16], v3(1)[:, :, P - 1], ALU.subtract).then_inc(mix0["scal"], 1)
            dve.wait_ge(mix0["rows_tr"], 1)
            link(V.tensor_copy(M0.TS[:], PS[:, 4, 0:4 * NT * HEADS]))
            V.memset(M0.z[:, :, 256:257], 1.0).then_inc(mix0["done"], 1)
            ts = M0.TS[:].rearrange("p (q c h) -> p q c h", q=4, c=NT)
            dve.wait_ge(mix0["decb"], 16)

            def steps0(n):
                for c in range(NT):
                    dve.wait_ge(mix0["qk"], 8 * n + (c - 7))
                    V.tensor_tensor(M0.ST[:], PS[:, 5, 0:P], M0.PR3[:, c, :], ALU.mult).then_inc(mix0["st"], 1)
                    if c < NT - 1:
                        dve.wait_ge(mix0["outp"], 8 * n + (c - 7))
                        dve.wait_ge(mix0["kv"], 7 * n + (c - 6))
                        V.scalar_tensor_tensor(out=M0.C[0:DQK, :], in0=M0.C[0:DQK, :], scalar=M0.dec[0:DQK, c:c + 1],
                                               in1=PS[0:DQK, 7, 0:DV + 1], op0=ALU.mult, op1=ALU.add).then_inc(mix0["state"], 1)

            def boundary0(n, last, nxt):
                u, wi, wk, em = (M0.th[:, i * NT:(i + 1) * NT, 0] for i in range(4))
                den = M0.NUM[:, :, DV]
                yh = Y[:, :, bass.ds(n * DV - DV, DV)] if last else None
                if last:
                    dve.wait_ge(mix0["num"], 8 * n)
                    V.tensor_tensor(yh, M0.NUM[:, :, 0:DV], M0.O[:], ALU.mult).then_inc(mix0["gated"], 1)
                    link(V.scalar_tensor_tensor(out=M0.den, in0=den, scalar=-1.0, in1=den, op0=ALU.mult, op1=ALU.max))
                    link(V.tensor_tensor(M0.den, M0.den, em, ALU.max))
                    link(V.reciprocal(M0.den, M0.den))
                    link(V.tensor_tensor(M0.rs, M0.ss, M0.den, ALU.mult))
                    V.tensor_tensor(M0.rs, M0.rs, M0.den, ALU.mult).then_inc(mix0["ss"], 1)
                if nxt:
                    V.tensor_copy(M0.dec[:], M0.DEC[:, bass.ds(n * NT, NT)])
                    link(V.tensor_copy(M0.th[:], ts[:, :, :, bass.ds(n, 1)]))
                    dve.wait_ge(mix0["bcast"], 16 * n + 16)
                    link(V.tensor_tensor(M0.PR3, M0.NM3, u.unsqueeze(2).to_broadcast([P, NT, P]), ALU.add))
                    V.tensor_tensor(M0.PR3, M0.PR3, M0.causal.unsqueeze(1).to_broadcast([P, NT, P]), ALU.min).then_inc(mix0["args"], 1)
                    dve.wait_ge(mix0["free"], 16 * n + 12)
                    V.memset(M0.C[:], 0.0)
                    link(V.tensor_scalar(M0.QS[:], M0.z[:, :, 0:DQK], DQK ** -0.5, None, ALU.mult))
                    V.tensor_tensor(M0.QW[:], M0.QS[:], wi.unsqueeze(2).to_broadcast([P, NT, DQK]), ALU.mult)
                    V.tensor_tensor(M0.KW[:], M0.z[:, :, DQK:2 * DQK], wk.unsqueeze(2).to_broadcast([P, NT, DQK]),
                                    ALU.mult).then_inc(mix0["prep"], 1)
                if last:
                    dve.wait_ge(mix0["rstd"], 2 * n)
                    link(V.tensor_tensor(M0.den, M0.den, M0.rs, ALU.mult))
                    V.tensor_tensor(yh, yh, M0.den.unsqueeze(2).to_broadcast([P, NT, DV]), ALU.mult).then_inc(mix0["done"], 1)
                if nxt:
                    dve.wait_ge(mix0["probs"], n + 1)

            boundary0(0, False, True)
            base0 = link.base + link.n
            with dve.Fori(1, HEADS) as n:
                link.base, link.n = n * LINKS0 + (base0 - LINKS0), 0
                steps0(n)
                boundary0(n, True, True)
                assert link.n == LINKS0, link.n
            link.base, link.n = base0 + (HEADS - 1) * LINKS0, 0
            steps0(HEADS)
            boundary0(HEADS, True, False)

            def tail(l):
                dve.wait_ge(mix0["done"] if l == 0 else mix1["done"], HEADS + 1)
                transition(tm[l], None, False, True, False, True, 1)

                def sums(ph, k0, j, t):
                    for nh in range(2):
                        m = 2 * t + nh
                        dve.wait_ge(ph["full"], k0 + (m + 1))
                        ys = Y[:, t, nh * 512:nh * 512 + 512]
                        if j == 0:
                            V.tensor_copy(ys, PS[:, m % 4, :]).then_inc(ph["free"], 1)
                        else:
                            V.tensor_tensor(ys, ys, PS[:, m % 4, :], ALU.add).then_inc(ph["free"], 1)

                def finish(ph, k0):
                    return lambda t: sums(ph, k0, 1, t)

                for j in range(3):
                    for t in range(NT):
                        sums(wo[l], 16 * j, j, t)
                dve.wait_ge(tw[l]["hin"], 16)
                transition(tw[l], finish(wo[l], 48), True, True, True, True, 2)

                ph = mlp[l]

                def lo_part(g, j, half, f):
                    dve.wait_ge(ph["hi"], 4 * g + (j + 1))
                    V.tensor_tensor(HTl[:, f, half * 512:half * 512 + 512], TMP[:, (j % 2) * 512:(j % 2) * 512 + 512],
                                    HTh[:, f, half * 512:half * 512 + 512].bitcast(F32), ALU.subtract).then_inc(ph["ht"], 1)

                def mlp_up(g):
                    for j, (half, f) in enumerate(((0, 0), (0, 1), (1, 0), (1, 1))):
                        lo_part(g, j, half, f)

                mlp_up(0)
                for t in range(NT):
                    sums(ph, 4, 0, t)
                with dve.Fori(1, NG - 1) as g:
                    mlp_up(g)
                    for t in range(NT):
                        sums(ph, 20 * g + 4, 1, t)
                mlp_up(NG - 1)
                transition(tp[l], finish(ph, 20 * (NG - 1) + 4), True, False, False, True, 1)

                ph = ple[l]
                for j in range(3):
                    for t in range(NT):
                        sums(ph, 16 * j, j, t)
                    if j in (0, 1):
                        for c in range(2):
                            dve.wait_ge(ph["phi"], 2 * j + c + 1)
                            V.tensor_tensor(HTl[:, c, j * 512:j * 512 + 512], PS[:, 4 + c, :],
                                            HTh[:, c, j * 512:j * 512 + 512].bitcast(F32), ALU.subtract).then_inc(ph["pt"], 1)
                for t in range(NT):
                    sums(ph, 48, 3, t)

                def gated(t):
                    dve.wait_ge(ph["sig"], t + 1)
                    for nh in range(2):
                        m = 2 * t + nh
                        dve.wait_ge(ph["full"], 64 + m + 1)
                        ys = Y[:, t, nh * 512:nh * 512 + 512]
                        V.tensor_tensor(ys, ys, PS[:, m % 4, :], ALU.mult).then_inc(ph["free"], 1)
                transition(te[l], gated, True, l == 0, True, l == 0, 2 if l == 0 else 1)

            tail(0)

            M1 = layer1_views(H, G, TMP, HTh, HTl)
            dve.wait_ge(mix1["bound"], 48)
            V.tensor_copy(M1.sums[:], Y[:, 0:2, :].rearrange("p a n -> p (a n)")[:, 0:(LV + 2) * P]).then_inc(mix1["const"], 1)
            V.tensor_tensor(Y[:, 2, :], Y[:, 2, :], Y[:, 3, :], ALU.subtract).then_inc(mix1["boundS"], 1)
            V.memset(M1.ST[:], 0.0).then_inc(mix1["done"], 1)
            dve.wait_ge(mix1["oml"], 1)
            b1 = link.base + link.n
            T3 = TMP[:].rearrange("p (t n) -> p t n", n=P)
            E3 = M1.E[:].rearrange("p (l n) -> p l n", n=P)

            def out_tile(n, c):
                dve.wait_ge(mix1["outp"], 8 * n + (c - 7))
                return V.tensor_scalar(Y[:, c, bass.ds(n * P - P, P)], PS[:, 7, P:2 * P], 1.0, None, ALU.mult)

            def steps1(n):
                def halves(l0, l1):
                    k = l1 - l0
                    V.tensor_tensor(M1.QE[:, l0:l1, :], M1.TQK[:, 0:P].unsqueeze(1).to_broadcast([P, k, P]),
                                    E3[:, l0:l1, :], ALU.mult)
                    V.tensor_tensor(M1.KE[:, l0:l1, :], M1.TQK[:, P:2 * P].unsqueeze(1).to_broadcast([P, k, P]),
                                    E3[:, l0:l1, :], ALU.mult).then_inc(mix1["qe"], 1)
                for c in range(NT):
                    dve.wait_ge(mix1["decays"], 8 * n + (c - 7))
                    V.tensor_tensor(M1.KG[:], M1.KG[:], M1.Zf[:, c, :], ALU.mult).then_inc(mix1["kg"], 1)
                    halves(0, 4)
                    if c:
                        out_tile(n, c - 1).then_inc(mix1["oev"], 1)
                        dve.wait_ge(mix1["kv"], 7 * n + (c - 7))
                        V.scalar_tensor_tensor(out=M1.ST[:], in0=M1.ST[:], scalar=M1.dec[(c - 1) % 2], in1=PS[:, 7, 0:P],
                                               op0=ALU.mult, op1=ALU.add).then_inc(mix1["state"], 1)
                    V.tensor_tensor(M1.QG[:], M1.TQK[:, 0:P], E3[:, LV, :], ALU.mult)
                    V.tensor_copy(M1.dec[c % 2], E3[:, LV, P - 1:P])
                    halves(4, LV)
                    for b in range(2):
                        dve.wait_ge(mix1["lev"], 16 * n + (2 * c + b - 15))
                        masked = V.tensor_tensor(TMP[:, b * 512:b * 512 + 512], PS[:, 4 + b, :], M1.MASK[:, b * 512:b * 512 + 512], ALU.mult)
                    link(masked)
                    V.tensor_reduce(M1.AT[:], TMP[:].rearrange("p (l n) -> p n l", n=P), AX_X, ALU.add).then_inc(mix1["at"], 1)

            def boundary1(n, last, nxt):
                yh = Y[:, :, bass.ds(n * P - P, P)] if last else None
                if last:
                    link(out_tile(n, NT - 1))
                    link(V.tensor_tensor(E3, yh, yh, ALU.mult))
                    V.tensor_reduce(M1.rs, E3, AX_X, ALU.add).then_inc(mix1["ss"], 1)
                dve.wait_ge(mix1["sg"], n + 1)
                if last:
                    V.tensor_tensor(M1.Zg[:], M1.Zg[:], T3, ALU.mult)
                if nxt:
                    link(V.tensor_tensor(M1.Zf[:], M1.Zf[:], M1.OML[:, bass.ds(n * P, P)].unsqueeze(1).to_broadcast([P, NT, P]), ALU.mult))
                    link(V.tensor_scalar(TMP[:], M1.Zf[:].rearrange("p t n -> p (t n)"), -1.0, 1.0, ALU.mult, ALU.add))
                    V.tensor_scalar(TMP[:], TMP[:], 1e-9, None, ALU.max).then_inc(mix1["onem"], 1)
                    V.memset(M1.ST[:], 0.0)
                if last:
                    dve.wait_ge(mix1["rstd"], 2 * n)
                    link(V.tensor_tensor(yh, yh, M1.rs.unsqueeze(2).to_broadcast([P, NT, P]), ALU.mult))
                    V.tensor_tensor(yh, yh, M1.Zg[:], ALU.mult).then_inc(mix1["done"], 1)
                if nxt:
                    dve.wait_ge(mix1["lfhi"], n + 1)
                    V.tensor_tensor(M1.LFl[:].rearrange("p t n -> p (t n)"), TMP[:],
                                    M1.LFh[:].rearrange("p t n -> p (t n)").bitcast(F32), ALU.subtract).then_inc(mix1["lf"], 1)

            boundary1(0, False, True)
            b1 = link.base + link.n
            with dve.Fori(1, HEADS) as n:
                link.base, link.n = n * LINKS1 + (b1 - LINKS1), 0
                steps1(n)
                boundary1(n, True, True)
                assert link.n == LINKS1, link.n
            link.base, link.n = b1 + (HEADS - 1) * LINKS1, 0
            steps1(HEADS)
            boundary1(HEADS, True, False)
            tail(1)


LINKS0 = 4 + 3 + 1
LINKS1 = NT + 5


class Views:
    pass


def layer0_views(H, G, TMP):
    v = Views()
    flat = H[:].rearrange("p t n -> p (t n)")
    at = [0]

    def take(src, n):
        a = src[:, at[0]:at[0] + n]
        at[0] += n
        return a
    v.z = take(flat, NT * 260).rearrange("p (t n) -> p t n", n=260)
    v.O = take(flat, NT * DV).rearrange("p (t n) -> p t n", n=DV)
    v.QS = take(flat, NT * DQK).rearrange("p (t n) -> p t n", n=DQK)
    v.QW = take(flat, NT * DQK).rearrange("p (t n) -> p t n", n=DQK)
    v.KW = take(flat, NT * DQK).rearrange("p (t n) -> p t n", n=DQK)
    v.PR = take(flat, S)
    v.PR3 = v.PR.rearrange("p (t n) -> p t n", n=P)
    v.NM = take(flat, S)
    v.NM3 = v.NM.rearrange("p (t n) -> p t n", n=P)
    v.NUM = take(flat, NT * 132).rearrange("p (t n) -> p t n", n=132)
    assert at[0] <= NT * D
    g = G[:].rearrange("p a n -> p (a n)")
    at[0] = 0
    v.TQ = take(g, 3 * P)
    v.ST = take(g, P)
    v.C = take(g, DV + 1)
    v.dec = take(g, NT)
    v.ss = take(g, NT)
    v.DEC = take(g, HEADS * NT)
    v.TS = take(g, 4 * NT * HEADS)
    v.th = take(g, 4 * NT).rearrange("p (q a) -> p q a", a=1)
    v.den = take(g, NT)
    v.rs = take(g, NT)
    v.causal = take(g, P)
    return v


def layer1_views(H, G, TMP, HTh, HTl):
    v = Views()
    flat = H[:].rearrange("p t n -> p (t n)")
    at = [0]

    def take(src, n):
        a = src[:, at[0]:at[0] + n]
        at[0] += n
        return a
    v.Zqf = take(flat, 2 * S).rearrange("p (a t n) -> p a t n", a=2, n=P)
    v.Zvg = take(flat, 2 * S).rearrange("p (a t n) -> p a t n", a=2, n=P)
    v.Zq, v.Zf, v.Zv, v.Zg = v.Zqf[:, 0], v.Zqf[:, 1], v.Zvg[:, 0], v.Zvg[:, 1]
    v.OML = take(flat, D)
    v.E = take(flat, (LV + 1) * P)
    v.QE = take(flat, LV * P).rearrange("p (l n) -> p l n", n=P)
    v.KE = take(flat, LV * P).rearrange("p (l n) -> p l n", n=P)
    v.ST = take(flat, P)
    g = G[:].rearrange("p a n -> p (a n)")
    at[0] = 0
    v.MASK = take(g, (LV + 1) * P)
    v.TQK = take(g, 2 * P)
    v.AT = take(g, P)
    v.QG = take(g, P)
    v.KG = take(g, P)
    v.dec = [take(g, 1), take(g, 1)]
    v.rs = take(g, NT)
    hh = HTh[:].rearrange("p a n -> p (a n)")
    hl = HTl[:].rearrange("p a n -> p (a n)")
    v.sums = hh[:, 0:(LV + 2) * P]
    v.LFh = hl[:, 0:S].rearrange("p (t n) -> p t n", n=P)
    v.LFl = hl[:, S:2 * S].rearrange("p (t n) -> p t n", n=P)
    return v


_INS = ["x", "p", "norm_gains", "mlp_w_up", "mlp_w_down", "ple_w_up", "ple_w_gate",
        "a_w_in", "a_ig_bias", "a_fg_bias", "a_head_gain", "a_w_out",
        "b_w_in", "b_lower_bound", "b_head_gain", "b_w_out"]


def kernel(**inputs):
    import concourse.bacc as _bacc
    from concourse import mybir as _mybir
    from concourse.bass_utils import run_bass_kernel_spmd as _run

    nc = _bacc.Bacc("TRN2", target_bir_lowering=False, num_devices=1)
    arrays, args = {}, []
    named = [(n, np.ascontiguousarray(inputs[n])) for n in _INS] + list(shape_constants().items())
    for name, a in named:
        arrays[f"in_{name}_dram"] = a
        args.append(nc.dram_tensor(f"in_{name}_dram", a.shape, _mybir.dt.from_np(a.dtype), kind="ExternalInput").ap())
    args.append(nc.dram_tensor("out_0_dram", (1, S, D), F32, kind="ExternalOutput").ap())
    trunk(nc, *args)
    r = _run(nc, [arrays], core_ids=[0])
    return r.results[0]["out_0_dram"]
```

```python
from contextlib import ExitStack

import numpy as np

import concourse.bass as bass
from concourse import mybir

P = 128
D = 1024
S = 1024
NT = S // P
NC = D // P
FF = 4 * D
FG = 256
NG = FF // FG
BLK = D * 256 // P
HEADS = 8
DQK = 64
DV = 128
PLE = 256
EPS = 1e-6
LV = 7
NEG = -3.0e38

ALU = mybir.AluOpType
ACT = mybir.ActivationFunctionType
F32 = mybir.dt.float32
F32R = mybir.dt.float32r
AX_X = mybir.AxisListType.X

L0_GATES = 0
GATES_COUNT = 4
L0_HEADS = GATES_COUNT
L0_OUT = L0_HEADS + 3 * HEADS // 2
L0_MLP = L0_OUT + 4
L0_GATE = L0_MLP + 2 * NG
L1_HEADS = L0_GATE + 5
L1_OUT = L1_HEADS + 2 * HEADS
L1_MLP = L1_OUT + 4
L1_GATE = L1_MLP + 2 * NG
BLOCKS = L1_GATE + 5
FG_AT = 32
LOADED = 48

PE_TR = 4
ACT_PRE, ACT_HI = 2, 4
DVE_B, DVE_C = 3, 4
HIDDEN_AT = (5, 6)
ROWS_AT, EXP_AT = 4, 2
LINKS0 = 4 + 3 + 1
LINKS1 = NT + 5


def shape_constants():
    i = np.arange(P)
    s, t = i[:, None], i[None, :]
    sums = np.zeros((P, LV + 2, P), np.float32)
    mask = np.zeros((P, LV + 1, P), np.float32)
    for l in range(LV):
        m = 64 >> l
        mid = (t // (2 * m)) * 2 * m + m
        sums[:, l] = np.where(t >= mid, (s >= mid) & (s <= t), (s > t) & (s < mid))
        mask[:, l] = (s // (2 * m) == t // (2 * m)) & (s % (2 * m) < m) & (t % (2 * m) >= m)
    sums[:, LV] = s <= t
    sums[:, LV + 1] = s > t
    mask[:, LV] = s == t
    causal = np.where(s <= t, 0.0, NEG).astype(np.float32)
    return {"c_sums": sums, "c_level_mask": mask, "c_causal": causal, "c_ident": np.eye(P, dtype=np.float32)}


class Link:

    def __init__(self, eng, sem):
        self.eng, self.sem, self.base, self.n = eng, sem, 0, 0

    def __call__(self, ins):
        ins.then_inc(self.sem, 1)
        self.n += 1
        self.eng.wait_ge(self.sem, self.base + self.n)


def trunk(nc, x, p, norm_gains, mlp_w_up, mlp_w_down, ple_w_up, ple_w_gate,
          a_w_in, a_ig_bias, a_fg_bias, a_head_gain, a_w_out,
          b_w_in, b_lower_bound, b_head_gain, b_w_out,
          c_sums, c_level_mask, c_causal, c_ident, out):
    ctx = ExitStack()
    with ctx:
        def sb(name, shape, dt=F32):
            return ctx.enter_context(nc.sbuf_tensor(name, shape, dt))

        def sem(name):
            return ctx.enter_context(nc.semaphore(name))

        XTh = sb("XTh", [P, NC, S], F32R)
        XTl = sb("XTl", [P, NC, S], F32R)
        H = sb("H", [P, NT, D])
        Y = sb("Y", [P, NT, D])
        Wh = [sb(f"Wh{i}", [P, BLK], F32R) for i in range(2)]
        Wl = [sb(f"Wl{i}", [P, BLK], F32R) for i in range(2)]
        Wraw = [sb(f"Wraw{i}", [P, BLK]) for i in range(2)]
        HTh = sb("HTh", [P, 2, S], F32R)
        HTl = sb("HTl", [P, 2, S], F32R)
        G = sb("G", [P, 2, D])
        TMP = sb("TMP", [P, D])
        IDN = sb("IDN", [P, P])
        zero1 = sb("zero1", [P, 1])
        eps1 = sb("eps1", [P, 1])
        ssA = sb("ssA", [P, NT])
        sdA = sb("sdA", [P, NT])
        rA = sb("rA", [P, NT])
        ssB = sb("ssB", [P, NT])
        sdB = sb("sdB", [P, NT])
        rB = sb("rB", [P, NT])
        rows8 = sb("rows8", [HEADS, 32])
        fg_bias = sb("fg_bias", [FG_AT + HEADS, 1])
        head_gain = sb("head_gain", [P, 2, HEADS])
        PS = ctx.enter_context(nc.psum_tensor("PS", [P, 8, 512], F32))
        WO = [a[:].rearrange("p a n -> p (a n)") for a in (HTh, HTl)]
        junk = PS[:, 6:8, :].rearrange("p a n -> p (a n)")

        h_dram = nc.dram_tensor("h_scratch", (S, D), F32, kind="Internal").ap()
        negm_dram = nc.dram_tensor("negm_scratch", (HEADS, S), F32, kind="Internal").ap()
        dec_dram = nc.dram_tensor("decay_scratch", (HEADS, NT), F32, kind="Internal").ap()

        tok = lambda a: a.rearrange("(t p) n -> p t n", p=P)
        x_tok = tok(x[0])
        out_tok = tok(out[0])
        h_tok = tok(h_dram)

        landed = [sem("landed0"), sem("landed1")]
        split_hi = sem("split_hi")
        split = sem("split")
        consts = sem("consts")
        ready = sem("ready")
        act_link = sem("act_link")
        dve_link = sem("dve_link")
        head_gains = sem("head_gains")
        stage0 = sem("stage0")

        block = ctx.enter_context(nc.Block())

        def phase(name, names):
            return {n: sem(f"{name}_{n}") for n in names}

        T_SEMS = ["gain", "sdA", "ya", "hA", "sdB", "xs", "tr", "hi", "xt"]
        start = phase("start", ["gain", "hin0", "hin1", "hin2", "hin3", "sdB", "xs", "tr", "hi", "xt"])
        mix0 = phase("mix0", ["full", "free", "fullO", "freeO", "rows", "rows_tr", "scal", "scratch", "saved", "decb", "bcast", "const",
                              "gates", "gates_out", "prep", "args", "probs", "tr", "tq", "qk", "kv", "st", "outp", "num", "state",
                              "gated", "ss", "rstd", "done"])
        mix1 = phase("mix1", ["fullA", "fullB", "freeA", "freeB", "const", "bound", "boundS", "oml",
                              "sg", "onem", "lnf", "lfhi", "lf", "sums", "decays", "kg", "qe", "lev", "kv",
                              "state", "at", "outp", "ss", "rstd", "done"])
        tm = [phase(f"tm{l}", ["tr", "hi", "xt"]) for l in range(2)]
        wo = [phase(f"wo{l}", ["full", "free"]) for l in range(2)]
        tw = [phase(f"tw{l}", T_SEMS + ["hin"]) for l in range(2)]
        mlp = [phase(f"mlp{l}", ["full", "free", "hi", "ht"]) for l in range(2)]
        tp = [phase(f"tp{l}", ["gain", "sdA", "ya", "hA", "tr", "hi", "xt"]) for l in range(2)]
        ple = [phase(f"ple{l}", ["full", "free", "sig", "pin", "ptr", "phi", "pt"]) for l in range(2)]
        te = [phase("te0", T_SEMS + ["hout"]), phase("te1", ["gain", "sdA", "ya", "hA", "hout"])]

        @block.sync
        def _(sp):
            def stage(n_parity, n_wait, parts):
                if n_wait is not None:
                    sp.wait_ge(split, n_wait)
                for k, (dst, src) in enumerate(parts):
                    add = LOADED - 16 * (len(parts) - 1) if k == 0 else 16
                    sp.dma_start(dst, src).then_inc(landed[n_parity], add)

            def cols(q, w, c0, n, at=0):
                return (Wraw[q][:].rearrange("p (c n) -> p c n", c=NC)[:, :, at:at + n],
                        w[:, c0].rearrange("(c p) n -> p c n", p=P))

            def rows(q, w, r0):
                return (Wraw[q][:].rearrange("p (c n) -> p c n", c=2),
                        w[r0, :].rearrange("(c p) n -> p c n", p=P))

            ds = bass.ds
            w = a_w_in[0]
            sp.dma_start(IDN[:], c_ident).then_inc(consts, 16)
            sp.wait_ge(stage0, 1)
            o_g = 2 * HEADS * DQK + 2 * D
            with nc.allow_non_contiguous_dma(reason="gate columns"):
                sp.dma_start(*cols(0, w, ds(o_g, 8), 8)).then_inc(landed[0], GATES_COUNT * LOADED - 16)
                sp.dma_start(*cols(0, w, ds(o_g + 8, 8), 8, FG_AT)).then_inc(landed[0], 16)

            def qkv(q, h, n_wait):
                stage(q, n_wait, [cols(q, w, ds(h * DQK, DQK), DQK),
                                  cols(q, w, ds(HEADS * DQK + h * DQK, DQK), DQK, DQK),
                                  cols(q, w, ds(2 * HEADS * DQK + h * DV, DV), DV, 2 * DQK)])

            def o_pair(m, n_wait):
                stage(1, n_wait, [cols(1, w, ds(2 * HEADS * DQK + D + m * 2 * DV, 2 * DV), 2 * DV)])

            qkv(1, 0, None)
            o_pair(0, L0_HEADS + 1)
            with sp.Fori(0, HEADS // 2 - 1) as m:
                qkv(0, 2 * m + 1, 3 * m + L0_HEADS)
                qkv(1, 2 * m + 2, 3 * m + (L0_HEADS + 2))
                o_pair(m + 1, 3 * m + (L0_HEADS + 4))
            qkv(0, HEADS - 1, L0_OUT - 3)

            def tail(l, n_out, n_mlp, n_gate, w_out, staging_free):
                for j in range(4):
                    q = (n_out + j) % 2
                    stage(q, staging_free if j == 0 else n_out + j - 1, [rows(q, w_out[0], ds(256 * j, 256))])
                qu, qd = n_mlp % 2, (n_mlp + 1) % 2
                with sp.Fori(0, NG) as g:
                    stage(qu, 2 * g + (n_mlp - 1), [cols(qu, mlp_w_up[l], ds(g * FG, FG), FG)])
                    stage(qd, 2 * g + n_mlp, [rows(qd, mlp_w_down[l], ds(g * FG, FG))])
                for j in range(4):
                    q = (n_gate + j) % 2
                    stage(q, n_gate + j - 1, [rows(q, ple_w_gate[l], ds(256 * j, 256))])
                q = (n_gate + 4) % 2
                stage(q, n_gate + 3, [rows(q, ple_w_up[l], ds(0, 256))])

            tail(0, L0_OUT, L0_MLP, L0_GATE, a_w_out, L0_OUT)
            w1 = b_w_in[0]
            with sp.Fori(0, HEADS) as h:
                for i in range(2):
                    q = (L1_HEADS + i) % 2
                    stage(q, 2 * h + (L1_HEADS - 1 + i), [cols(q, w1, ds(2 * i * D + h * P, P), P),
                                                          cols(q, w1, ds((2 * i + 1) * D + h * P, P), P, P)])
            tail(1, L1_OUT, L1_MLP, L1_GATE, b_w_out, L1_OUT - 1)

        @block.gpsimd
        def _(pool):
            def cols_of(buf, width):
                return buf.rearrange("p (c n) -> p c n", c=NC)[:, :, 0:width]
            nc.gpsimd.memset(cols_of(Wraw[0][:], 2 * FG_AT), 0.0).then_inc(stage0, 1)
            nc.gpsimd.memset(zero1[:], 0.0).then_inc(ready, 1)
            pool.wait_ge(ready, 1)
            nc.gpsimd.memset(eps1[:], EPS).then_inc(ready, 1)

            def split_block(q, n, used, nth, width=256, dst=None, count=1):
                pool.wait_ge(landed[q], nth * LOADED + LOADED)
                if used:
                    pool.wait_ge(*used)
                wh, wl = dst or (Wh[q][:], Wl[q][:])
                raw, hi, lo = cols_of(Wraw[q][:], width), cols_of(wh, width), cols_of(wl, width)
                nc.gpsimd.tensor_tensor(hi, raw, zero1[:].unsqueeze(2).to_broadcast([P, NC, width]), ALU.subtract).then_inc(split_hi, count)
                pool.wait_ge(split_hi, n + count)
                nc.gpsimd.tensor_tensor(lo, raw, hi.bitcast(F32), ALU.subtract).then_inc(split, count)

            def one(n, used=None):
                split_block(n % 2, n, used, n // 2)

            def pair(i, n0, used0, used1):
                split_block(n0 % 2, 2 * i + n0, used0, i + n0 // 2)
                split_block((n0 + 1) % 2, 2 * i + (n0 + 1), used1, i + (n0 + 1) // 2)

            split_block(0, 0, None, GATES_COUNT - 1, 2 * FG_AT, count=GATES_COUNT)
            split_block(1, L0_HEADS, None, 0)
            split_block(1, L0_HEADS + 1, None, 1, dst=WO)
            split_block(0, L0_HEADS + 2, (mix0["gates"], 2), GATES_COUNT)
            split_block(1, L0_HEADS + 3, (mix0["full"], 8), 2)
            split_block(1, L0_HEADS + 4, (mix0["fullO"], 8), 3, dst=WO)
            with pool.Fori(1, HEADS // 2 - 1) as m:
                split_block(0, 3 * m + (L0_HEADS + 2), (mix0["full"], 16 * m), m + GATES_COUNT)
                split_block(1, 3 * m + (L0_HEADS + 3), (mix0["full"], 16 * m + 8), 2 * m + 2)
                split_block(1, 3 * m + (L0_HEADS + 4), (mix0["fullO"], 8 * m + 8), 2 * m + 3, dst=WO)
            split_block(0, L0_OUT - 1, (mix0["full"], 8 * (HEADS - 2)), GATES_COUNT + HEADS // 2 - 1)

            def residual(ph, t0, t1):
                for t in range(t0, t1):
                    pool.wait_ge(ph["ya"], t + 1)
                    nc.gpsimd.tensor_tensor(H[:, t, :], H[:, t, :], Y[:, t, :], ALU.add).then_inc(ph["hA"], 1)

            def tail(l, n_out, n_mlp, n_gate, heads_done, n_next):
                one(n_out, heads_done[0])
                one(n_out + 1, heads_done[1])
                one(n_out + 2, (wo[l]["full"], 16))
                one(n_out + 3, (wo[l]["full"], 32))
                one(n_mlp, (wo[l]["full"], 48))
                residual(tw[l], 0, NT)
                one(n_mlp + 1, (wo[l]["full"], 64))
                pair(1, n_mlp, (mlp[l]["full"], 12), (mlp[l]["full"], 20))
                with pool.Fori(2, NG) as g:
                    pair(g, n_mlp, (mlp[l]["full"], 20 * g - 16), (mlp[l]["full"], 20 * g))
                one(n_gate, (mlp[l]["full"], 20 * NG - 16))
                residual(tp[l], 0, NT)
                one(n_gate + 1, (mlp[l]["full"], 20 * NG))
                for j in range(2, 5):
                    one(n_gate + j, (ple[l]["full"], 16 * (j - 1)))
                if n_next is not None:
                    one(n_next, (ple[l]["full"], 64))
                residual(te[l], 0, NT)
                if n_next is not None:
                    one(n_next + 1, (ple[l]["full"], 80))

            tail(0, L0_OUT, L0_MLP, L0_GATE, ((mix0["full"], 8 * HEADS), (mix0["full"], 8 * HEADS)), L1_HEADS)
            with pool.Fori(1, HEADS) as h:
                pair(h, L1_HEADS, (mix1["fullA"], 8 * h), (mix1["fullB"], 8 * h))
            tail(1, L1_OUT, L1_MLP, L1_GATE, ((mix1["fullA"], 8 * HEADS), (mix1["fullB"], 8 * HEADS)), None)

        @block.tensor
        def _(pe):
            def mm3(out_, sh, sl, mh, ml, start, stop):
                nc.tensor.matmul(out_, sh, mh, start=start, stop=False)
                nc.tensor.matmul(out_, sh, ml, start=False, stop=False)
                return nc.tensor.matmul(out_, sl, mh, start=False, stop=stop)

            def transpose_tile(ph, src, pre, t):
                pe.wait_ge(ph["xs"] if pre else ph["hA"], t + 1)
                for b in range(2):
                    if t:
                        pe.wait_ge(ph["xt"], 2 * t - 1 + b)
                    for k in range(4):
                        c = 4 * b + k
                        last = nc.tensor.transpose(PS[:, 4 + b, k * P:(k + 1) * P], src[:, t, c * P:(c + 1) * P], IDN[:])
                    last.then_inc(ph["tr"], 1)

            def transition(ph, src, pre, first=0):
                for t in range(first, NT):
                    transpose_tile(ph, src, pre, t)

            def down_block(ph, q, n, k0, stat_h, stat_l, chunk0, tile_wait=None, bank_wait=None, after=None,
                           tiles=(0, NT)):
                if tiles[0] == 0:
                    pe.wait_ge(split, n + 1)
                wh = Wh[q][:].rearrange("p (c n) -> p c n", c=2)
                wl = Wl[q][:].rearrange("p (c n) -> p c n", c=2)
                for t in range(*tiles):
                    if tile_wait:
                        tile_wait(t)
                    for nh in range(2):
                        m = 2 * t + nh
                        if bank_wait and m < 4:
                            bank_wait(m)
                        elif not (isinstance(k0, int) and k0 + m < 4):
                            pe.wait_ge(ph["free"], k0 + (m - 3))
                        for c in range(2):
                            cc = chunk0 + c
                            last = mm3(PS[:, m % 4, :], stat_h[:, cc, t * P:(t + 1) * P], stat_l[:, cc, t * P:(t + 1) * P],
                                       wh[:, c, nh * 512:(nh + 1) * 512], wl[:, c, nh * 512:(nh + 1) * 512],
                                       c == 0, c == 1)
                        last.then_inc(ph["full"], 1)
                    if after:
                        after(t)

            def head_transposes(ph, done, n_done, c):
                if c in (0, HEADS - 1):
                    pe.wait_ge(done, n_done)
                for b in range(2):
                    if 0 < c < HEADS - 1:
                        pe.wait_ge(ph["xt"], 2 * c - 1 + b)
                    for k in range(4):
                        last = nc.tensor.transpose(PS[:, (4 if c == HEADS - 1 else 0) + b, k * P:(k + 1) * P],
                                                   Y[:, 4 * b + k, c * P:(c + 1) * P], IDN[:])
                    last.then_inc(ph["tr"], 1)

            def behind(ph, src, pre, lag=PE_TR):
                return lambda t: transpose_tile(ph, src, pre, t - lag) if t >= lag else None

            pe.wait_ge(consts, 16)

            def gemm0(slot, count, full, t, part=(0, NC)):
                lo, hi = part
                wh, wl = (a.rearrange("p (c n) -> p c n", c=NC) for a in slot)
                if lo == 0 and t == 0:
                    pe.wait_ge(split, count)
                for c in range(lo, hi):
                    last = mm3(PS[:, t % 4, 0:256], XTh[:, c, t * P:(t + 1) * P], XTl[:, c, t * P:(t + 1) * P],
                               wh[:, c, :], wl[:, c, :], c == 0, c == NC - 1)
                if hi == NC:
                    last.then_inc(full, 1)

            slot0, slot1 = (Wh[0][:], Wl[0][:]), (Wh[1][:], Wl[1][:])

            def qkv(n, odd, m, t, part=(0, NC)):
                if part[0] == 0:
                    if odd and t < 4:
                        pe.wait_ge(mix0["freeO"], 8 * m + (t + 5))
                    else:
                        pe.wait_ge(mix0["free"], 8 * n + (t - 3))
                gemm0(slot0 if odd else slot1, 3 * m + (L0_HEADS + (3 if odd else 4)), mix0["full"], t, part)

            def o_tile(m, t):
                if t < 4:
                    pe.wait_ge(mix0["free"], 16 * m + (t + 21))
                else:
                    pe.wait_ge(mix0["freeO"], 8 * m + (t + 5))
                gemm0(WO, 3 * m + (L0_HEADS + 5), mix0["fullO"], t)

            for t in range(NT):
                transpose_tile(start, Y, True, t)
                if t >= 4:
                    pe.wait_ge(start["xt"], 2 * t - 6)
                    gemm0(slot1, L0_HEADS + 1, mix0["full"], t - 4)

            pe.wait_ge(split, GATES_COUNT)
            pe.wait_ge(start["xt"], 2 * NT)
            g_h = Wh[0][:].rearrange("p (c n) -> p c n", c=NC)
            g_l = Wl[0][:].rearrange("p (c n) -> p c n", c=NC)
            for half in range(2):
                for c in range(NC):
                    hs = slice(half * 512, half * 512 + 512)
                    last = mm3(PS[0:2 * FG_AT, 4 + half, :], g_h[:, c, 0:2 * FG_AT], g_l[:, c, 0:2 * FG_AT],
                               XTh[:, c, hs], XTl[:, c, hs], c == 0, c == NC - 1)
                last.then_inc(mix0["gates"], 1)
            for t in range(4, NT):
                pe.wait_ge(mix0["free"], t - 3)
                gemm0(slot1, L0_HEADS + 1, mix0["full"], t)
            for t in range(NT):
                if t == ROWS_AT:
                    pe.wait_ge(mix0["rows"], 1)
                    for qn in range(4):
                        for c in range(NT):
                            o = (qn * NT + c) * HEADS
                            last = nc.tensor.transpose(PS[:, 4, o:o + HEADS],
                                                       Y[0:HEADS, 3 + qn, c * P:(c + 1) * P], IDN[0:HEADS, 0:HEADS])
                    last.then_inc(mix0["rows_tr"], 1)
                if t < 4:
                    pe.wait_ge(mix0["free"], t + 5)
                else:
                    pe.wait_ge(mix0["freeO"], t - 3)
                gemm0(WO, L0_HEADS + 2, mix0["fullO"], t)

            M0 = layer0_views(H, G, TMP)

            def tile_per_chunk(n, m):
                return lambda c, part: qkv(n, True, m, c, ((0, 3), (3, 6), (6, NC))[part])

            def half_tile_per_chunk(n, m):
                def fill(c, part):
                    if c == 0:
                        return
                    u0 = 5 * (c - 1) if c <= 5 else 4 * c
                    u1 = 5 * c if c <= 4 else 4 * c + 4
                    cuts = (u0, u0 + 2, min(u0 + 4, u1), u1)
                    for t in range(4, NT):
                        lo, hi = max(cuts[part], 8 * (t - 4)), min(cuts[part + 1], 8 * (t - 3))
                        if lo < hi:
                            qkv(n, False, m, t, (lo - 8 * (t - 4), hi - 8 * (t - 4)))
                return fill

            def last_transposes(c, part):
                if part == 1 and c < NT - 1:
                    head_transposes(tm[0], mix0["done"], HEADS - 1, c)

            def steps0(n, fill):
                pe.wait_ge(mix0["prep"], n)
                for c in range(NT):
                    if c < NT - 1:
                        if c:
                            pe.wait_ge(mix0["state"], 7 * n + (c - 7))
                        nc.tensor.matmul(PS[0:DQK, 7, 0:DV + 1], M0.KW[:, c, :], M0.z[:, c, 2 * DQK:2 * DQK + DV + 1],
                                         start=True, stop=True).then_inc(mix0["kv"], 1)
                    nc.tensor.transpose(PS[0:DQK, 4, 0:P], M0.QS[:, c, :], IDN[:])
                    nc.tensor.transpose(PS[0:DQK, 4, P:2 * P], M0.z[:, c, DQK:2 * DQK], IDN[:])
                    nc.tensor.transpose(PS[0:DQK, 4, 2 * P:3 * P], M0.QW[:, c, :], IDN[:]).then_inc(mix0["tr"], 1)
                    fill(c, 0)
                    pe.wait_ge(mix0["tq"], 8 * n + (c - 7))
                    nc.tensor.matmul(PS[:, 5, 0:P], M0.TQ[0:DQK, P:2 * P], M0.TQ[0:DQK, 0:P],
                                     start=True, stop=True).then_inc(mix0["qk"], 1)
                    fill(c, 1)
                    if c:
                        pe.wait_ge(mix0["num"], 8 * n + (c - 8))
                    if c == NT - 1:
                        pe.wait_ge(mix0["state"], 7 * n)
                    pe.wait_ge(mix0["st"], 8 * n + (c - 7))
                    nc.tensor.matmul(PS[:, 6, 0:DV + 1], M0.ST[:], M0.z[:, c, 2 * DQK:2 * DQK + DV + 1], start=True, stop=False)
                    nc.tensor.matmul(PS[:, 6, 0:DV + 1], M0.TQ[0:DQK, 2 * P:3 * P], M0.C[0:DQK, 0:DV + 1],
                                     start=False, stop=True).then_inc(mix0["outp"], 1)
                    fill(c, 2)

            with pe.Fori(0, HEADS // 2 - 1) as m:
                steps0(2 * m + 1, tile_per_chunk(2 * m + 1, m))
                for t in range(4):
                    qkv(2 * m + 2, False, m, t)
                steps0(2 * m + 2, half_tile_per_chunk(2 * m + 2, m))
                for t in range(NT):
                    o_tile(m, t)
            steps0(HEADS - 1, tile_per_chunk(HEADS - 1, HEADS // 2 - 1))
            steps0(HEADS, last_transposes)

            def tail(l, n_out, n_mlp, n_gate, mix_done):
                for j in range(4):
                    def wait_xt(t, j=j):
                        if t == 0 and j in (0, 3):
                            pe.wait_ge(tm[l]["xt"], 2 * (HEADS - 1) if j == 0 else 2 * HEADS)

                    def last_head(t):
                        if t == 1:
                            head_transposes(tm[l], *mix_done, HEADS - 1)
                    after = last_head if j == 0 else behind(tw[l], Y, True) if j == 3 else None
                    down_block(wo[l], (n_out + j) % 2, n_out + j, 16 * j, XTh, XTl, 2 * j, wait_xt, after=after)

                ph = mlp[l]
                qu, qd = n_mlp % 2, (n_mlp + 1) % 2
                uh = Wh[qu][:].rearrange("p (c n) -> p c n", c=NC)
                ul = Wl[qu][:].rearrange("p (c n) -> p c n", c=NC)

                def up(g, j, wait_free=True, halfway=None):
                    half, f = j // 2, j % 2
                    if wait_free:
                        pe.wait_ge(ph["free"], 16 * g + (j - 3))
                    for c in range(NC):
                        if halfway and c == NC // 2:
                            halfway()
                        last = mm3(PS[:, j, :], uh[:, c, f * P:(f + 1) * P], ul[:, c, f * P:(f + 1) * P],
                                   XTh[:, c, half * 512:half * 512 + 512], XTl[:, c, half * 512:half * 512 + 512],
                                   c == 0, c == NC - 1)
                    last.then_inc(ph["full"], 1)

                def first_step():
                    def tr(t):
                        transpose_tile(tw[l], Y, True, t)
                    pe.wait_ge(split, n_mlp + 1)
                    pe.wait_ge(tw[l]["xt"], NT)
                    tr(NT - 4)
                    up(0, 0, False, lambda: tr(NT - 3))
                    tr(NT - 2)
                    up(0, 1, False)
                    tr(NT - 1)

                    def wait_ht(t):
                        if t == 0:
                            pe.wait_ge(ph["ht"], 2)
                        if t == 4:
                            pe.wait_ge(ph["ht"], 4)
                    down_block(ph, qd, n_mlp + 1, 0, HTh, HTl, 0, wait_ht, lambda m: None,
                               None, (0, 4))
                    pe.wait_ge(tw[l]["xt"], 2 * NT)
                    pe.wait_ge(ph["free"], 7)
                    up(0, 2, False)
                    pe.wait_ge(ph["free"], 8)
                    up(0, 3, False)
                    down_block(ph, qd, n_mlp + 1, 0, HTh, HTl, 0, wait_ht, None, None, (4, NT))

                def mlp_step(g, after=None):
                    pe.wait_ge(split, 2 * g + (n_mlp + 1))
                    for j in range(4):
                        up(g, j)

                    def wait_ht(t):
                        if t % 4 == 0:
                            pe.wait_ge(ph["ht"], 4 * g + (2 if t == 0 else 4))

                    def wait_up(m):
                        pe.wait_ge(ph["ht"], 4 * g + (m + 1))
                    down_block(ph, qd, 2 * g + (n_mlp + 1), 16 * g, HTh, HTl, 0, wait_ht, wait_up, after)

                first_step()
                with pe.Fori(1, NG - 1) as g:
                    mlp_step(g)
                mlp_step(NG - 1, behind(tp[l], H, False, PE_TR - 1))

                ph = ple[l]
                for j in range(5):
                    if j in (1, 2):
                        hv = j - 1
                        pe.wait_ge(ph["pin"], 16 * hv + 16)
                        if hv == 0:
                            pe.wait_ge(tp[l]["xt"], 2 * NT)
                        else:
                            pe.wait_ge(ph["pt"], 2)
                        for c in range(2):
                            for k in range(4):
                                last = nc.tensor.transpose(PS[:, 4 + c, k * P:(k + 1) * P],
                                                           TMP[:, k * PLE + c * P:k * PLE + (c + 1) * P], IDN[:])
                            last.then_inc(ph["ptr"], 1)

                    def wait_in(t, j=j):
                        if j == 0:
                            pe.wait_ge(tp[l]["xt"], 2 * t + 2)
                        if j == 4 and t % 4 == 0:
                            pe.wait_ge(ph["pt"], 2 + t // 2)
                    stat = (HTh, HTl, 0) if j == 4 else (XTh, XTl, 2 * j)

                    def rest(t):
                        if t == 0:
                            transpose_tile(tp[l], H, False, 5)
                        if t == 1:
                            transition(tp[l], H, False, 6)
                    after = rest if j == 0 else behind(te[l], Y, True) if j == 4 and l == 0 else None
                    down_block(ph, (n_gate + j) % 2, n_gate + j, 16 * j, *stat, wait_in, after=after)

            tail(0, L0_OUT, L0_MLP, L0_GATE, (mix0["done"], HEADS))

            M1 = layer1_views(H, G, TMP, HTh, HTl)

            def gemm1(n, which, t, part=None):
                lo, hi = part or (0, NC)
                wh = Wh[(L1_HEADS + which) % 2][:].rearrange("p (c n) -> p c n", c=NC)
                wl = Wl[(L1_HEADS + which) % 2][:].rearrange("p (c n) -> p c n", c=NC)
                bank = t % (4 if which else 2)
                if lo == 0:
                    if t == 0:
                        pe.wait_ge(split, 2 * n + (L1_HEADS + 1 + which))
                    if which == 0 and t >= 2:
                        pe.wait_ge(mix1["freeA"], 8 * n + (t - 1))
                    if which == 1 and t < 2:
                        pe.wait_ge(mix1["freeA"], 8 * n + (7 + t))
                    if which == 1 and t >= 4:
                        pe.wait_ge(mix1["freeB"], 8 * n + (t - 3))
                for c in range(lo, hi):
                    last = mm3(PS[:, bank, 0:256], XTh[:, c, t * P:(t + 1) * P], XTl[:, c, t * P:(t + 1) * P],
                               wh[:, c, :], wl[:, c, :], c == 0, c == NC - 1)
                if hi == NC:
                    last.then_inc(mix1["fullB" if which else "fullA"], 1)

            def decay_sums(c):
                for b in range(2):
                    nc.tensor.matmul(PS[:, 2 + b, :], M1.LFh[:, c, :], M1.sums[:, b * 512:b * 512 + 512], start=True, stop=False)
                    nc.tensor.matmul(PS[:, 2 + b, :], M1.LFl[:, c, :], M1.sums[:, b * 512:b * 512 + 512], start=False, stop=True)
                nc.tensor.matmul(PS[:, 6, 2 * P:3 * P], M1.sums[:, 8 * P:9 * P], M1.LFh[:, c, :], start=True, stop=False)
                nc.tensor.matmul(PS[:, 6, 2 * P:3 * P], M1.sums[:, 8 * P:9 * P], M1.LFl[:, c, :], start=False, stop=True)
                nc.tensor.transpose(PS[:, 6, 0:P], M1.Zq[:, c, :], IDN[:])
                nc.tensor.transpose(PS[:, 6, P:2 * P], M1.Zf[:, c, :], IDN[:]).then_inc(mix1["sums"], 1)

            def levels(l0, l1):
                for l in range(l0, l1):
                    kk = M1.KE[:, l, :] if l < LV else M1.TQK[:, P:2 * P]
                    qq = M1.QE[:, l, :] if l < LV else M1.TQK[:, 0:P]
                    last = nc.tensor.matmul(PS[:, 4 + l // 4, (l % 4) * P:(l % 4 + 1) * P], kk, qq, start=True, stop=True)
                last.then_inc(mix1["lev"], 1)

            def steps1(n, gemm):
                def fill(c, lo, hi):
                    if gemm and hi > lo:
                        gemm1(n, 0, c, (lo, hi))
                    if not gemm and hi == NC and c < NT - 1:
                        head_transposes(tm[1], mix1["done"], HEADS, c)
                pe.wait_ge(mix1["lf"], n)
                pe.wait_ge(mix1["freeB"], 8 * n)
                decay_sums(0)
                for c in range(NT):
                    fill(c, 0, 3)
                    pe.wait_ge(mix1["qe"], 16 * n + (2 * c - 15))
                    levels(0, 4)
                    if c < NT - 1:
                        decay_sums(c + 1)
                    fill(c, 3, 3)
                    pe.wait_ge(mix1["qe"], 16 * n + (2 * c - 14))
                    levels(4, 8)
                    if c < NT - 1:
                        nc.tensor.matmul(PS[:, 7, 0:P], M1.KG[:], M1.Zv[:, c, :], start=True, stop=True).then_inc(mix1["kv"], 1)
                    fill(c, 3, NC)
                    pe.wait_ge(mix1["at"], 8 * n + (c - 7))
                    nc.tensor.matmul(PS[:, 7, P:2 * P], M1.AT[:], M1.Zv[:, c, :], start=True, stop=False)
                    nc.tensor.matmul(PS[:, 7, P:2 * P], M1.QG[:], M1.ST[:], start=False, stop=True).then_inc(mix1["outp"], 1)

            for t in range(NT):
                if t == 0:
                    transpose_tile(te[0], Y, True, 4)
                pe.wait_ge(te[0]["xt"], 2 * t + 2)
                gemm1(0, 0, t)
                if t == 0:
                    transpose_tile(te[0], Y, True, 5)
                if t == 1:
                    transition(te[0], Y, True, 6)
            for t in range(NT):
                gemm1(0, 1, t)
            pe.wait_ge(mix1["const"], 1)
            with pe.Fori(1, HEADS) as n:
                steps1(n, True)
                for t in range(NT):
                    gemm1(n, 1, t)
            steps1(HEADS, False)

            tail(1, L1_OUT, L1_MLP, L1_GATE, (mix1["done"], HEADS + 1))

        @block.scalar
        def _(act):
            link = Link(act, act_link)

            def transition(ph, post, pre, norm_pre=True, h_out=None, after=None):
                pre_lag, hi_lag = (ACT_PRE, ACT_HI if norm_pre else ACT_HI - 1) if post else (0, 1)
                for k in range(NT + hi_lag):
                    if post and k < NT:
                        act.wait_ge(post[0], post[1] + (2 * k + 2))
                        link(nc.scalar.activation(junk, Y[:, k, :], ACT.Square, accum_out=ssA[:, k:k + 1]))
                        nc.scalar.activation(sdA[:, k:k + 1], ssA[:, k:k + 1], ACT.Sqrt, bias=eps1[:], scale=1.0 / D).then_inc(ph["sdA"], 1)
                    t = k - pre_lag
                    if 0 <= t < NT and post and (pre and norm_pre or h_out is not None):
                        act.wait_ge(ph["hA"], t + 1)
                    if 0 <= t < NT and pre and norm_pre:
                        if not post and t % 2 == 0:
                            act.wait_ge(ph[f"hin{t // 2}"], 16)
                        link(nc.scalar.activation(junk, H[:, t, :], ACT.Square, accum_out=ssB[:, t:t + 1]))
                        nc.scalar.activation(sdB[:, t:t + 1], ssB[:, t:t + 1], ACT.Sqrt, bias=eps1[:], scale=1.0 / D).then_inc(ph["sdB"], 1)
                    if 0 <= t < NT and h_out is not None:
                        act.dma_start(h_out[:, t, :], H[:, t, :]).then_inc(ph["hout"], 16)
                    t = k - hi_lag
                    if t >= 0 and not (h_out is out_tok):
                        for b in range(2):
                            act.wait_ge(ph["tr"], 2 * t + b + 1)
                            nc.scalar.activation(XTh[:, 4 * b:4 * b + 4, t * P:(t + 1) * P],
                                                 PS[:, 4 + b, :].rearrange("p (k n) -> p k n", k=4), ACT.Copy).then_inc(ph["hi"], 1)
                    if after:
                        after(k)

            def head_hi(l, c):
                for b in range(2):
                    act.wait_ge(tm[l]["tr"], 2 * c + b + 1)
                    nc.scalar.activation(XTh[:, c, b * 512:b * 512 + 512], PS[:, (4 if c == HEADS - 1 else 0) + b, :],
                                         ACT.Copy, scale=head_gain[:, l, c:c + 1]).then_inc(tm[l]["hi"], 1)

            def gain(ph, slot, row):
                act.dma_start(G[:, slot, :], row.partition_broadcast(P)).then_inc(ph["gain"], 16)

            act.wait_ge(ready, 2)
            gain(start, 1, norm_gains[0, 0])
            for i in range(4):
                act.dma_start(H[:, 2 * i:2 * i + 2, :], x_tok[:, 2 * i:2 * i + 2, :]).then_inc(start[f"hin{i}"], 16)
            with nc.allow_non_contiguous_dma(reason="head gains, feature-major"):
                act.dma_start(head_gain[:, 0, :], a_head_gain[0].rearrange("h v -> v h")).then_inc(head_gains, 16)
                act.dma_start(head_gain[:, 1, :], b_head_gain[0].rearrange("h v -> v h")).then_inc(head_gains, 16)
            transition(start, False, True)

            M0 = layer0_views(H, G, TMP)
            R = lambda i: Y[0:HEADS, i, :]
            act.wait_ge(start["xt"], 2 * NT)
            act.dma_start(M0.causal, c_causal).then_inc(mix0["const"], 16)
            act.dma_start(rows8[:, 0:1], a_ig_bias.rearrange("a h -> h a")).then_inc(mix0["const"], 16)
            act.dma_start(fg_bias[FG_AT:FG_AT + HEADS, :], a_fg_bias.rearrange("a h -> h a")).then_inc(mix0["const"], 16)
            act.wait_ge(mix0["const"], 48)

            def evac_qkv(n, t):
                act.wait_ge(mix0["full"], 8 * n + (t + 1))
                nc.scalar.activation(M0.z[:, t, 0:256], PS[:, t % 4, 0:256], ACT.Copy).then_inc(mix0["free"], 1)

            for t in range(4):
                evac_qkv(0, t)
            for half in range(2):
                hs = slice(half * 512, half * 512 + 512)
                act.wait_ge(mix0["gates"], half + 1)
                nc.scalar.activation(R(0)[:, hs], PS[0:HEADS, 4 + half, :], ACT.Identity, bias=rows8[:, 0:1]).then_inc(mix0["gates_out"], 1)
                nc.scalar.activation(R(1)[:, hs], PS[FG_AT:FG_AT + HEADS, 4 + half, :], ACT.Identity,
                                     bias=fg_bias[FG_AT:FG_AT + HEADS, :]).then_inc(mix0["gates_out"], 1)
            act.wait_ge(mix0["gates_out"], 4)
            link(nc.scalar.activation(R(2), R(1), ACT.Abs))
            link(nc.scalar.activation(R(2), R(2), ACT.Exp, scale=-1.0))
            nc.scalar.activation(R(2), R(2), ACT.Ln, bias=1.0).then_inc(mix0["scal"], 1)

            def evac_o(m, t):
                act.wait_ge(mix0["fullO"], 8 * m + (t + 1))
                nc.scalar.activation(M0.O2[:, :, t, :], PS[:, t % 4, 0:2 * DV].rearrange("p (a n) -> p a n", a=2),
                                     ACT.Sigmoid).then_inc(mix0["freeO"], 1)

            for t in range(4, NT):
                evac_qkv(0, t)
            for t in range(EXP_AT):
                evac_o(0, t)
            act.wait_ge(mix0["scal"], 2)
            nc.scalar.activation(Y[0:HEADS, 4:7, :], Y[0:HEADS, 4:7, :], ACT.Exp).then_inc(mix0["rows"], 1)
            nc.scalar.activation(rows8[:, 16:24], rows8[:, 16:24], ACT.Exp).then_inc(mix0["scratch"], 1)
            act.wait_ge(mix0["scratch"], 1)
            act.dma_start(dec_dram, rows8[:, 16:24]).then_inc(mix0["saved"], 16)
            act.dma_start(negm_dram, R(7)).then_inc(mix0["saved"], 16)
            for t in range(EXP_AT, NT - 2):
                evac_o(0, t)
            act.wait_ge(mix0["saved"], 32)
            act.dma_start(M0.DEC[:], dec_dram.rearrange("h c -> (h c)").partition_broadcast(P)).then_inc(mix0["decb"], 16)

            def load_max(n):
                act.dma_start(M0.NM, negm_dram[bass.ds(n, 1), :].rearrange("a n -> (a n)").partition_broadcast(P)).then_inc(mix0["bcast"], 16)

            def steps0(n, gemm):
                for c in range(NT):
                    act.wait_ge(mix0["tr"], 8 * n + (c - 7))
                    nc.scalar.activation(M0.TQ[0:DQK, :], PS[0:DQK, 4, 0:3 * P], ACT.Copy).then_inc(mix0["tq"], 1)
                    if not gemm and c < NT - 1:
                        head_hi(0, c)
                    act.wait_ge(mix0["outp"], 8 * n + (c - 7))
                    nc.scalar.activation(M0.NUM[:, c, 0:DV + 1], PS[:, 6, 0:DV + 1], ACT.Copy)
                    nc.scalar.activation(M0.squares, PS[:, 6, 0:DV], ACT.Square,
                                         accum_out=M0.ss[:, c:c + 1]).then_inc(mix0["num"], 1)
                    if gemm:
                        evac_qkv(n, c)

            def boundary0(n, last, nxt, m=None):
                if m is not None:
                    act.wait_ge(mix0["gated"], n)
                    for t in range(NT // 2):
                        evac_o(m, t)
                if last:
                    act.wait_ge(mix0["ss"], n)
                    nc.scalar.activation(M0.rs, M0.rs, ACT.Ln, bias=eps1[:], scale=1.0 / DV).then_inc(mix0["rstd"], 1)
                    act.wait_ge(mix0["rstd"], 2 * n - 1)
                    nc.scalar.activation(M0.rs, M0.rs, ACT.Exp, scale=-0.5).then_inc(mix0["rstd"], 1)
                if nxt:
                    act.wait_ge(mix0["args"], n + 1)
                    nc.scalar.activation(M0.PR[:], M0.PR[:], ACT.Exp).then_inc(mix0["probs"], 1)
                if m is not None:
                    for t in range(NT // 2, NT):
                        evac_o(m, t)

            load_max(0)
            for t in range(NT - 2, NT):
                evac_o(0, t)
            boundary0(0, False, True)
            act.wait_ge(head_gains, 32)

            def start_head(n):
                act.wait_ge(mix0["args"], n)
                load_max(n)

            with act.Fori(0, HEADS // 2 - 1) as m:
                for n, pair in ((2 * m + 1, None), (2 * m + 2, m + 1)):
                    start_head(n)
                    steps0(n, True)
                    boundary0(n, True, True, pair)
            start_head(HEADS - 1)
            steps0(HEADS - 1, True)
            boundary0(HEADS - 1, True, True)
            steps0(HEADS, False)
            boundary0(HEADS, True, False)

            def tail(l, h_src, mix_done):
                mix_done()
                act.dma_start(H[:], h_src).then_inc(tw[l]["hin"], 16)
                gain(tw[l], 0, norm_gains[l, 1])
                gain(tw[l], 1, norm_gains[l, 2])
                head_hi(l, HEADS - 1)
                ph = mlp[l]

                def hidden(j, full, ht=None):
                    half, f = j // 2, j % 2
                    sq = TMP[:, (j % 2) * 512:(j % 2) * 512 + 512]
                    act.wait_ge(ph["full"], full)
                    if ht is not None:
                        act.wait_ge(ph["ht"], ht)
                    link(nc.scalar.activation(sq, PS[:, j, :], ACT.Relu))
                    link(nc.scalar.activation(sq, sq, ACT.Square))
                    nc.scalar.activation(HTh[:, f, half * 512:half * 512 + 512], sq, ACT.Copy).then_inc(ph["hi"], 1)

                def mlp_step(g):
                    for j in range(4):
                        hidden(j, 20 * g + (j + 1), 4 * g + (j - 1))

                def first_half(k):
                    if k - ACT_HI in HIDDEN_AT:
                        j = HIDDEN_AT.index(k - ACT_HI)
                        hidden(j, j + 1)
                transition(tw[l], (wo[l]["free"], 48), True, after=first_half)
                gain(tp[l], 0, norm_gains[l, 3])
                for j in (2, 3):
                    hidden(j, 9 + j, j - 1)
                base = link.base + link.n
                with act.Fori(1, NG) as g:
                    link.base, link.n = 8 * g + (base - 8), 0
                    mlp_step(g)
                link.base, link.n = base + 8 * (NG - 1), 0
                transition(tp[l], (mlp[l]["free"], 16 * (NG - 1)), True, norm_pre=False)
                act.wait_ge(tp[l]["ya"], NT)
                gain(te[l], 0, norm_gains[l, 4])
                if l == 0:
                    gain(te[l], 1, norm_gains[1, 0])
                ph = ple[l]
                for hv in range(2):
                    if hv == 0:
                        act.wait_ge(mlp[l]["ht"], 4 * NG)
                    else:
                        act.wait_ge(ph["ptr"], 2)
                    act.dma_start(TMP[:].rearrange("p (k n) -> p k n", k=4),
                                  tok(p[l, 0])[:, 4 * hv:4 * hv + 4, :]).then_inc(ph["pin"], 16)
                    for c in range(2):
                        act.wait_ge(ph["ptr"], 2 * hv + c + 1)
                        nc.scalar.activation(HTh[:, c, hv * 512:hv * 512 + 512], PS[:, 4 + c, :], ACT.Copy).then_inc(ph["phi"], 1)
                for t in range(NT):
                    act.wait_ge(ph["free"], 48 + 2 * t + 2)
                    nc.scalar.activation(Y[:, t, :], Y[:, t, :], ACT.Sigmoid).then_inc(ph["sig"], 1)
                transition(te[l], (ple[l]["free"], 64), l == 0, h_out=h_tok if l == 0 else out_tok)

            def mix0_done():
                act.wait_ge(mix0["done"], HEADS)
            tail(0, x_tok, mix0_done)

            M1 = layer1_views(H, G, TMP, HTh, HTl)
            act.wait_ge(te[0]["hout"], 16 * NT)
            act.wait_ge(te[0]["xt"], 2 * NT)
            act.dma_start(Y[:, 0:2, :].rearrange("p a n -> p (a n)")[:, 0:(LV + 2) * P],
                          c_sums.rearrange("p l n -> p (l n)")).then_inc(mix1["bound"], 16)
            act.dma_start(M1.MASK[:], c_level_mask.rearrange("p l n -> p (l n)")).then_inc(mix1["bound"], 16)
            act.dma_start(Y[:, 2:4, :].rearrange("p a n -> p (a n)"),
                          b_lower_bound.rearrange("a n -> (a n)").partition_broadcast(P)).then_inc(mix1["bound"], 16)
            def one_minus_bound():
                act.wait_ge(mix1["boundS"], 1)
                nc.scalar.activation(M1.OML[:], Y[:, 2, :], ACT.Sigmoid).then_inc(mix1["oml"], 1)

            def evac_qf(n, t):
                act.wait_ge(mix1["fullA"], 8 * n + (t + 1))
                nc.scalar.activation(M1.Zqf[:, :, t, :], PS[:, t % 2, 0:256].rearrange("p (a n) -> p a n", a=2),
                                     ACT.Copy).then_inc(mix1["freeA"], 1)

            def decays(n, c):
                act.wait_ge(mix1["sums"], 8 * n + (c - 7))
                if c:
                    act.wait_ge(mix1["qe"], 16 * n + (2 * c - 16))
                nc.scalar.activation(M1.E[:], PS[:, 2:4, :].rearrange("p a n -> p (a n)"), ACT.Exp)
                if c:
                    act.wait_ge(mix1["kv"], 7 * n + (c - 7))
                nc.scalar.activation(M1.KG[:], PS[:, 6, 2 * P:3 * P], ACT.Exp)
                nc.scalar.activation(M1.TQK[:], PS[:, 6, 0:2 * P], ACT.Copy).then_inc(mix1["decays"], 1)

            def boundary1(n, last, nxt):
                if last:
                    act.wait_ge(mix1["at"], 8 * n)
                    sg = nc.scalar.activation(TMP[:], M1.Zg[:].rearrange("p t n -> p (t n)"), ACT.Sigmoid)
                if nxt:
                    act.wait_ge(mix1["freeA"], 8 * n + 8)
                    sg = nc.scalar.activation(M1.Zf[:], M1.Zf[:], ACT.Sigmoid, scale=-1.0)
                sg.then_inc(mix1["sg"], 1)
                if last:
                    act.wait_ge(mix1["ss"], n)
                    nc.scalar.activation(M1.rs, M1.rs, ACT.Ln, bias=eps1[:], scale=1.0 / DV).then_inc(mix1["rstd"], 1)
                if nxt:
                    act.wait_ge(mix1["onem"], n + 1)
                    nc.scalar.activation(TMP[:], TMP[:], ACT.Ln).then_inc(mix1["lnf"], 1)
                    act.wait_ge(mix1["lnf"], n + 1)
                    nc.scalar.activation(M1.LFh[:].rearrange("p t n -> p (t n)"), TMP[:], ACT.Copy).then_inc(mix1["lfhi"], 1)
                if last:
                    act.wait_ge(mix1["rstd"], 2 * n - 1)
                    nc.scalar.activation(M1.rs, M1.rs, ACT.Exp, scale=-0.5).then_inc(mix1["rstd"], 1)
                if nxt:
                    act.wait_ge(mix1["done"], n + 1)
                    for t in range(NT):
                        act.wait_ge(mix1["fullB"], 8 * n + (t + 1))
                        nc.scalar.activation(M1.Zvg[:, :, t, :], PS[:, t % 4, 0:256].rearrange("p (a n) -> p a n", a=2),
                                             ACT.Copy).then_inc(mix1["freeB"], 1)

            def steps1(n, gemm):
                decays(n, 0)
                for c in range(NT):
                    if c < NT - 1:
                        decays(n, c + 1)
                    if gemm:
                        act.wait_ge(mix1["kg"], 8 * n + (c - 7))
                        evac_qf(n, c)
                    elif c < NT - 1:
                        head_hi(1, c)

            for t in range(NT):
                evac_qf(0, t)
            one_minus_bound()
            boundary1(0, False, True)
            with act.Fori(1, HEADS) as n:
                steps1(n, True)
                boundary1(n, True, True)
            steps1(HEADS, False)
            boundary1(HEADS, True, False)

            def mix1_done():
                act.wait_ge(mix1["done"], HEADS + 1)
            tail(1, h_tok, mix1_done)
            act.wait_ge(te[1]["hout"], 16 * NT)

        @block.vector
        def _(dve):
            link = Link(dve, dve_link)
            V = nc.vector

            def stage_a(ph, t):
                dve.wait_ge(ph["sdA"], t + 1)
                link(V.reciprocal(rA[:, t:t + 1], sdA[:, t:t + 1]))
                V.scalar_tensor_tensor(out=Y[:, t, :], in0=Y[:, t, :], scalar=rA[:, t:t + 1], in1=G[:, 0, :],
                                       op0=ALU.mult, op1=ALU.mult).then_inc(ph["ya"], 1)

            def stage_b(ph, t, norm, post):
                if norm:
                    dve.wait_ge(ph["sdB"], t + 1)
                    if post:
                        dve.wait_ge(ph["hA"], t + 1)
                    link(V.reciprocal(rB[:, t:t + 1], sdB[:, t:t + 1]))
                    V.scalar_tensor_tensor(out=Y[:, t, :], in0=H[:, t, :], scalar=rB[:, t:t + 1], in1=G[:, 1, :],
                                           op0=ALU.mult, op1=ALU.mult).then_inc(ph["xs"], 1)
                else:
                    V.tensor_tensor(Y[:, t, :], Y[:, t, :], G[:, 1, :], ALU.mult).then_inc(ph["xs"], 1)

            def stage_c(ph, t):
                for b in range(2):
                    dve.wait_ge(ph["hi"], 2 * t + b + 1)
                    V.tensor_tensor(XTl[:, 4 * b:4 * b + 4, t * P:(t + 1) * P],
                                    PS[:, 4 + b, :].rearrange("p (k n) -> p k n", k=4),
                                    XTh[:, 4 * b:4 * b + 4, t * P:(t + 1) * P].bitcast(F32), ALU.subtract).then_inc(ph["xt"], 1)

            def transition(ph, finish, post, pre, norm_pre, c_on, gains, after=None):
                b_lag, c_lag = (DVE_B, DVE_C if norm_pre else DVE_C - 1) if post else (0, 1)
                for k in range(NT + c_lag):
                    if finish and k < NT:
                        finish(k)
                    if k == (1 if post else 0):
                        dve.wait_ge(ph["gain"], 16 * gains)
                    if post and 0 <= k - 1 < NT:
                        stage_a(ph, k - 1)
                    if pre and 0 <= k - b_lag < NT:
                        stage_b(ph, k - b_lag, norm_pre, post)
                    if c_on and 0 <= k - c_lag < NT:
                        stage_c(ph, k - c_lag)
                    if after:
                        after(k)

            def head_lo(l, c):
                for b in range(2):
                    dve.wait_ge(tm[l]["hi"], 2 * c + b + 1)
                    V.scalar_tensor_tensor(out=XTl[:, c, b * 512:b * 512 + 512], in0=PS[:, (4 if c == HEADS - 1 else 0) + b, :],
                                           scalar=head_gain[:, l, c:c + 1], in1=XTh[:, c, b * 512:b * 512 + 512].bitcast(F32),
                                           op0=ALU.mult, op1=ALU.subtract).then_inc(tm[l]["xt"], 1)

            dve.wait_ge(ready, 2)
            transition(start, None, False, True, True, True, 1)

            M0 = layer0_views(H, G, TMP)
            R = lambda i: Y[0:HEADS, i, :]
            dve.wait_ge(mix0["scal"], 1)
            dve.wait_ge(mix0["gates_out"], 4)
            link(V.memset(rows8[:, 8:9], 0.0))
            dve.wait_ge(start["xs"], NT)
            link(V.scalar_tensor_tensor(out=R(1), in0=R(1), scalar=0.0, in1=R(2), op0=ALU.min, op1=ALU.subtract))
            link(V.memset(R(2), 1.0))
            ones = TMP[0:HEADS, 0:P]
            link(V.memset(ones, 1.0))
            for c in range(NT):
                cs = slice(c * P, c * P + P)
                last = V.tensor_tensor_scan(out=R(2)[:, cs], data0=ones, data1=R(1)[:, cs], initial=0.0,
                                            op0=ALU.mult, op1=ALU.add)
            link(last)
            link(V.tensor_tensor(R(3), R(0), R(2), ALU.subtract))
            for c in range(NT):
                cs = slice(c * P, c * P + P)
                link(V.tensor_tensor_scan(out=R(1)[:, cs], data0=R(3)[:, cs], data1=R(3)[:, cs],
                                          initial=rows8[:, 8 + c:9 + c], op0=ALU.max, op1=ALU.max))
                if c < NT - 1:
                    link(V.tensor_tensor(rows8[:, 9 + c:10 + c], R(2)[:, c * P + P - 1:c * P + P],
                                         R(1)[:, c * P + P - 1:c * P + P], ALU.add))
            v3 = lambda i: R(i).rearrange("h (c t) -> h c t", c=NT)
            mst = rows8[:, 8:16].unsqueeze(2).to_broadcast([HEADS, NT, P])
            ml = v3(1)[:, :, P - 1:P].to_broadcast([HEADS, NT, P])
            V.tensor_tensor(v3(4), mst, v3(1), ALU.subtract)
            V.tensor_tensor(v3(5), v3(3), ml, ALU.subtract)
            V.scalar_tensor_tensor(out=R(6), in0=R(2), scalar=-1.0, in1=R(1), op0=ALU.mult, op1=ALU.subtract)
            V.tensor_scalar(R(7), R(1), -1.0, None, ALU.mult)
            V.tensor_tensor(rows8[:, 16:24], rows8[:, 8:16], v3(1)[:, :, P - 1], ALU.subtract).then_inc(mix0["scal"], 1)
            dve.wait_ge(mix0["rows_tr"], 1)
            link(V.tensor_copy(M0.TS[:], PS[:, 4, 0:4 * NT * HEADS]))
            V.memset(M0.z[:, :, 256:257], 1.0)
            ts = M0.TS[:].rearrange("p (q c h) -> p q c h", q=4, c=NT)
            dve.wait_ge(mix0["decb"], 16)

            def steps0(n, last=False):
                for c in range(NT):
                    dve.wait_ge(mix0["qk"], 8 * n + (c - 7))
                    V.tensor_tensor(M0.ST[:], PS[:, 5, 0:P], M0.PR3[:, c, :], ALU.mult).then_inc(mix0["st"], 1)
                    if c < NT - 1:
                        dve.wait_ge(mix0["outp"], 8 * n + (c - 7))
                        dve.wait_ge(mix0["kv"], 7 * n + (c - 6))
                        V.scalar_tensor_tensor(out=M0.C[0:DQK, :], in0=M0.C[0:DQK, :], scalar=M0.dec[0:DQK, c:c + 1],
                                               in1=PS[0:DQK, 7, 0:DV + 1], op0=ALU.mult, op1=ALU.add).then_inc(mix0["state"], 1)
                    if last and c < NT - 1:
                        head_lo(0, c)

            def boundary0(n, last, nxt, odd=0):
                u, wi, wk, em = (M0.th[:, i * NT:(i + 1) * NT, 0] for i in range(4))
                den = M0.NUM[:, :, DV]
                yh = Y[:, :, bass.ds(n * DV - DV, DV)] if last else None
                if last:
                    dve.wait_ge(mix0["num"], 8 * n)
                    V.tensor_tensor(yh, M0.NUM[:, :, 0:DV], M0.O2[:, odd], ALU.mult).then_inc(mix0["gated"], 1)
                    link(V.scalar_tensor_tensor(out=M0.den, in0=den, scalar=-1.0, in1=den, op0=ALU.mult, op1=ALU.max))
                    link(V.tensor_tensor(M0.den, M0.den, em, ALU.max))
                    link(V.reciprocal(M0.den, M0.den))
                    link(V.tensor_tensor(M0.rs, M0.ss, M0.den, ALU.mult))
                    V.tensor_tensor(M0.rs, M0.rs, M0.den, ALU.mult).then_inc(mix0["ss"], 1)
                if nxt:
                    V.tensor_copy(M0.dec[:], M0.DEC[:, bass.ds(n * NT, NT)])
                    link(V.tensor_copy(M0.th[:], ts[:, :, :, bass.ds(n, 1)]))
                    dve.wait_ge(mix0["bcast"], 16 * n + 16)
                    link(V.tensor_tensor(M0.PR3, M0.NM3, u.unsqueeze(2).to_broadcast([P, NT, P]), ALU.add))
                    V.tensor_tensor(M0.PR3, M0.PR3, M0.causal.unsqueeze(1).to_broadcast([P, NT, P]), ALU.min).then_inc(mix0["args"], 1)
                    dve.wait_ge(mix0["free"], 8 * n + 8)
                    V.memset(M0.C[:], 0.0)
                    link(V.tensor_scalar(M0.QS[:], M0.z[:, :, 0:DQK], DQK ** -0.5, None, ALU.mult))
                    V.tensor_tensor(M0.QW[:], M0.QS[:], wi.unsqueeze(2).to_broadcast([P, NT, DQK]), ALU.mult)
                    V.tensor_tensor(M0.KW[:], M0.z[:, :, DQK:2 * DQK], wk.unsqueeze(2).to_broadcast([P, NT, DQK]),
                                    ALU.mult).then_inc(mix0["prep"], 1)
                if last:
                    dve.wait_ge(mix0["rstd"], 2 * n)
                    link(V.tensor_tensor(M0.den, M0.den, M0.rs, ALU.mult))
                    V.tensor_tensor(yh, yh, M0.den.unsqueeze(2).to_broadcast([P, NT, DV]), ALU.mult).then_inc(mix0["done"], 1)
                if nxt:
                    dve.wait_ge(mix0["probs"], n + 1)

            boundary0(0, False, True)
            base0 = link.base + link.n
            dve.wait_ge(head_gains, 32)
            with dve.Fori(0, HEADS // 2 - 1) as m:
                link.base, link.n = m * (2 * LINKS0) + base0, 0
                for odd in range(2):
                    steps0(2 * m + (1 + odd))
                    boundary0(2 * m + (1 + odd), True, True, odd)
                assert link.n == 2 * LINKS0, link.n
            link.base, link.n = base0 + (HEADS - 2) * LINKS0, 0
            steps0(HEADS - 1)
            boundary0(HEADS - 1, True, True, 0)
            steps0(HEADS, True)
            boundary0(HEADS, True, False, 1)

            def tail(l):
                head_lo(l, HEADS - 1)

                def sums(ph, k0, j, t, f0=None):
                    for nh in range(2):
                        m = 2 * t + nh
                        dve.wait_ge(ph["full"], (k0 if f0 is None else f0) + (m + 1))
                        ys = Y[:, t, nh * 512:nh * 512 + 512]
                        if j == 0:
                            V.tensor_copy(ys, PS[:, m % 4, :]).then_inc(ph["free"], 1)
                        else:
                            V.tensor_tensor(ys, ys, PS[:, m % 4, :], ALU.add).then_inc(ph["free"], 1)

                def finish(ph, k0):
                    return lambda t: sums(ph, k0, 1, t)

                for j in range(3):
                    for t in range(NT):
                        sums(wo[l], 16 * j, j, t)
                dve.wait_ge(tw[l]["hin"], 16)
                ph = mlp[l]

                def lo_part(g, j):
                    half, f = j // 2, j % 2
                    dve.wait_ge(ph["hi"], 4 * g + (j + 1))
                    V.tensor_tensor(HTl[:, f, half * 512:half * 512 + 512], TMP[:, (j % 2) * 512:(j % 2) * 512 + 512],
                                    HTh[:, f, half * 512:half * 512 + 512].bitcast(F32), ALU.subtract).then_inc(ph["ht"], 1)

                def mlp_up(g):
                    for j in range(4):
                        lo_part(g, j)

                def first_half(k):
                    if k - DVE_C in HIDDEN_AT:
                        lo_part(0, HIDDEN_AT.index(k - DVE_C))
                transition(tw[l], finish(wo[l], 48), True, True, True, True, 2, first_half)
                for t in range(4):
                    sums(ph, 2, 0, t)
                lo_part(0, 2)
                lo_part(0, 3)
                for t in range(4, NT):
                    sums(ph, 4, 0, t)
                with dve.Fori(1, NG - 1) as g:
                    mlp_up(g)
                    for t in range(NT):
                        sums(ph, 20 * g + 4, 1, t)
                mlp_up(NG - 1)
                transition(tp[l], finish(ph, 20 * (NG - 1) + 4), True, False, False, True, 1)

                ph = ple[l]
                for j in range(3):
                    for t in range(NT):
                        sums(ph, 16 * j, j, t)
                    if j in (0, 1):
                        for c in range(2):
                            dve.wait_ge(ph["phi"], 2 * j + c + 1)
                            V.tensor_tensor(HTl[:, c, j * 512:j * 512 + 512], PS[:, 4 + c, :],
                                            HTh[:, c, j * 512:j * 512 + 512].bitcast(F32), ALU.subtract).then_inc(ph["pt"], 1)
                for t in range(NT):
                    sums(ph, 48, 3, t)

                def gated(t):
                    dve.wait_ge(ph["sig"], t + 1)
                    for nh in range(2):
                        m = 2 * t + nh
                        dve.wait_ge(ph["full"], 64 + m + 1)
                        ys = Y[:, t, nh * 512:nh * 512 + 512]
                        V.tensor_tensor(ys, ys, PS[:, m % 4, :], ALU.mult).then_inc(ph["free"], 1)
                transition(te[l], gated, True, l == 0, True, l == 0, 2 if l == 0 else 1)

            tail(0)

            M1 = layer1_views(H, G, TMP, HTh, HTl)
            dve.wait_ge(mix1["bound"], 48)
            V.tensor_copy(M1.sums[:], Y[:, 0:2, :].rearrange("p a n -> p (a n)")[:, 0:(LV + 2) * P]).then_inc(mix1["const"], 1)
            V.tensor_tensor(Y[:, 2, :], Y[:, 2, :], Y[:, 3, :], ALU.subtract).then_inc(mix1["boundS"], 1)
            V.memset(M1.ST[:], 0.0).then_inc(mix1["done"], 1)
            dve.wait_ge(mix1["oml"], 1)
            b1 = link.base + link.n
            T3 = TMP[:].rearrange("p (t n) -> p t n", n=P)
            E3 = M1.E[:].rearrange("p (l n) -> p l n", n=P)

            def out_tile(n, c):
                dve.wait_ge(mix1["outp"], 8 * n + (c - 7))
                return V.tensor_scalar(Y[:, c, bass.ds(n * P - P, P)], PS[:, 7, P:2 * P], 1.0, None, ALU.mult)

            def steps1(n, last=False):
                def halves(l0, l1):
                    k = l1 - l0
                    V.tensor_tensor(M1.QE[:, l0:l1, :], M1.TQK[:, 0:P].unsqueeze(1).to_broadcast([P, k, P]),
                                    E3[:, l0:l1, :], ALU.mult)
                    V.tensor_tensor(M1.KE[:, l0:l1, :], M1.TQK[:, P:2 * P].unsqueeze(1).to_broadcast([P, k, P]),
                                    E3[:, l0:l1, :], ALU.mult).then_inc(mix1["qe"], 1)
                for c in range(NT):
                    dve.wait_ge(mix1["decays"], 8 * n + (c - 7))
                    V.tensor_tensor(M1.KG[:], M1.KG[:], M1.Zf[:, c, :], ALU.mult).then_inc(mix1["kg"], 1)
                    halves(0, 4)
                    if c:
                        out_tile(n, c - 1)
                        dve.wait_ge(mix1["kv"], 7 * n + (c - 7))
                        V.scalar_tensor_tensor(out=M1.ST[:], in0=M1.ST[:], scalar=M1.dec[(c - 1) % 2], in1=PS[:, 7, 0:P],
                                               op0=ALU.mult, op1=ALU.add).then_inc(mix1["state"], 1)
                    V.tensor_tensor(M1.QG[:], M1.TQK[:, 0:P], E3[:, LV, :], ALU.mult)
                    V.tensor_copy(M1.dec[c % 2], E3[:, LV, P - 1:P])
                    halves(4, LV)
                    for b in range(2):
                        dve.wait_ge(mix1["lev"], 16 * n + (2 * c + b - 15))
                        masked = V.tensor_tensor(TMP[:, b * 512:b * 512 + 512], PS[:, 4 + b, :], M1.MASK[:, b * 512:b * 512 + 512], ALU.mult)
                    link(masked)
                    V.tensor_reduce(M1.AT[:], TMP[:].rearrange("p (l n) -> p n l", n=P), AX_X, ALU.add).then_inc(mix1["at"], 1)
                    if last and c < NT - 1:
                        head_lo(1, c)

            def boundary1(n, last, nxt):
                yh = Y[:, :, bass.ds(n * P - P, P)] if last else None
                if last:
                    link(out_tile(n, NT - 1))
                    link(V.tensor_tensor(E3, yh, yh, ALU.mult))
                    V.tensor_reduce(M1.rs, E3, AX_X, ALU.add).then_inc(mix1["ss"], 1)
                dve.wait_ge(mix1["sg"], n + 1)
                if last:
                    V.tensor_tensor(M1.Zg[:], M1.Zg[:], T3, ALU.mult)
                if nxt:
                    link(V.tensor_tensor(M1.Zf[:], M1.Zf[:], M1.OML[:, bass.ds(n * P, P)].unsqueeze(1).to_broadcast([P, NT, P]), ALU.mult))
                    link(V.tensor_scalar(TMP[:], M1.Zf[:].rearrange("p t n -> p (t n)"), -1.0, 1.0, ALU.mult, ALU.add))
                    V.tensor_scalar(TMP[:], TMP[:], 1e-9, None, ALU.max).then_inc(mix1["onem"], 1)
                    V.memset(M1.ST[:], 0.0)
                if last:
                    dve.wait_ge(mix1["rstd"], 2 * n)
                    link(V.tensor_tensor(yh, yh, M1.rs.unsqueeze(2).to_broadcast([P, NT, P]), ALU.mult))
                    V.tensor_tensor(yh, yh, M1.Zg[:], ALU.mult).then_inc(mix1["done"], 1)
                if nxt:
                    dve.wait_ge(mix1["lfhi"], n + 1)
                    V.tensor_tensor(M1.LFl[:].rearrange("p t n -> p (t n)"), TMP[:],
                                    M1.LFh[:].rearrange("p t n -> p (t n)").bitcast(F32), ALU.subtract).then_inc(mix1["lf"], 1)

            boundary1(0, False, True)
            b1 = link.base + link.n
            with dve.Fori(1, HEADS) as n:
                link.base, link.n = n * LINKS1 + (b1 - LINKS1), 0
                steps1(n)
                boundary1(n, True, True)
                assert link.n == LINKS1, link.n
            link.base, link.n = b1 + (HEADS - 1) * LINKS1, 0
            steps1(HEADS, True)
            boundary1(HEADS, True, False)
            tail(1)


class Views:
    pass


def layer0_views(H, G, TMP):
    v = Views()
    flat = H[:].rearrange("p t n -> p (t n)")
    at = [0]

    def take(src, n):
        a = src[:, at[0]:at[0] + n]
        at[0] += n
        return a
    v.z = take(flat, NT * 260).rearrange("p (t n) -> p t n", n=260)
    v.O2 = take(flat, 2 * NT * DV).rearrange("p (a t n) -> p a t n", a=2, n=DV)
    v.QS = take(flat, NT * DQK).rearrange("p (t n) -> p t n", n=DQK)
    v.QW = take(flat, NT * DQK).rearrange("p (t n) -> p t n", n=DQK)
    v.KW = take(flat, NT * DQK).rearrange("p (t n) -> p t n", n=DQK)
    v.PR = take(flat, S)
    v.PR3 = v.PR.rearrange("p (t n) -> p t n", n=P)
    v.NM = TMP[:]
    v.NM3 = v.NM.rearrange("p (t n) -> p t n", n=P)
    v.NUM = take(flat, NT * 132).rearrange("p (t n) -> p t n", n=132)
    assert at[0] <= NT * D
    g = G[:].rearrange("p a n -> p (a n)")
    at[0] = 0
    v.TQ = take(g, 3 * P)
    v.squares = take(g, DV)
    v.ST = take(g, P)
    v.C = take(g, DV + 1)
    v.dec = take(g, NT)
    v.ss = take(g, NT)
    v.DEC = take(g, HEADS * NT)
    v.TS = take(g, 4 * NT * HEADS)
    v.th = take(g, 4 * NT).rearrange("p (q a) -> p q a", a=1)
    v.den = take(g, NT)
    v.rs = take(g, NT)
    v.causal = take(g, P)
    return v


def layer1_views(H, G, TMP, HTh, HTl):
    v = Views()
    flat = H[:].rearrange("p t n -> p (t n)")
    at = [0]

    def take(src, n):
        a = src[:, at[0]:at[0] + n]
        at[0] += n
        return a
    v.Zqf = take(flat, 2 * S).rearrange("p (a t n) -> p a t n", a=2, n=P)
    v.Zvg = take(flat, 2 * S).rearrange("p (a t n) -> p a t n", a=2, n=P)
    v.Zq, v.Zf, v.Zv, v.Zg = v.Zqf[:, 0], v.Zqf[:, 1], v.Zvg[:, 0], v.Zvg[:, 1]
    v.OML = take(flat, D)
    v.E = take(flat, (LV + 1) * P)
    v.QE = take(flat, LV * P).rearrange("p (l n) -> p l n", n=P)
    v.KE = take(flat, LV * P).rearrange("p (l n) -> p l n", n=P)
    v.ST = take(flat, P)
    g = G[:].rearrange("p a n -> p (a n)")
    at[0] = 0
    v.MASK = take(g, (LV + 1) * P)
    v.TQK = take(g, 2 * P)
    v.AT = take(g, P)
    v.QG = take(g, P)
    v.KG = take(g, P)
    v.dec = [take(g, 1), take(g, 1)]
    v.rs = take(g, NT)
    hh = HTh[:].rearrange("p a n -> p (a n)")
    hl = HTl[:].rearrange("p a n -> p (a n)")
    v.sums = hh[:, 0:(LV + 2) * P]
    v.LFh = hl[:, 0:S].rearrange("p (t n) -> p t n", n=P)
    v.LFl = hl[:, S:2 * S].rearrange("p (t n) -> p t n", n=P)
    return v


_INS = ["x", "p", "norm_gains", "mlp_w_up", "mlp_w_down", "ple_w_up", "ple_w_gate",
        "a_w_in", "a_ig_bias", "a_fg_bias", "a_head_gain", "a_w_out",
        "b_w_in", "b_lower_bound", "b_head_gain", "b_w_out"]


def kernel(**inputs):
    import concourse.bacc as _bacc
    from concourse import mybir as _mybir
    from concourse.bass_utils import run_bass_kernel_spmd as _run

    nc = _bacc.Bacc("TRN2", target_bir_lowering=False, num_devices=1)
    arrays, args = {}, []
    named = [(n, np.ascontiguousarray(inputs[n])) for n in _INS] + list(shape_constants().items())
    for name, a in named:
        arrays[f"in_{name}_dram"] = a
        args.append(nc.dram_tensor(f"in_{name}_dram", a.shape, _mybir.dt.from_np(a.dtype), kind="ExternalInput").ap())
    args.append(nc.dram_tensor("out_0_dram", (1, S, D), F32, kind="ExternalOutput").ap())
    trunk(nc, *args)
    r = _run(nc, [arrays], core_ids=[0])
    return r.results[0]["out_0_dram"]
```
